# Optimizing a Trainium2 kernel written in Bass

```python
import math
import jax, jax.numpy as jnp
from jax import lax
import numpy as np

D_MODEL = 1024
BATCH = 1
SEQ = 128
DEPTH = 1
DEC_BATCH = 1
DEC_SEQ = 2048
PAST_LEN = 128

GRID_W = 64
D_HYENA = 512
D_RET = 512
N_RET_HEADS = 4
RET_HEAD_DIM = D_RET // N_RET_HEADS
RET_CHUNK = 128
SHORT_CONV = 3
FILTER_EMB = 33
FILTER_HIDDEN = 64
N_EXPERTS = 16
EC_CAPACITY_FACTOR = 2
D_EXPERT = 1024
ROPE_BASE = 10000.0
EPS = 1e-6
IN_COLS = 3 * D_HYENA + 4 * D_RET + 2 * D_MODEL

kernel_name = "hybrid_hyena_retention_ec_dit_step"

F32 = jnp.float32

def rmsnorm(x, g):
    xf = x.astype(F32)
    y = xf * lax.rsqrt(jnp.mean(xf * xf, axis=-1, keepdims=True) + EPS)
    return (y * g.astype(F32)).astype(x.dtype)

def adaln(cvec, w_mod, b_mod):
    m = jax.nn.silu(cvec) @ w_mod + b_mod
    return jnp.split(m[..., None, :], 6, axis=-1)

def short_conv(x, w, b):
    L = x.shape[1]
    pad = SHORT_CONV // 2
    xp = jnp.pad(x, ((0, 0), (pad, pad), (0, 0)))
    y = b
    for j in range(SHORT_CONV):
        y = y + xp[:, j:j + L] * w[j]
    return y

def hyena_filters(L, w1, b1, freq, w2, b2, w3, decay):
    t = jnp.linspace(0.0, 1.0, L, dtype=F32)[:, None]
    bands = (FILTER_EMB - 1) // 2
    w = 2.0 * math.pi * jnp.arange(L, dtype=F32) / L
    f = jnp.linspace(1e-4, bands - 1, bands, dtype=F32)
    ang = w[:, None] * f[None, :]
    z = jnp.concatenate([t, jnp.cos(ang), -jnp.sin(ang)], axis=-1)
    fr = freq.astype(F32)
    h = jnp.sin(fr * (z @ w1.astype(F32) + b1.astype(F32)))
    h = jnp.sin(fr * (h @ w2.astype(F32) + b2.astype(F32)))
    h = (h @ w3.astype(F32)) * jnp.exp(-t * jnp.abs(decay.astype(F32)))
    return h[:, :D_HYENA], h[:, D_HYENA:]

def bidir_long_conv(u, h_fwd, h_bwd):
    L, C = h_fwd.shape
    k = jnp.concatenate([h_fwd, jnp.zeros((1, C), F32), h_bwd[:0:-1]], axis=0)
    uf = jnp.fft.rfft(u, n=2 * L, axis=1)
    kf = jnp.fft.rfft(k, n=2 * L, axis=0)
    return jnp.fft.irfft(uf * kf[None], n=2 * L, axis=1)[:, :L]

def hyena_branch(z, p):
    z = short_conv(z, p["hy_conv_w"], p["hy_conv_b"])
    v, x1, x2 = jnp.split(z, 3, axis=-1)
    L = z.shape[1]
    h_fwd, h_bwd = hyena_filters(L, p["hy_f_w1"], p["hy_f_b1"], p["hy_f_freq"], p["hy_f_w2"],
                                 p["hy_f_b2"], p["hy_f_w3"], p["hy_decay"])
    u = (v * x1).astype(F32)
    y = bidir_long_conv(u, h_fwd, h_bwd) + u * p["hy_bias"].astype(F32)
    return (y * x2.astype(F32)).astype(z.dtype)

def rope_2d(x):
    L = x.shape[1]
    rows = L // GRID_W
    rr, cc = jnp.meshgrid(jnp.arange(rows), jnp.arange(GRID_W), indexing="ij")
    row = rr.reshape(L).astype(F32)
    col = cc.reshape(L).astype(F32)
    half = RET_HEAD_DIM // 2
    nf = half // 2
    inv = ROPE_BASE ** (-jnp.arange(nf, dtype=F32) / nf)

    def rot(xp, pos):
        ang = pos[:, None] * inv[None, :]
        cs = jnp.cos(ang)[None, :, None, :]
        sn = jnp.sin(ang)[None, :, None, :]
        a, b = xp[..., :nf], xp[..., nf:]
        return jnp.concatenate([a * cs - b * sn, a * sn + b * cs], axis=-1)

    return jnp.concatenate([rot(x[..., :half], row), rot(x[..., half:], col)], axis=-1)

def retention_scan(q, k, v, log_gamma, s0):
    B, L, H, Dh = q.shape
    C = RET_CHUNK
    N = L // C
    qc = q.reshape(B, N, C, H, Dh)
    kc = k.reshape(B, N, C, H, Dh)
    vc = v.reshape(B, N, C, H, Dh)
    lg = log_gamma.astype(F32)
    pos = jnp.arange(C, dtype=F32)
    diff = pos[:, None] - pos[None, :]
    dmask = jnp.where(diff[None] >= 0, jnp.exp(lg[:, None, None] * jnp.maximum(diff, 0.0)[None]), 0.0)
    scores = jnp.einsum("bnihd,bnjhd->bnhij", qc, kc) * dmask
    inner = jnp.einsum("bnhij,bnjhe->bnihe", scores, vc)
    zeta = jnp.exp(lg[None, :] * (C - 1 - pos)[:, None])
    kv = jnp.einsum("bnjhd,jh,bnjhe->nbhde", kc, zeta, vc)
    chunk_decay = jnp.exp(lg * C)[None, :, None, None]

    def step(s, kv_n):
        return chunk_decay * s + kv_n, s

    s_final, s_prev = lax.scan(step, s0.astype(F32), kv)
    xi = jnp.exp(lg[None, :] * (pos + 1.0)[:, None])
    cross = jnp.einsum("bnihd,ih,nbhde->bnihe", qc, xi, s_prev)
    return (inner + cross).reshape(B, L, H, Dh), s_final

def retention_branch(q, k, v, g, p, s0_f, s0_b, use_rope):
    B, L, _ = q.shape
    sh = (B, L, N_RET_HEADS, RET_HEAD_DIM)
    qf = q.astype(F32).reshape(sh)
    kf = k.astype(F32).reshape(sh) * (RET_HEAD_DIM ** -0.5)
    vf = v.astype(F32).reshape(sh)
    if use_rope:
        qf, kf = rope_2d(qf), rope_2d(kf)
    lg_f = jax.nn.log_sigmoid(p["ret_decay_fwd"].astype(F32))
    lg_b = jax.nn.log_sigmoid(p["ret_decay_bwd"].astype(F32))
    o_f, s_f = retention_scan(qf, kf, vf, lg_f, s0_f)
    o_b, s_b = retention_scan(qf[:, ::-1], kf[:, ::-1], vf[:, ::-1], lg_b, s0_b)
    o = o_f + o_b[:, ::-1]
    mu = jnp.mean(o, axis=-1, keepdims=True)
    var = jnp.mean(jnp.square(o - mu), axis=-1, keepdims=True)
    o = ((o - mu) * lax.rsqrt(var + EPS)).reshape(B, L, D_RET) * p["ret_gn_g"].astype(F32)
    o = o * jax.nn.silu(g.astype(F32))
    return o.astype(q.dtype), s_f, s_b

def mixer(h, p, s0_f, s0_b, use_rope):
    proj = h @ p["w_in"]
    z_hy = proj[..., :3 * D_HYENA]
    q, k, v, g = jnp.split(proj[..., 3 * D_HYENA:3 * D_HYENA + 4 * D_RET], 4, axis=-1)
    gates = jax.nn.sigmoid(proj[..., 3 * D_HYENA + 4 * D_RET:])
    g_hy, g_ret = jnp.split(gates, 2, axis=-1)
    y_hy = hyena_branch(z_hy, p)
    y_ret, s_f, s_b = retention_branch(q, k, v, g, p, s0_f, s0_b, use_rope)
    merged = g_hy * (y_hy @ p["w_hy_o"]) + g_ret * (y_ret @ p["w_ret_o"])
    return merged @ p["w_out"], s_f, s_b

def ec_moe(h, p):
    B, L, D = h.shape
    T = B * L
    xt = h.reshape(T, D)
    aff = jax.nn.softmax((xt @ p["w_router"]).astype(F32), axis=-1)
    cap = (EC_CAPACITY_FACTOR * T) // N_EXPERTS
    vals, idx = lax.top_k(aff.T, cap)
    xs = xt[idx]
    hid = jax.nn.silu(jnp.einsum("ecd,edf->ecf", xs, p["w_e_gate"])) * jnp.einsum("ecd,edf->ecf", xs, p["w_e_up"])
    ye = jnp.einsum("ecf,efd->ecd", hid, p["w_e_down"]) * vals[..., None].astype(h.dtype)
    y = jnp.zeros((T, D), h.dtype).at[idx.reshape(-1)].add(ye.reshape(-1, D))
    return y.reshape(B, L, D)

def trunk_layer(x, mod, p, s0_f, s0_b, use_rope):
    sh1, sc1, g1, sh2, sc2, g2 = mod
    h = rmsnorm(x, p["norm1_g"]) * (1.0 + sc1) + sh1
    out, s_f, s_b = mixer(h, p, s0_f, s0_b, use_rope)
    x = x + g1 * out
    h = rmsnorm(x, p["norm2_g"]) * (1.0 + sc2) + sh2
    x = x + g2 * ec_moe(h, p)
    return x, s_f, s_b

def setup_inputs(seed: int = 0) -> dict:
    key = jax.random.key(seed)
    ks = iter(jax.random.split(key, 40))

    def nrm(shape, scale):
        return jax.random.normal(next(ks), shape, F32) * scale

    st_shape = (DEC_BATCH, DEPTH, N_RET_HEADS, RET_HEAD_DIM, RET_HEAD_DIM)
    gam = 1.0 - 2.0 ** (-5.0 - jnp.arange(N_RET_HEADS, dtype=F32))
    gam_logit = jnp.log(gam / (1.0 - gam))
    decay_base = jnp.linspace(3.07, 15.35, 2 * D_HYENA, dtype=F32)
    return {
        "x_prompt": nrm((BATCH, SEQ, D_MODEL), 1.0),
        "x_sample": nrm((DEC_BATCH, DEC_SEQ, D_MODEL), 1.0),
        "state_ret_fwd": nrm(st_shape, 0.5),
        "state_ret_bwd": nrm(st_shape, 0.5),
        "c": nrm((DEC_BATCH, D_MODEL), 1.0),
        "c_ctx": nrm((D_MODEL,), 1.0),
        "w_mod": nrm((DEPTH, D_MODEL, 6 * D_MODEL), 0.5 * D_MODEL ** -0.5),
        "b_mod": nrm((DEPTH, 6 * D_MODEL), 0.02),
        "norm1_g": 1.0 + nrm((DEPTH, D_MODEL), 0.02),
        "w_in": nrm((DEPTH, D_MODEL, IN_COLS), D_MODEL ** -0.5),
        "hy_conv_w": nrm((DEPTH, SHORT_CONV, 3 * D_HYENA), SHORT_CONV ** -0.5),
        "hy_conv_b": nrm((DEPTH, 3 * D_HYENA), 0.02),
        "hy_f_w1": nrm((DEPTH, FILTER_EMB, FILTER_HIDDEN), FILTER_EMB ** -0.5),
        "hy_f_b1": nrm((DEPTH, FILTER_HIDDEN), 0.1),
        "hy_f_freq": 1.0 + nrm((DEPTH, FILTER_HIDDEN), 0.05),
        "hy_f_w2": nrm((DEPTH, FILTER_HIDDEN, FILTER_HIDDEN), FILTER_HIDDEN ** -0.5),
        "hy_f_b2": nrm((DEPTH, FILTER_HIDDEN), 0.1),
        "hy_f_w3": nrm((DEPTH, FILTER_HIDDEN, 2 * D_HYENA), 0.1 * FILTER_HIDDEN ** -0.5),
        "hy_decay": decay_base[None] * (1.0 + nrm((DEPTH, 2 * D_HYENA), 0.05)),
        "hy_bias": nrm((DEPTH, D_HYENA), 0.5),
        "ret_decay_fwd": gam_logit[None] + nrm((DEPTH, N_RET_HEADS), 0.1),
        "ret_decay_bwd": gam_logit[None] + nrm((DEPTH, N_RET_HEADS), 0.1),
        "ret_gn_g": 1.0 + nrm((DEPTH, D_RET), 0.02),
        "w_hy_o": nrm((DEPTH, D_HYENA, D_MODEL), D_HYENA ** -0.5),
        "w_ret_o": nrm((DEPTH, D_RET, D_MODEL), D_RET ** -0.5),
        "w_out": nrm((DEPTH, D_MODEL, D_MODEL), D_MODEL ** -0.5),
        "norm2_g": 1.0 + nrm((DEPTH, D_MODEL), 0.02),
        "w_router": nrm((DEPTH, D_MODEL, N_EXPERTS), D_MODEL ** -0.5),
        "w_e_gate": nrm((DEPTH, N_EXPERTS, D_MODEL, D_EXPERT), D_MODEL ** -0.5),
        "w_e_up": nrm((DEPTH, N_EXPERTS, D_MODEL, D_EXPERT), D_MODEL ** -0.5),
        "w_e_down": nrm((DEPTH, N_EXPERTS, D_EXPERT, D_MODEL), D_EXPERT ** -0.5),
        "norm_f_g": 1.0 + nrm((D_MODEL,), 0.02),
    }

def reference(x_prompt, x_sample, state_ret_fwd, state_ret_bwd, c, c_ctx, w_mod, b_mod, norm1_g,
              w_in, hy_conv_w, hy_conv_b, hy_f_w1, hy_f_b1, hy_f_freq, hy_f_w2, hy_f_b2, hy_f_w3,
              hy_decay, hy_bias, ret_decay_fwd, ret_decay_bwd, ret_gn_g, w_hy_o, w_ret_o, w_out,
              norm2_g, w_router, w_e_gate, w_e_up, w_e_down, norm_f_g):
    xp = x_prompt
    xs = x_sample
    B = x_prompt.shape[0]
    zero_state = jnp.zeros((B, N_RET_HEADS, RET_HEAD_DIM, RET_HEAD_DIM), F32)
    new_f = []
    new_b = []
    for l in range(DEPTH):
        p = {
            "norm1_g": norm1_g[l], "w_in": w_in[l], "hy_conv_w": hy_conv_w[l], "hy_conv_b": hy_conv_b[l],
            "hy_f_w1": hy_f_w1[l], "hy_f_b1": hy_f_b1[l], "hy_f_freq": hy_f_freq[l],
            "hy_f_w2": hy_f_w2[l], "hy_f_b2": hy_f_b2[l], "hy_f_w3": hy_f_w3[l],
            "hy_decay": hy_decay[l], "hy_bias": hy_bias[l], "ret_decay_fwd": ret_decay_fwd[l],
            "ret_decay_bwd": ret_decay_bwd[l], "ret_gn_g": ret_gn_g[l], "w_hy_o": w_hy_o[l],
            "w_ret_o": w_ret_o[l], "w_out": w_out[l], "norm2_g": norm2_g[l],
            "w_router": w_router[l], "w_e_gate": w_e_gate[l], "w_e_up": w_e_up[l],
            "w_e_down": w_e_down[l],
        }
        mod_ctx = adaln(c_ctx, w_mod[l], b_mod[l])
        mod_lat = adaln(c, w_mod[l], b_mod[l])
        xp, s_f, s_b = trunk_layer(xp, mod_ctx, p, zero_state, zero_state, False)
        new_f.append(s_f)
        new_b.append(s_b)
        xs, _, _ = trunk_layer(xs, mod_lat, p, state_ret_fwd[:, l], state_ret_bwd[:, l], True)
    y_prompt = rmsnorm(xp, norm_f_g)
    y_sample = rmsnorm(xs, norm_f_g)
    new_state_fwd = jnp.stack(new_f, axis=1).astype(x_prompt.dtype)
    new_state_bwd = jnp.stack(new_b, axis=1).astype(x_prompt.dtype)
    return (y_prompt, y_sample, new_state_fwd, new_state_bwd)


_drawn_inputs = setup_inputs


def setup_inputs(seed=0):
    import zlib

    import numpy as np

    out = dict(_drawn_inputs(seed))
    spreads = {}
    factors = {'state_ret_fwd': 8.0,
     'state_ret_bwd': 8.0,
     'norm1_g': 2.675,
     'hy_conv_b': 4.789,
     'hy_f_freq': 6.93,
     'ret_gn_g': 8.0,
     'norm2_g': 7.259,
     'norm_f_g': 2.901}
    for name, (base, spread) in spreads.items():
        noise = np.random.default_rng([zlib.crc32(name.encode()), seed]).standard_normal(out[name].shape)
        drawn = base * np.exp(spread * noise) if base else spread * noise
        out[name] = __import__('jax').numpy.asarray(drawn.astype(out[name].dtype))
    for name, factor in factors.items():
        out[name] = (out[name] * factor).astype(out[name].dtype)
    return out
```

```python
import numpy as np
import concourse.bass as bass
from concourse import mybir
from contextlib import ExitStack

F32 = mybir.dt.float32
I32 = mybir.dt.int32
BF16 = mybir.dt.bfloat16
F32R = mybir.dt.float32r
ALU = mybir.AluOpType
ACT = mybir.ActivationFunctionType
AX = mybir.AxisListType

P = 128
DM = 1024
KT = DM // P
LAT, CTX = 2048, 128
NLAT = LAT // P
NT = NLAT + 1
TOK = LAT + CTX
DH = 512
CB = DH // P
HEADS, HD = 4, 128
NE, CAP, CCAP = 16, 2 * LAT // 16, 2 * CTX // 16
FH = 64
N2, K1 = 32, 64
PAIRS = K1 // 2
EPS = 1e-6
GRID_W = 64


class Steps:

    def __init__(self, sem, steps):
        self.sem = sem
        self.steps, self.k, self.next = list(steps), len(steps), 0
        assert len(set(self.steps)) == self.k

    def give(self, eng):
        eng.sem_inc(self.sem, 2 * self.k)

    def at(self, rnd, step):
        return (rnd + 2) * self.k + self.steps.index(step) + 1

    def inc(self, step):
        assert self.steps[self.next % self.k] == step, (self.steps[self.next % self.k], step)
        self.next += 1
        return self.sem, 1


def in_turn(eng, rounds, looped, front, back):
    front(0, 0)
    with eng.Fori(0, looped // 2, 1) as i:
        for h in range(2):
            front(i * 2 + (h + 1), 1 - h)
            back(i * 2 + h, h)
    for t in range(looped, rounds):
        if t + 1 < rounds:
            front(t + 1, (t + 1) % 2)
        back(t, t % 2)


def product(pe, out, lhs, rhs, start, stop):
    pe.matmul(out, lhs[0], rhs[0], start=start, stop=False)
    pe.matmul(out, lhs[0], rhs[1], start=False, stop=False)
    return pe.matmul(out, lhs[1], rhs[0], start=False, stop=stop)


def makers(nc, ctx, s, phase):
    sb = lambda n, sh, dt=F32: ctx.enter_context(nc.sbuf_tensor(f"{phase}_{n}", sh, dt))
    pb = lambda n, sh: ctx.enter_context(nc.psum_tensor(f"{phase}_{n}", sh, F32))

    def sem(n):
        s["own"].append(s["stack"].enter_context(nc.semaphore(f"{phase}_{n}")))
        return s["own"][-1]

    return sb, pb, sem, lambda n, steps: Steps(sem(n), steps)


HAD = 16


def had(sp, *sems):
    for each in sems:
        for sem in each if isinstance(each, list) else [each]:
            sp.sem_inc(sem, HAD)


def retire(sp, s):
    for sem in s["last"]:
        sp.sem_clear(sem)


def take(v, k):
    return bass.ds(v, k)


def constants():
    f8 = np.float64
    c = {}
    c["ident"] = np.eye(P)

    def position_features(pos, L):
        t = pos / (L - 1)
        ang = (2 * np.pi * pos / L)[:, None] * np.linspace(1e-4, 15, 16)[None, :]
        return np.concatenate([t[:, None], np.cos(ang), -np.sin(ang)], axis=1).T, t

    n2, j = np.meshgrid(np.arange(N2), np.arange(K1), indexing="ij")
    ahead, behind = (32 * j + n2).ravel().astype(f8), (LAT - 32 * j - n2).ravel().astype(f8)
    zf, tf = position_features(ahead, LAT)
    zb, tb = position_features(behind, LAT)
    cf, ctf = position_features(np.arange(CTX, dtype=f8), CTX)
    cb, ctb = position_features(CTX - np.arange(CTX, dtype=f8), CTX)
    c["z"] = np.concatenate([np.concatenate([zf, cf], 1), np.concatenate([zb, cb], 1)], 0)
    negt = np.zeros((P, N2 + 2))
    negt[:64, :N2] = -tf.reshape(N2, K1).T
    negt[64:, :N2] = -tb.reshape(N2, K1).T
    negt[:, N2], negt[:, N2 + 1] = -ctf, -ctb
    c["negt"] = negt
    n1, k1 = np.arange(P)[:, None], np.arange(K1)[None, :]
    ph = -2 * np.pi * n1 * (k1 + 0.5) / P
    f1 = np.stack([np.cos(ph), np.sin(ph)], axis=2).reshape(P, P)
    f1[64:] *= -1.0
    c["f1"] = f1
    up = np.zeros((P, 2, P))
    up[:64, 0], up[64:, 1] = f1[:64], f1[:64]
    c["f1u"] = up.reshape(P, 2 * P)
    n2, k2 = np.arange(N2), np.arange(N2)
    tg = np.zeros((PAIRS, P, 448))
    for p in range(PAIRS):
        for b in range(2):
            kk = 2 * p + b
            ph = -2 * np.pi * (n2[:, None] * (kk + 0.5) / 4096 + n2[:, None] * k2[None, :] / N2)
            cs, sn = np.cos(ph), np.sin(ph)
            re = np.concatenate([cs, -sn], 0)
            im = np.concatenate([sn, cs], 0)
            rows = slice(64 * b, 64 * b + 64)
            for s, m in ((0, -im), (64, re), (128, re), (192, im), (256, im)):
                tg[p, rows, s + 32 * b:s + 32 * b + 32] = m
            ics, isn = cs.T, -sn.T
            tg[p, 32 * b:32 * b + 32, 320 + 64 * b:320 + 64 * b + 64] = np.concatenate([ics, isn], 1)
            tg[p, 64 + 32 * b:96 + 32 * b, 320 + 64 * b:320 + 64 * b + 64] = np.concatenate([-isn, ics], 1)
    c["tg"] = tg
    n1, k1 = np.arange(K1)[None, :], np.arange(K1)[:, None]
    ph = 2 * np.pi * n1 * (k1 + 0.5) / P
    c["f2"] = (np.stack([np.cos(ph), -np.sin(ph)], axis=1) * (2.0 / 4096)).reshape(P, K1)
    n, k = np.arange(256)[:, None], np.arange(P)[None, :]
    ph = -2 * np.pi * n * (k + 0.5) / 256
    cc = np.concatenate([np.cos(ph), np.sin(ph)], 1)
    cc[128:] *= -1.0
    c["cf"] = np.concatenate([cc[:128], cc[128:]], 1)
    ph = 2 * np.pi * np.arange(P)[None, :] * (np.arange(P)[:, None] + 0.5) / 256
    c["ci"] = np.concatenate([np.cos(ph), -np.sin(ph)], 1) * (2.0 / 256)
    inv = 10000.0 ** (-np.arange(32) / 32.0)
    pos = np.arange(LAT)
    ar, ac = (pos // GRID_W)[:, None] * inv, (pos % GRID_W)[:, None] * inv
    cos = np.concatenate([np.cos(ar), np.cos(ar), np.cos(ac), np.cos(ac)], 1)
    sin = np.concatenate([-np.sin(ar), np.sin(ar), -np.sin(ac), np.sin(ac)], 1)
    cos = np.concatenate([cos, np.ones((CTX, P))])
    sin = np.concatenate([sin, np.zeros((CTX, P))])
    c["rope"] = np.concatenate([cos, sin, cos * HD ** -0.5, sin * HD ** -0.5], 1).reshape(NT, P, 512)
    j, i = np.arange(P)[:, None], np.arange(P)[None, :]
    c["dist"] = np.concatenate([np.maximum(i - j, 0), np.maximum(j - i, 0),
                                np.broadcast_to(i + 1, (P, P)), np.broadcast_to(P - i, (P, P))], 1)
    c["expo"] = np.concatenate([P - 1 - j, j], 1)
    q = np.arange(P)
    c["seg"] = np.concatenate([(q[:, None] // 8 == q[None, :] // 8), (q[:, None] // 8 == q[None, :] // 8) &
                               (q[:, None] < q[None, :])], 1)
    c["caps"] = np.broadcast_to(np.array([CAP, CCAP]), (P, 2))
    c["slot"] = np.broadcast_to(np.arange(CAP), (P, CAP))
    return {k: np.ascontiguousarray(v, dtype=np.float32) for k, v in c.items()}


TWO_PI_A, TWO_PI_B = 6.28125, 1.93500518798828125e-3
TWO_PI_C = 2 * np.pi - TWO_PI_A - TWO_PI_B
ROUND = 1.5 * 2.0 ** 23


def phase_filters(nc, d, s):
    CH = 12
    with ExitStack() as ctx:
        sb, pb, sem, counted = makers(nc, ctx, s, "filters")
        wm = sb("wm", [P, 2, KT, 512])
        cond = sb("cond", [P, KT, 2])
        scond = sb("scond", [P, KT, 2])
        bmod = sb("bmod", [2, 6 * DM])
        g1n = sb("g1n", [P, KT])
        mrow = sb("mrow", [2, 6 * DM])
        zt = sb("zt", [66, TOK])
        w1 = sb("w1", [66, P])
        w2 = sb("w2", [P, P])
        fcol = sb("fcol", [P, 3])
        fb = sb("fb", [P, 2])
        w3 = sb("w3", [P, DH])
        dec = sb("dec", [P, 3, DH])
        negt = sb("negt", [P, N2 + 2])
        bias0 = sb("bias0", [1, DH])
        f1 = sb("f1", [P, P])
        cf = sb("cf", [P, 512])
        arg = sb("arg", [P, TOK])
        rnd = sb("rnd", [P, TOK])
        hid1 = sb("hid1", [P, TOK])
        hid2 = sb("hid2", [P, N2 + 2, P])
        hs = sb("hs", [P, 2, P])
        env = sb("env", [P, 2, DH])
        taps = sb("taps", [P, 2, DH])
        spec = sb("spec", [P, 2, DH])
        pa = pb("pa", [P, 5, 512])
        pm = pb("pm", [P, 2, 512])
        pmt = pb("pmt", [P, P])

        ld, lc = sem("ld_filter"), sem("ld_cond")
        wld = [sem("wmod0"), sem("wmod1")]
        silu, bar, modpe, modcol, modt, modr = (sem(x) for x in
                                                ("silu_c", "clear", "mod_pe", "mod_col", "mod_t", "mod_r"))
        sin_pe, sin_act, sin_dve = sem("sin_pe"), sem("sin_act"), sem("sin_dve")
        wfree = sem("wmod_used")
        ast = counted("act_taps", ["hid", "env"])
        pst = counted("pe_taps", ["taps", "spec"])
        vst = counted("dve_taps", ["taps", "spec"])
        sst = [sem("spec_out0"), sem("spec_out1")]
        outs = sem("mod_out")
        cspec = sem("ctx_spec")

        with nc.Block() as block:
            @block.sync
            def _(sp):
                had(sp, modcol, sst)
                sp.dma_start(cond[:], d["cond"]).then_inc(lc, 16)
                sp.dma_start(bmod[:], d["b_mod"].partition_broadcast(2)).then_inc(lc, 16)
                sp.dma_start(g1n[:], d["norm1_g"]).then_inc(lc, 16)
                sp.dma_start(s["ident"][:], d["ident"]).then_inc(lc, 16)
                for dst, src in ((zt, "z"), (w1, "f_w1"), (w2, "f_w2"), (fcol, "f_col"), (w3, "f_w3"),
                                 (negt, "negt"), (f1, "f1"), (cf, "cf")):
                    if src in ("f_w1", "f_w2"):
                        continue
                    sp.dma_start(dst[:], d[src]).then_inc(ld, 16)
                sp.dma_start(bias0[:], d["hy_bias"]).then_inc(ld, 16)
                sp.wait_ge(bar, 3)
                for h, (r1, r2) in enumerate(((0, 0), (33, 64))):
                    sp.dma_start(w1[r1:r1 + 33, 64 * h:64 * h + 64], d["f_w1"]).then_inc(ld, 16)
                    sp.dma_start(w2[r2:r2 + 64, 64 * h:64 * h + 64], d["f_w2"]).then_inc(ld, 16)
                for n, (lo, hi) in enumerate(((0, 64), (0, 128), (0, 128))):
                    if n == 0:
                        for h in range(2):
                            sp.dma_start(dec[64 * h:64 * h + 64, 0, :],
                                         d["decay"][h:h + 1, :].partition_broadcast(64)).then_inc(ld, 16)
                    else:
                        sp.dma_start(dec[:, n, :], d["decay"][n - 1:n, :].partition_broadcast(P)).then_inc(ld, 16)
                for h in range(2):
                    sp.dma_start(wm[:, h], d["w_mod"][h:h + 1]).then_inc(wld[h], 16)
                with sp.Fori(0, N2 // 2, 1) as i:
                    for h in range(2):
                        t = i * 2 + h
                        sp.wait_ge(vst.sem, vst.at(t, "spec"))
                        sp.dma_start(d["kspec"][:, take(t, 1), :], spec[:, h, :]).then_inc(sst[h], 16)
                sp.wait_ge(cspec, 2)
                sp.dma_start(d["cspec"].rearrange("a p c -> p a c"), spec[:]).then_inc(outs, 16)
                with sp.Fori(1, CH // 2, 1) as i:
                    for h in range(2):
                        sp.wait_ge(wfree, i * 2 + (h - 1))
                        sp.dma_start(wm[:, h], d["w_mod"][take(i * 2 + h, 1)]).then_inc(wld[h], 16)
                sp.wait_ge(modcol, CH + HAD)
                sp.dma_start(d["mod"], mrow[:]).then_inc(outs, 16)
                sp.wait_ge(outs, 32)
                retire(sp, s)

            @block.tensor
            def _(pe):
                pst.give(pe)
                pe.wait_ge(ld, 16 * 15)
                for b in range(5):
                    n = min(512, TOK - 512 * b)
                    mm = pe.matmul(pa[:, b, 0:n], w1[:], zt[:, 512 * b:512 * b + n], start=True, stop=True)
                mm.then_inc(sin_pe, 1)
                pe.wait_ge(sin_act, 2)
                for b in range(5):
                    n = min(512, TOK - 512 * b)
                    mm = pe.matmul(pa[:, b, 0:n], w2[:], hid1[:, 512 * b:512 * b + n], start=True, stop=True)
                mm.then_inc(sin_pe, 1)

                def taps_mm(t, h):
                    pe.wait_ge(ast.sem, ast.at(t, "hid"))
                    pe.wait_ge(vst.sem, vst.at(t - 2, "taps"))
                    pe.matmul(pa[:, h, :], hs[:, h, :], w3[:], start=True, stop=True).then_inc(*pst.inc("taps"))

                def spec_mm(t, h):
                    pe.wait_ge(vst.sem, vst.at(t, "taps"))
                    pe.wait_ge(vst.sem, vst.at(t - 2, "spec"))
                    pe.matmul(pa[:, 2 + h, :], f1[:], taps[:, h, :], start=True, stop=True)\
                      .then_inc(*pst.inc("spec"))

                with pe.Fori(0, N2 // 2, 1) as i:
                    for h in range(2):
                        taps_mm(i * 2 + h, h)
                        spec_mm(i * 2 + h, h)
                for h in range(2):
                    pe.wait_ge(ast.sem, ast.at(N2 + h, "hid"))
                    pe.wait_ge(vst.sem, vst.at(N2 + h - 2, "taps"))
                    pe.matmul(pa[:, h, :], hs[:, h, :], w3[:], start=True, stop=True).then_inc(*pst.inc("taps"))
                    pe.wait_ge(vst.sem, vst.at(N2 + h - 2, "spec"))
                    pe.wait_ge(vst.sem, vst.at(N2 + h, "taps"))
                    for r in range(2):
                        mm = pe.matmul(pa[:, 2 + r, :], cf[:, 256 * h + P * r:256 * h + P * r + P], taps[:, h, :],
                                       start=(h == 0), stop=(h == 1))
                    mm.then_inc(*pst.inc("spec"))
                pe.wait_ge(silu, 1)
                with pe.Fori(0, CH // 2, 1) as i:
                    for h in range(2):
                        pe.wait_ge(wld[h], i * 16 + 16)
                        pe.wait_ge(modcol, i * 2 + HAD)
                        for k in range(KT):
                            mm = pe.matmul(pm[0:2, h, :], scond[:, k, :], wm[:, h, k, :],
                                           start=(k == 0), stop=(k == KT - 1))
                        mm.then_inc(wfree, 1)
                pe.wait_ge(modcol, CH + HAD)
                for m in range(2 * KT):
                    mm = pe.transpose(pmt[:, 2 * m:2 * m + 2], mrow[:, P * m:P * m + P], s["ident"][0:2, 0:2])
                mm.then_inc(modt, 1)

            @block.scalar
            def _(act):
                ast.give(act)
                act.wait_ge(lc, 64)
                act.activation(scond[:], cond[:], ACT.Silu).then_inc(silu, 1)
                act.wait_ge(bar, 4)
                for layer in range(2):
                    act.wait_ge(sin_pe, layer + 1)
                    act.activation(arg[:], pa[:].rearrange("p a b -> p (a b)")[:, 0:TOK], ACT.Identity,
                                   bias=fb[:, layer:layer + 1], scale=fcol[:, 1:2]).then_inc(sin_act, 1)
                    act.wait_ge(sin_dve, 5 * (layer + 1))
                    if layer == 0:
                        act.activation(hid1[:], arg[:], ACT.Sin).then_inc(sin_act, 1)
                    else:
                        for h in range(2):
                            a = arg[64 * h:64 * h + 64, 0:LAT].rearrange("p (a b) -> p a b", b=K1)
                            act.activation(hid2[64 * h:64 * h + 64, 0:N2, 64 * h:64 * h + 64], a, ACT.Sin)\
                               .then_inc(sin_act, 1)
                            act.activation(hid2[64 * h:64 * h + 64, N2 + h, :],
                                           arg[64 * h:64 * h + 64, LAT:TOK], ACT.Sin).then_inc(sin_act, 1)
                act.wait_ge(bar, 9)

                def group(t, h, direction):
                    act.wait_ge(pst.sem, pst.at(t - 2, "taps"))
                    act.activation(hs[:, h, :], hid2[:, take(t, 1), :], ACT.Copy).then_inc(*ast.inc("hid"))
                    act.wait_ge(vst.sem, vst.at(t - 2, "taps"))
                    act.activation(env[:, h, :], dec[:, direction, :], ACT.Exp, scale=negt[:, take(t, 1)])\
                       .then_inc(*ast.inc("env"))

                with act.Fori(0, N2 // 2, 1) as i:
                    for h in range(2):
                        group(i * 2 + h, h, 0)
                for h in range(2):
                    group(N2 + h, h, 1 + h)

            @block.vector
            def _(v):
                vst.give(v)
                v.memset(w1[:], 0.0).then_inc(bar, 1)
                v.memset(w2[:], 0.0).then_inc(bar, 1)
                v.memset(hid2[:], 0.0).then_inc(bar, 1)
                v.wait_ge(ld, 16 * 15)
                v.tensor_tensor(fb[:], fcol[:, 0:3:2], fcol[:, 1:2].broadcast_to([P, 2]), ALU.mult).then_inc(bar, 1)
                n = 0
                for layer in range(2):
                    v.wait_ge(sin_act, 2 * layer + 1)
                    v.tensor_scalar(rnd[:], arg[:], float(1 / (2 * np.pi)), ROUND, ALU.mult, ALU.add)\
                     .then_inc(sin_dve, 1)
                    v.wait_ge(sin_dve, n + 1)
                    v.tensor_scalar(rnd[:], rnd[:], -ROUND, None, ALU.add).then_inc(sin_dve, 1)
                    for m, part in enumerate((TWO_PI_A, TWO_PI_B, TWO_PI_C)):
                        v.wait_ge(sin_dve, n + 2 + m)
                        if m < 2:
                            v.scalar_tensor_tensor(arg[:], rnd[:], -part, arg[:], ALU.mult, ALU.add)\
                             .then_inc(sin_dve, 1)
                        else:
                            v.scalar_tensor_tensor(rnd[:], rnd[:], -part, arg[:], ALU.mult, ALU.add)\
                             .then_inc(bar, 1)
                            v.wait_ge(bar, 5 + layer)
                            v.tensor_scalar(arg[:], rnd[:], 3.1415925, -3.1415925, ALU.min, ALU.max)\
                             .then_inc(sin_dve, 1)
                    n += 5
                v.wait_ge(sin_act, 7)
                v.memset(hid2[64:P, 0, 64:65], 0.0).then_inc(bar, 1)
                v.memset(hid2[64:P, N2 + 1, 0:1], 0.0).then_inc(bar, 1)
                v.scalar_tensor_tensor(dec[:], dec[:], -1.0, dec[:], ALU.mult, ALU.max).then_inc(bar, 1)

                def taps_of(t, h):
                    v.wait_ge(pst.sem, pst.at(t, "taps"))
                    v.wait_ge(ast.sem, ast.at(t, "env"))
                    v.wait_ge(pst.sem, pst.at(t - 2, "spec"))
                    v.tensor_tensor(taps[:, h, :], pa[:, h, :], env[:, h, :], ALU.mult)\
                     .then_inc(*vst.inc("taps"))

                def tap_zero(t, h):
                    v.wait_ge(pst.sem, pst.at(t, "taps"))
                    v.wait_ge(ast.sem, ast.at(t, "env"))
                    v.wait_ge(pst.sem, pst.at(t - 2, "spec"))
                    v.tensor_tensor(taps[:, h, :], pa[:, h, :], env[:, h, :], ALU.mult).then_inc(bar, 1)

                def spec_of(t, h, k):
                    v.wait_ge(pst.sem, pst.at(t, "spec"))
                    v.wait_ge(sst[h], k * 16 + HAD)
                    v.tensor_copy(spec[:, h, :], pa[:, 2 + h, :]).then_inc(*vst.inc("spec"))

                def skip_weight(count):
                    v.wait_ge(bar, count)
                    v.tensor_tensor(taps[0:1, 0, :], taps[0:1, 0, :], bias0[:], ALU.add)\
                     .then_inc(*vst.inc("taps"))

                tap_zero(0, 0)
                skip_weight(10)
                spec_of(0, 0, 0)
                taps_of(1, 1)
                spec_of(1, 1, 0)
                with v.Fori(1, N2 // 2, 1) as i:
                    for h in range(2):
                        taps_of(i * 2 + h, h)
                        spec_of(i * 2 + h, h, i)
                tap_zero(N2, 0)
                skip_weight(11)
                v.wait_ge(sst[0], N2 * 8 + HAD)
                v.wait_ge(sst[1], N2 * 8 + HAD)
                v.wait_ge(pst.sem, pst.at(N2, "spec"))
                v.engine_nop().then_inc(*vst.inc("spec"))
                taps_of(N2 + 1, 1)
                v.wait_ge(pst.sem, pst.at(N2 + 1, "spec"))
                for r in range(2):
                    v.tensor_copy(spec[:, r, :], pa[:, 2 + r, :]).then_inc(cspec, 1)

                with v.Fori(0, CH // 2, 1) as i:
                    for h in range(2):
                        t = i * 2 + h
                        v.wait_ge(wfree, t + 1)
                        v.tensor_tensor(mrow[:, take(t * 512, 512)], pm[0:2, h, :],
                                        bmod[:, take(t * 512, 512)], ALU.add)\
                         .then_inc(modcol, 1)
                v.wait_ge(modt, 1)
                v.tensor_copy(s["shift1"][:], pmt[:, 0:2 * KT].rearrange("p (a b) -> p a b", b=2)).then_inc(modr, 1)
                v.scalar_tensor_tensor(s["scale1"][:], pmt[:, 2 * KT:4 * KT].rearrange("p (a b) -> p a b", b=2), 1.0,
                                       g1n[:].unsqueeze(2).broadcast_to([P, KT, 2]), ALU.add, ALU.mult)\
                 .then_inc(modr, 1)


def layout(x):
    c = np.ascontiguousarray
    o = {}
    o["xs"] = c(np.concatenate([x["x_sample"][0], x["x_prompt"][0]], 0).reshape(NT, P, DM))
    col = lambda v: c(v.reshape(-1, P).T)
    o["cond"] = c(np.stack([col(x["c"][0]), col(x["c_ctx"])], 2))
    o["w_mod"] = c(x["w_mod"][0].reshape(KT, P, 12, 512).transpose(2, 1, 0, 3))
    o["b_mod"] = c(x["b_mod"])
    o["norm1_g"] = col(x["norm1_g"][0])
    w = x["w_in"][0].reshape(KT, P, 5632)
    o["w_hy"] = c(w[:, :, :1536].reshape(KT, P, 3, CB, P).transpose(3, 1, 2, 0, 4))
    o["w_qkvg"] = c(w[:, :, 1536:3584].reshape(KT, P, 4, 512).transpose(2, 1, 0, 3))
    o["w_gates"] = c(w[:, :, 3584:].transpose(1, 0, 2))
    o["conv"] = c(np.concatenate([x["hy_conv_w"][0], x["hy_conv_b"]], 0).reshape(4, 3, CB, P).transpose(2, 3, 1, 0))
    o["f_w1"], o["f_w2"] = c(x["hy_f_w1"][0]), c(x["hy_f_w2"][0])
    o["f_col"] = c(np.tile(np.stack([x["hy_f_b1"][0], x["hy_f_freq"][0], x["hy_f_b2"][0]], 1), (2, 1)))
    o["f_w3"] = c(x["hy_f_w3"][0].reshape(FH, 2, DH).transpose(1, 0, 2).reshape(P, DH))
    o["decay"] = c(x["hy_decay"][0].reshape(2, DH))
    o["hy_bias"] = c(x["hy_bias"])
    o["ret_decay"] = c(np.concatenate([x["ret_decay_fwd"], x["ret_decay_bwd"]], 1))
    o["ret_gn_g"] = c(x["ret_gn_g"])
    o["state_f"] = c(x["state_ret_fwd"][0, 0].transpose(1, 0, 2).reshape(P, 512))
    o["state_b"] = c(x["state_ret_bwd"][0, 0].transpose(1, 0, 2).reshape(P, 512))
    o["w_hy_o"] = c(x["w_hy_o"][0].reshape(CB, P, DM).transpose(1, 0, 2))
    o["w_ret_o"] = c(x["w_ret_o"][0].reshape(CB, P, DM).transpose(1, 0, 2))
    o["w_out"] = c(x["w_out"][0].reshape(KT, P, DM).transpose(1, 0, 2))
    o["norm2_g"] = c(x["norm2_g"])
    o["norm_f_g"] = c(x["norm_f_g"].reshape(1, DM))
    o["w_router"] = c(x["w_router"][0].reshape(KT, P, NE).transpose(1, 0, 2))
    o["w_gate"] = c(x["w_e_gate"][0].reshape(NE, KT, P, 4, 256).transpose(0, 3, 2, 1, 4))
    o["w_up"] = c(x["w_e_up"][0].reshape(NE, KT, P, 4, 256).transpose(0, 3, 2, 1, 4))
    o["w_down"] = c(x["w_e_down"][0].reshape(NE, 4, 2, P, DM).transpose(0, 1, 3, 2, 4))
    return o


def persistent(nc, ctx):
    sb = lambda n, sh, dt=F32: ctx.enter_context(nc.sbuf_tensor(n, sh, dt))
    return {
        "own": [], "last": [], "stack": ExitStack(), "last_stack": ExitStack(),
        "ident": sb("ident", [P, P]),
        "scale1": sb("scale1", [P, KT, 2]),
        "shift1": sb("shift1", [P, KT, 2]),
        "aff": sb("aff", [P, NT, NE]),
    }


def log_decays_vector(v, lg, raw, tmp, done_a, done_v):
    a, y, w, r, e = (tmp[:, n, :] for n in range(5))
    v.scalar_tensor_tensor(a, raw[:], -1.0, raw[:], ALU.mult, ALU.max).then_inc(done_v, 1)
    v.wait_ge(done_a, 1)
    v.tensor_scalar(w, y, 1.0, None, ALU.add).then_inc(done_v, 1)
    v.wait_ge(done_a, 2)
    v.tensor_scalar(a, w, -1.0, 1e-30, ALU.add, ALU.max).then_inc(done_v, 1)
    v.wait_ge(done_v, 3)
    v.reciprocal(e, a).then_inc(done_v, 1)
    v.wait_ge(done_v, 4)
    v.tensor_tensor(e, e, r, ALU.mult).then_inc(done_v, 1)
    v.tensor_scalar(a, w, 1.0, None, ALU.is_equal).then_inc(done_v, 1)
    v.wait_ge(done_v, 6)
    v.tensor_tensor(e, e, a, ALU.add).then_inc(done_v, 1)
    v.wait_ge(done_v, 7)
    v.tensor_tensor(e, e, y, ALU.mult).then_inc(done_v, 1)
    v.wait_ge(done_v, 8)
    v.scalar_tensor_tensor(lg[:], raw[:], 0.0, e, ALU.min, ALU.subtract).then_inc(done_v, 1)


def log_decays_scalar(act, tmp, done_a, done_v):
    a, y, w, r = (tmp[:, n, :] for n in range(4))
    act.wait_ge(done_v, 1)
    act.activation(y, a, ACT.Exp, scale=-1.0).then_inc(done_a, 1)
    act.wait_ge(done_v, 2)
    act.activation(r, w, ACT.Ln).then_inc(done_a, 1)


def phase_tokens(nc, d, s):
    with ExitStack() as ctx:
        sb, pb, sem, counted = makers(nc, ctx, s, "tokens")
        wh = sb("w_high", [P, 4, KT, 512], F32R)
        wl = sb("w_low", [P, 4, KT, 512], F32R)
        x = sb("x", [P, 2, DM])
        ssq = sb("ssq", [P, 2])
        rstd = sb("rstd", [P, 2])
        eps = sb("eps", [P, 1])
        xn = sb("xn", [P, DM])
        hT = sb("hT", [P, KT, P])
        hh = sb("h_high", [P, 2, KT, P], F32R)
        hl = sb("h_low", [P, 2, KT, P], F32R)
        rope = sb("rope", [P, 2, 4, P])
        cosm = sb("cosm", [P, 512])
        qk = sb("qk", [P, 2, 512])
        sinm = sb("sinm", [P, 512])
        qkT = sb("qkT", [P, 2, 2, 512])
        vs = sb("vs", [P, 2, 512])
        vz = sb("vz", [P, 2, 512])
        gs = sb("gs", [P, 2, 512])
        gn = sb("gn", [P, 512])
        state = sb("state", [P, 2, 512])
        kvb = sb("kvb", [P, 2, 512])
        kvf = sb("kvf", [P, 512])
        raw = sb("raw", [P, 8])
        lg = sb("lg", [P, 8])
        tmp = sb("tmp", [P, 5, 8])
        expo = sb("expo", [P, 2])
        zeta = sb("zeta", [P, 8])
        dec = sb("dec", [P, 8])
        tp = pb("tp", [P, KT * P])
        pq = [pb(f"p{n}", [P, 512]) for n in "qkvg"]
        qt = [pb(f"pt{n}", [P, 512]) for n in "qk"]

        ldw, ldc = [sem(f"ld_w{n}") for n in range(3)], sem("ld_c")
        w_act, w_dve = sem("w_high_ready"), sem("w_split")
        staged = [qkT[:, 0].rearrange("p a b -> p (a b)"), qkT[:, 1].rearrange("p a b -> p (a b)"),
                  kvb[:].rearrange("p a b -> p (a b)")]
        PIECES = [(n, k) for n in range(4) for k in range(0, KT, 2)]
        xld = [sem(f"ld_x{h}") for h in range(2)]
        rld = [sem(f"ld_rope{h}") for h in range(2)]
        hst = sem("st_h")
        qst = [sem(f"st_qk{h}") for h in range(2)]
        vst = [sem(f"st_v{h}") for h in range(2)]
        sst = [sem(f"st_state{h}") for h in range(2)]
        kst = [sem(f"st_kvb{h}") for h in range(2)]
        fin = sem("st_final")
        ca, cv, cs = sem("decay_act"), sem("decay_dve"), sem("consts")
        AF = counted("act_front", ["square", "sqrt", "xn"] + [f"h{k}" for k in range(KT // 2)] + ["high"])
        VF = counted("dve_front", ["rstd"] + [f"h{k}" for k in range(KT // 2, KT)] + ["low"])
        PF = counted("pe_front", ["xT"])
        PB = counted("pe_back", ["q", "k", "v", "g", "qkT", "kvf", "kvb"])
        AB = counted("act_back", ["v", "silu", "qT", "kT", "kvb"])
        VB = counted("dve_back", ["qc", "qs1", "qs2", "q", "kc", "ks1", "ks2", "k",
                                         "s0", "s1", "s2", "s3"])
        GB = counted("pool_back", ["vzf", "vzb", "gs"])
        LOOP = NLAT - 2

        with nc.Block() as block:
            @block.sync
            def _(sp):
                had(sp, hst, qst, vst, kst, sst)
                sp.dma_start(raw[:], d["ret_decay"].partition_broadcast(P)).then_inc(ldc, 16)
                sp.dma_start(expo[:], d["expo"]).then_inc(ldc, 16)
                sp.dma_start(gn[:], d["ret_gn_g"].partition_broadcast(P)).then_inc(ldc, 16)
                sp.dma_start(state[:, 0, :], d["state_f"]).then_inc(ldc, 16)

                def load_x(t, h):
                    sp.wait_ge(AF.sem, AF.at(t - 2, "xn"))
                    sp.dma_start(x[:, h, :], d["xs"][take(t, 1)]).then_inc(xld[h], 16)

                def load_rope(t, h):
                    sp.wait_ge(VB.sem, VB.at(t - 2, "k"))
                    sp.dma_start(rope[:, h].rearrange("p a b -> p (a b)"), d["rope"][take(t, 1)])\
                      .then_inc(rld[h], 16)

                def stores(t, h, more):
                    context = isinstance(t, int) and t == NLAT
                    sp.wait_ge(AF.sem, AF.at(t, "h3"))
                    sp.wait_ge(VF.sem, VF.at(t, "h7"))
                    sp.dma_start(d["hT"][:, :, take(t * P, P)], hT[:]).then_inc(hst, 16)
                    if more:
                        load_x(t + 2, h)
                    if not context:
                        sp.wait_ge(VB.sem, VB.at(t - 1, "s3"))
                        sp.dma_start(d["state"][take(t, 1)], state[:, h, :]).then_inc(sst[h], 16)
                    if more:
                        load_rope(t + 2, h)
                    sp.wait_ge(AB.sem, AB.at(t, "v"))
                    sp.dma_start(d["v"][take(t, 1)], vs[:, h, :]).then_inc(vst[h], 16)
                    sp.wait_ge(GB.sem, GB.at(t, "gs"))
                    sp.dma_start(d["gs"][take(t, 1)], gs[:, h, :]).then_inc(vst[h], 16)
                    sp.wait_ge(AB.sem, AB.at(t, "kT"))
                    sp.dma_start(d["qkT"][take(t, 1)], qkT[:, h].rearrange("p a b -> p (a b)")).then_inc(qst[h], 16)
                    sp.wait_ge(AB.sem, AB.at(t, "kvb"))
                    if context:
                        sp.dma_start(d["new_b"].rearrange("e p c -> p e c"),
                                     kvb[:, h, :].rearrange("p (e c) -> p e c", e=HEADS)).then_inc(kst[h], 16)
                        sp.wait_ge(VB.sem, VB.at(t, "s3"))
                        sp.dma_start(d["new_f"].rearrange("e p c -> p e c"),
                                     kvf[:].rearrange("p (e c) -> p e c", e=HEADS)).then_inc(fin, 16)
                    else:
                        sp.dma_start(d["kvb"][take(t, 1)], kvb[:, h, :]).then_inc(kst[h], 16)

                load_x(0, 0)
                load_x(1, 1)
                load_rope(0, 0)
                load_rope(1, 1)
                for m, (n, k) in enumerate(PIECES):
                    if m >= 3:
                        sp.wait_ge(w_dve, m - 2)
                    sp.dma_start(staged[m % 3].rearrange("p (a b) -> p a b", b=512), d["w_qkvg"][n, :, k:k + 2, :])\
                      .then_inc(ldw[m % 3], 16)
                sp.wait_ge(ldc, 64)
                with sp.Fori(0, LOOP // 2, 1) as i:
                    for h in range(2):
                        stores(i * 2 + h, h, True)
                for t in range(LOOP, NT):
                    stores(t, t % 2, t + 2 < NT)
                for h in range(2):
                    rounds = (NT + 1 - h) // 2
                    sp.wait_ge(qst[h], 16 * rounds + HAD)
                    sp.wait_ge(vst[h], 32 * rounds + HAD)
                    sp.wait_ge(kst[h], 16 * rounds + HAD)
                    sp.wait_ge(sst[h], 16 * (NLAT // 2) + HAD)
                sp.wait_ge(hst, 16 * NT + HAD)
                sp.wait_ge(fin, 16)
                retire(sp, s)

            @block.tensor
            def _(pe):
                PF.give(pe)
                PB.give(pe)

                def front(t, h):
                    pe.wait_ge(AF.sem, AF.at(t, "xn"))
                    pe.wait_ge(AF.sem, AF.at(t - 1, "h3"))
                    pe.wait_ge(VF.sem, VF.at(t - 1, "h7"))
                    for k in range(KT):
                        mm = pe.transpose(tp[:, P * k:P * k + P], xn[:, P * k:P * k + P], s["ident"][:])
                    mm.then_inc(*PF.inc("xT"))

                def project(t, h, n, name):
                    pe.wait_ge(w_dve, 4 * n + 4)
                    for k in range(KT):
                        mm = product(pe, pq[n][:], (hh[:, h, k, :], hl[:, h, k, :]), (wh[:, n, k, :], wl[:, n, k, :]),
                                     k == 0, k == KT - 1)
                    mm.then_inc(*PB.inc(name))

                def back_1(t, h):
                    pe.wait_ge(AF.sem, AF.at(t, "high"))
                    pe.wait_ge(VF.sem, VF.at(t, "low"))
                    pe.wait_ge(VB.sem, VB.at(t - 1, "q"))
                    project(t, h, 0, "q")
                    pe.wait_ge(VB.sem, VB.at(t - 1, "k"))
                    project(t, h, 1, "k")

                def back_2(t, h):
                    pe.wait_ge(VB.sem, VB.at(t - 1, "s3"))
                    project(t, h, 2, "v")
                    pe.wait_ge(AB.sem, AB.at(t - 1, "kvb"))
                    project(t, h, 3, "g")
                    pe.wait_ge(VB.sem, VB.at(t, "k"))
                    pe.wait_ge(AB.sem, AB.at(t - 1, "kT"))
                    for n in range(2):
                        for e in range(HEADS):
                            mm = pe.transpose(qt[n][:, P * e:P * e + P], qk[:, n, P * e:P * e + P], s["ident"][:])
                    mm.then_inc(*PB.inc("qkT"))
                    for n, name in enumerate(("kvf", "kvb")):
                        pe.wait_ge(GB.sem, GB.at(t, ("vzf", "vzb")[n]))
                        pe.wait_ge(AB.sem, AB.at(t, ("v", "silu")[n]))
                        for e in range(HEADS):
                            mm = pe.matmul(pq[2 + n][:, P * e:P * e + P], qk[:, 1, P * e:P * e + P],
                                           vz[:, n, P * e:P * e + P], start=True, stop=True)
                        mm.then_inc(*PB.inc(name))

                front(0, 0)
                with pe.Fori(0, LOOP // 2, 1) as i:
                    for h in range(2):
                        back_1(i * 2 + h, h)
                        front(i * 2 + (h + 1), 1 - h)
                        back_2(i * 2 + h, h)
                for t in range(LOOP, NT):
                    back_1(t, t % 2)
                    if t + 1 < NT:
                        front(t + 1, (t + 1) % 2)
                    back_2(t, t % 2)

            @block.scalar
            def _(act):
                AF.give(act)
                AB.give(act)
                log_decays_scalar(act, tmp, ca, cv)
                act.wait_ge(cv, 9)
                for n in range(2):
                    act.activation(zeta[:, 4 * n:4 * n + 4], lg[:, 4 * n:4 * n + 4], ACT.Exp, scale=expo[:, n:n + 1])\
                       .then_inc(cs, 1)
                act.activation(dec[:], lg[:], ACT.Exp, scale=float(P)).then_inc(cs, 1)
                act.wait_ge(cs, 4)

                def front(t, h, cond, k):
                    act.wait_ge(xld[h], 16 * (k + 1))
                    act.wait_ge(PF.sem, PF.at(t - 1, "xT"))
                    act.wait_ge(AF.sem, AF.at(t - 1, "xn"))
                    act.activation(xn[:], x[:, h, :], ACT.Square, scale=DM ** -0.5, accum_out=ssq[:, h:h + 1])\
                       .then_inc(*AF.inc("square"))
                    act.wait_ge(AF.sem, AF.at(t, "square"))
                    act.activation(rstd[:, h:h + 1], ssq[:, h:h + 1], ACT.Sqrt, bias=eps[:]).then_inc(*AF.inc("sqrt"))
                    act.wait_ge(VF.sem, VF.at(t, "rstd"))
                    act.activation(xn[:], x[:, h, :], ACT.Copy, scale=rstd[:, h:h + 1]).then_inc(*AF.inc("xn"))
                    act.wait_ge(PF.sem, PF.at(t, "xT"))
                    act.wait_ge(hst, 16 * t + HAD)
                    act.wait_ge(VF.sem, VF.at(t - 1, "low"))
                    for m in range(KT // 2):
                        act.activation(hT[:, m, :], tp[:, P * m:P * m + P], ACT.Identity,
                                       bias=s["shift1"][:, m, cond:cond + 1], scale=s["scale1"][:, m, cond:cond + 1])\
                           .then_inc(*AF.inc(f"h{m}"))
                    act.wait_ge(AF.sem, AF.at(t, "h3"))
                    act.wait_ge(VF.sem, VF.at(t, "h7"))
                    act.wait_ge(PB.sem, PB.at(t - 2, "g"))
                    act.activation(hh[:, h].rearrange("p a b -> p (a b)"), hT[:].rearrange("p a b -> p (a b)"),
                                   ACT.Copy).then_inc(*AF.inc("high"))

                def back_1(t, h, k):
                    act.wait_ge(PB.sem, PB.at(t, "v"))
                    act.wait_ge(vst[h], 32 * k + HAD)
                    act.wait_ge(GB.sem, GB.at(t - 2, "vzb"))
                    act.activation(vs[:, h, :], pq[2][:], ACT.Copy).then_inc(*AB.inc("v"))
                    act.wait_ge(PB.sem, PB.at(t, "g"))
                    act.activation(gs[:, h, :], pq[3][:], ACT.Silu).then_inc(*AB.inc("silu"))
                    act.wait_ge(PB.sem, PB.at(t, "qkT"))
                    act.wait_ge(qst[h], 16 * k + HAD)
                    for n, name in enumerate(("qT", "kT")):
                        act.activation(qkT[:, h, n, :], qt[n][:], ACT.Copy).then_inc(*AB.inc(name))
                    act.wait_ge(PB.sem, PB.at(t, "kvb"))
                    act.wait_ge(kst[h], 16 * k + HAD)
                    act.activation(kvb[:, h, :], pq[3][:], ACT.Copy).then_inc(*AB.inc("kvb"))

                front(0, 0, 0, 0)
                for m, (n, k) in enumerate(PIECES):
                    act.wait_ge(ldw[m % 3], 16 * (m // 3 + 1))
                    act.activation(wh[:, n, k:k + 2].rearrange("p a b -> p (a b)"), staged[m % 3], ACT.Copy)\
                       .then_inc(w_act, 1)
                with act.Fori(0, LOOP // 2, 1) as i:
                    front(i * 2 + 1, 1, 0, i)
                    back_1(i * 2, 0, i)
                    front(i * 2 + 2, 0, 0, i + 1)
                    back_1(i * 2 + 1, 1, i)
                for t in range(LOOP, NT):
                    if t + 1 < NT:
                        front(t + 1, (t + 1) % 2, int(t + 1 == NT - 1), (t + 1) // 2)
                    back_1(t, t % 2, t // 2)

            @block.vector
            def _(v):
                VF.give(v)
                VB.give(v)
                v.memset(eps[:], EPS).then_inc(cs, 1)
                v.wait_ge(ldc, 64)
                log_decays_vector(v, lg, raw, tmp, ca, cv)
                v.wait_ge(cs, 4)

                def front(t, h, cond, k):
                    v.wait_ge(PF.sem, PF.at(t, "xT"))
                    v.wait_ge(hst, 16 * t + HAD)
                    v.wait_ge(AF.sem, AF.at(t - 1, "high"))
                    for m in range(KT // 2, KT):
                        v.tensor_scalar(hT[:, m, :], tp[:, P * m:P * m + P], s["scale1"][:, m, cond:cond + 1],
                                        s["shift1"][:, m, cond:cond + 1], ALU.mult, ALU.add).then_inc(*VF.inc(f"h{m}"))
                    v.wait_ge(AF.sem, AF.at(t, "high"))
                    v.wait_ge(VF.sem, VF.at(t, "h7"))
                    v.wait_ge(PB.sem, PB.at(t - 2, "g"))
                    v.tensor_tensor(hl[:, h].rearrange("p a b -> p (a b)"), hT[:].rearrange("p a b -> p (a b)"),
                                    hh[:, h].rearrange("p a b -> p (a b)").bitcast(F32), ALU.subtract)\
                     .then_inc(*VF.inc("low"))

                def norm(t, h):
                    v.wait_ge(AF.sem, AF.at(t, "sqrt"))
                    v.reciprocal(rstd[:, h:h + 1], rstd[:, h:h + 1]).then_inc(*VF.inc("rstd"))

                def turn(t, h, k, n, name):
                    v.wait_ge(PB.sem, PB.at(t, name))
                    if n == 0:
                        v.wait_ge(rld[h], 16 * (k + 1))
                    v.wait_ge(PB.sem, PB.at(t - 1, "kvb" if n else "qkT"))
                    v.wait_ge(VB.sem, VB.at(t, "q") if n else VB.at(t - 1, "k"))
                    heads = lambda a: a.rearrange("p (e c) -> p e c", e=HEADS)
                    v.tensor_tensor(heads(cosm[:]), heads(pq[n][:]),
                                    rope[:, h, 2 * n, :].unsqueeze(1).broadcast_to([P, HEADS, P]), ALU.mult)\
                     .then_inc(*VB.inc(name + "c"))
                    part = lambda a: a.rearrange("p (e g u c) -> p e g u c", e=HEADS, g=2, u=2)
                    sin = rope[:, h, 2 * n + 1, :].rearrange("p (g u c) -> p g u c", g=2, u=2)
                    for u in range(2):
                        v.tensor_tensor(part(sinm[:])[:, :, :, u, :], part(pq[n][:])[:, :, :, 1 - u, :],
                                        sin[:, :, u, :].unsqueeze(1).broadcast_to([P, HEADS, 2, 32]), ALU.mult)\
                         .then_inc(*VB.inc(f"{name}s{u + 1}"))
                    v.wait_ge(VB.sem, VB.at(t, name + "s2"))
                    v.tensor_tensor(qk[:, n, :], cosm[:], sinm[:], ALU.add).then_inc(*VB.inc(name))

                def back_1(t, h, k):
                    turn(t, h, k, 0, "q")
                    turn(t, h, k, 1, "k")

                def back_2(t, h, k):
                    v.wait_ge(PB.sem, PB.at(t, "kvf"))
                    context = isinstance(t, int) and t == NLAT
                    if not context:
                        v.wait_ge(sst[1 - h], 16 * (k + h) + HAD)
                    for e in range(HEADS):
                        cut = slice(P * e, P * e + P)
                        if context:
                            v.tensor_copy(kvf[:, cut], pq[2][:, cut]).then_inc(*VB.inc(f"s{e}"))
                        else:
                            v.wait_ge(VB.sem, VB.at(t - 1, f"s{e}"))
                            v.scalar_tensor_tensor(state[:, 1 - h, cut], state[:, h, cut], dec[:, e:e + 1],
                                                   pq[2][:, cut], ALU.mult, ALU.add).then_inc(*VB.inc(f"s{e}"))

                norm(0, 0)
                front(0, 0, 0, 0)
                for m, (n, k) in enumerate(PIECES):
                    v.wait_ge(w_act, m + 1)
                    flat = lambda a: a[:, n, k:k + 2].rearrange("p a b -> p (a b)")
                    v.tensor_tensor(flat(wl), staged[m % 3], flat(wh).bitcast(F32), ALU.subtract).then_inc(w_dve, 1)
                with v.Fori(0, LOOP // 2, 1) as i:
                    for h in range(2):
                        norm(i * 2 + (h + 1), 1 - h)
                        back_1(i * 2 + h, h, i)
                        front(i * 2 + (h + 1), 1 - h, 0, i + h)
                        back_2(i * 2 + h, h, i)
                for t in range(LOOP, NT):
                    if t + 1 < NT:
                        norm(t + 1, (t + 1) % 2)
                    back_1(t, t % 2, t // 2)
                    if t + 1 < NT:
                        front(t + 1, (t + 1) % 2, int(t + 1 == NLAT), (t + 1) // 2)
                    back_2(t, t % 2, t // 2)

            @block.gpsimd
            def _(g):
                GB.give(g)
                g.wait_ge(cs, 4)
                g.wait_ge(ldc, 64)

                def back(t, h, k):
                    g.wait_ge(AB.sem, AB.at(t, "v"))
                    g.wait_ge(PB.sem, PB.at(t - 1, "kvb"))
                    for n, name in enumerate(("vzf", "vzb")):
                        g.tensor_tensor(vz[:, n, :].rearrange("p (e c) -> p e c", e=HEADS),
                                        vs[:, h, :].rearrange("p (e c) -> p e c", e=HEADS),
                                        zeta[:, 4 * n:4 * n + 4].unsqueeze(2).broadcast_to([P, HEADS, P]), ALU.mult)\
                         .then_inc(*GB.inc(name))
                    g.wait_ge(AB.sem, AB.at(t, "silu"))
                    g.tensor_tensor(gs[:, h, :], gs[:, h, :], gn[:], ALU.mult).then_inc(*GB.inc("gs"))

                with g.Fori(0, NLAT // 2, 1) as i:
                    for h in range(2):
                        back(i * 2 + h, h, i)
                back(NLAT, 0, NLAT // 2)


ZW = TOK + 4
SPANS = [(512 * b, min(512, TOK - 512 * b)) for b in range(5)]


def place_of(token):
    return token + 1 if token < LAT else token + 3


def phase_hyena_in(nc, d, s):
    GR = N2 // 4
    with ExitStack() as ctx:
        sb, pb, sem, counted = makers(nc, ctx, s, "hyin")
        hT = sb("hT_all", [P, KT, TOK])
        w = sb("w_hy", [P, 2, 3, KT, P])
        conv = sb("conv", [P, CB, 3, 4])
        z = sb("z", [P, 3, ZW])
        c = sb("c", [P, 3, ZW])
        u = sb("u", [P, TOK])
        f1 = sb("f1u", [P, 2 * P])
        ut = sb("ut", [P, 2, 256])
        us = sb("us", [P, 2, 4, P])
        uc = sb("uc", [P, P])
        pz = pb("pz", [P, 5, 512])
        pt = pb("pt", [P, 2, 512])
        ps = pb("ps", [P, 512])
        hld = [sem(f"ld_h{b}") for b in range(5)]
        wld = [sem(f"ld_why{h}") for h in range(2)]
        ldc = sem("ld_hyc")
        xst = sem("st_x2")
        ust = [sem(f"st_u{h}") for h in range(2)]
        cst = sem("st_uctx")
        pads = sem("pads")
        zs = [[f"z{m}{b}" for b in range(5)] for m in range(3)]
        tail = ["T0"] + sum([[f"T{g + 1}", f"S{g}"] for g in range(GR - 1)], []) + ["TC", f"S{GR - 1}"]
        PS = counted("pe_hy", sum(zs, []) + tail)
        AS = counted("act_hy", sum([zs[m] + [f"c{m}"] for m in range(3)], []) + [f"S{g}" for g in range(GR)])
        VS = counted("dve_hy", ["a0", "b0", "a1", "b1", "ul", "u", "a2", "b2"] + [f"T{g}" for g in range(GR)] + ["TC"])

        with nc.Block() as block:
            @block.sync
            def _(sp):
                had(sp, xst, cst, ust)
                sp.dma_start(conv[:], d["conv"].rearrange("i p z k -> p i z k")).then_inc(ldc, 16)
                sp.dma_start(f1[:], d["f1u"]).then_inc(ldc, 16)
                sp.dma_start(w[:, 0], d["w_hy"][0]).then_inc(wld[0], 16)
                for b, (at, n) in enumerate(SPANS):
                    sp.dma_start(hT[:, :, at:at + n], d["hT"][:, :, at:at + n]).then_inc(hld[b], 16)
                sp.dma_start(w[:, 1], d["w_hy"][1]).then_inc(wld[1], 16)

                def stores(i, h, k):
                    sp.wait_ge(VS.sem, VS.at(i, "b2"))
                    sp.dma_start(d["x2"][take(i, 1)], c[:, 2, 1:ZW - 1]).then_inc(xst, 16)
                    for g in range(GR):
                        sp.wait_ge(AS.sem, AS.at(i, f"S{g}"))
                        sp.dma_start(d["uspec"][:, 4 * g:4 * g + 4, take(i * P, P)], us[:, g % 2])\
                          .then_inc(ust[g % 2], 16)
                    sp.wait_ge(VS.sem, VS.at(i, "TC"))
                    sp.dma_start(d["uctx"][:, take(i * P, P)], uc[:]).then_inc(cst, 16)

                with sp.Fori(0, 1, 1) as i:
                    for h in range(2):
                        sp.wait_ge(PS.sem, PS.at(i * 2 + h, "z24"))
                        sp.dma_start(w[:, h], d["w_hy"][take(i * 2 + (h + 2), 1)]).then_inc(wld[h], 16)
                        stores(i * 2 + h, h, i)
                for i in range(2, CB):
                    stores(i, i % 2, i // 2)
                sp.wait_ge(xst, 16 * CB + HAD)
                sp.wait_ge(cst, 16 * CB + HAD)
                for h in range(2):
                    sp.wait_ge(ust[h], 16 * CB * GR // 2 + HAD)
                retire(sp, s)

            @block.tensor
            def _(pe):
                PS.give(pe)
                pe.wait_ge(ldc, 32)

                def block_of(i, h, k):
                    pe.wait_ge(wld[h], 16 * (k + 1))
                    for m in range(3):
                        for b, (at, n) in enumerate(SPANS):
                            if m == 0:
                                pe.wait_ge(hld[b], 16)
                            if m == 0:
                                pe.wait_ge(AS.sem, AS.at(i - 1, zs[2][b]))
                            else:
                                pe.wait_ge(AS.sem, AS.at(i, zs[m - 1][b]))
                            for q in range(KT):
                                mm = pe.matmul(pz[:, b, 0:n], w[:, h, m, q, :], hT[:, q, at:at + n],
                                               start=(q == 0), stop=(q == KT - 1))
                            mm.then_inc(*PS.inc(zs[m][b]))
                    pe.wait_ge(VS.sem, VS.at(i, "u"))

                    def turn(g):
                        if g < 2:
                            pe.wait_ge(VS.sem, VS.at(i - 1, f"T{g + GR - 2}" if g else "TC"))
                        else:
                            pe.wait_ge(VS.sem, VS.at(i, f"T{g - 2}"))
                        for q in range(2):
                            at = K1 * (4 * g + 2 * q)
                            mm = pe.transpose(pt[:, g % 2, P * q:P * q + P], u[:, at:at + P], s["ident"][:])
                        mm.then_inc(*PS.inc(f"T{g}"))

                    def stage(g):
                        pe.wait_ge(VS.sem, VS.at(i, f"T{g}"))
                        pe.wait_ge(AS.sem, AS.at(i, f"S{g - 1}") if g else AS.at(i - 1, f"S{GR - 1}"))
                        for r in range(2):
                            mm = pe.matmul(ps[:].rearrange("p (q r c) -> p q r c", r=2, c=P)[:, :, r, :],
                                           f1[:, P * r:P * r + P], ut[:, g % 2, :].rearrange("p (q c) -> p q c", c=P),
                                           start=True, stop=True)
                        mm.then_inc(*PS.inc(f"S{g}"))

                    turn(0)
                    for g in range(GR - 1):
                        turn(g + 1)
                        stage(g)
                    pe.wait_ge(VS.sem, VS.at(i, f"T{GR - 2}"))
                    pe.transpose(pt[:, 0, 0:P], u[:, LAT:TOK], s["ident"][:]).then_inc(*PS.inc("TC"))
                    stage(GR - 1)

                with pe.Fori(0, CB // 2, 1) as i:
                    for h in range(2):
                        block_of(i * 2 + h, h, i)

            @block.scalar
            def _(act):
                AS.give(act)
                act.wait_ge(pads, 2)
                act.wait_ge(ldc, 32)

                def block_of(i, h, k):
                    for m in range(3):
                        for b, (at, n) in enumerate(SPANS):
                            act.wait_ge(PS.sem, PS.at(i, zs[m][b]))
                            if b == 0:
                                act.wait_ge(VS.sem, VS.at(i - 1, f"b{m}"))
                            act.activation(z[:, m, place_of(at):place_of(at) + n], pz[:, b, 0:n], ACT.Copy)\
                               .then_inc(*AS.inc(zs[m][b]))
                        act.wait_ge(AS.sem, AS.at(i, zs[m][4]))
                        if m < 2:
                            act.wait_ge(VS.sem, VS.at(i - 1, "u"))
                        if m == 2:
                            act.wait_ge(xst, 16 * i + HAD)
                        act.activation(c[:, m, 1:ZW - 1], z[:, m, 1:ZW - 1], ACT.Identity,
                                       bias=conv[:, take(i, 1), m, 3], scale=conv[:, take(i, 1), m, 1])\
                           .then_inc(*AS.inc(f"c{m}"))
                    for g in range(GR):
                        act.wait_ge(PS.sem, PS.at(i, f"S{g}"))
                        act.wait_ge(ust[g % 2], 16 * (i * (GR // 2) + g // 2) + HAD)
                        act.activation(us[:, g % 2].rearrange("p a b -> p (a b)"), ps[:], ACT.Copy)\
                           .then_inc(*AS.inc(f"S{g}"))

                with act.Fori(0, CB // 2, 1) as i:
                    for h in range(2):
                        block_of(i * 2 + h, h, i)

            @block.vector
            def _(v):
                VS.give(v)
                v.memset(z[:].rearrange("p m c -> p (m c)"), 0.0).then_inc(pads, 1)
                v.memset(c[:].rearrange("p m c -> p (m c)"), 0.0).then_inc(pads, 1)
                v.wait_ge(ldc, 32)

                def block_of(i, h, k):
                    def convolve(m):
                        v.wait_ge(AS.sem, AS.at(i, f"c{m}"))
                        for step, (tap, off) in (("a", (0, 0)), ("b", (2, 2))):
                            if step == "b":
                                v.wait_ge(VS.sem, VS.at(i, f"a{m}"))
                            v.scalar_tensor_tensor(c[:, m, 1:ZW - 1], z[:, m, off:off + ZW - 2],
                                                   conv[:, take(i, 1), m, tap], c[:, m, 1:ZW - 1],
                                                   ALU.mult, ALU.add).then_inc(*VS.inc(f"{step}{m}"))

                    convolve(0)
                    convolve(1)
                    v.wait_ge(VS.sem, VS.at(i, "b1"))
                    v.wait_ge(PS.sem, PS.at(i - 1, "TC"))
                    by_n2 = lambda m: c[:, m, 1:1 + LAT].rearrange("p (a b) -> p b a", b=N2)
                    v.tensor_tensor(u[:, 0:LAT].rearrange("p (b a) -> p b a", b=N2), by_n2(0), by_n2(1), ALU.mult)\
                     .then_inc(*VS.inc("ul"))
                    at = place_of(LAT)
                    v.tensor_tensor(u[:, LAT:TOK], c[:, 0, at:at + CTX], c[:, 1, at:at + CTX], ALU.mult)\
                     .then_inc(*VS.inc("u"))
                    convolve(2)
                    for g in range(GR):
                        v.wait_ge(PS.sem, PS.at(i, f"T{g}"))
                        v.wait_ge(PS.sem, PS.at(i, f"S{g - 2}") if g >= 2 else PS.at(i - 1, f"S{g + GR - 2}"))
                        v.tensor_copy(ut[:, g % 2, :], pt[:, g % 2, 0:256]).then_inc(*VS.inc(f"T{g}"))
                    v.wait_ge(PS.sem, PS.at(i, "TC"))
                    v.wait_ge(cst, 16 * i + HAD)
                    v.tensor_copy(uc[:], pt[:, 0, 0:P]).then_inc(*VS.inc("TC"))

                with v.Fori(0, CB // 2, 1) as i:
                    for h in range(2):
                        block_of(i * 2 + h, h, i)


def phase_spectrum(nc, d, s):
    SL = 4
    LOOP = PAIRS - SL
    with ExitStack() as ctx:
        sb, pb, sem, counted = makers(nc, ctx, s, "spectrum")
        ks = sb("ks", [P, SL, 512])
        us = sb("us2", [P, SL, 512])
        tg = sb("tg", [P, SL, 448])
        kr = sb("kr", [P, 2, 512])
        ki = sb("ki", [P, 2, 512])
        a = sb("prod_a", [P, 2, 512])
        b = sb("prod_b", [P, 2, 512])
        q = sb("q", [P, 2, 512])
        pk = pb("pk", [P, 2, 512])
        pu = pb("pu", [P, 4, 512])
        pq = pb("pq", [P, 2, 512])
        ld = [sem(f"ld_pair{n}") for n in range(SL)]
        st = [sem(f"st_pair{n}") for n in range(2)]
        PS = counted("pe_sp", ["kr", "ki", "u1", "u2"])
        PB = counted("pe_sp_back", ["q"])
        AS = counted("act_sp", ["kr", "ki"])
        AB = counted("act_sp_back", ["q"])
        VS = counted("dve_sp", ["a", "b", "p"])
        pairs = lambda name: d[name].rearrange("(a r) n c -> a (r n) c", r=4)

        def rounds(eng, front, back):
            front(0, 0, 0)
            with eng.Fori(0, LOOP // SL, 1) as i:
                for m in range(SL):
                    front(i * SL + (m + 1), (m + 1) % SL, i + (m + 1) // SL)
                    back(i * SL + m, m)
            for t in range(LOOP, PAIRS):
                if t + 1 < PAIRS:
                    front(t + 1, (t + 1) % SL, (t + 1) // SL)
                back(t, t % SL)

        with nc.Block() as block:
            @block.sync
            def _(sp):
                had(sp, st)
                def load(t, m):
                    sp.dma_start(ks[:, m], pairs("kspec")[take(t, 1)]).then_inc(ld[m], 16)
                    sp.dma_start(us[:, m], pairs("uspec")[take(t, 1)]).then_inc(ld[m], 16)
                    sp.dma_start(tg[:, m], d["tg"][take(t, 1)]).then_inc(ld[m], 16)

                def store(t, m):
                    sp.wait_ge(AB.sem, AB.at(t, "q"))
                    sp.dma_start(pairs("qspec")[take(t, 1)], q[:, m % 2]).then_inc(st[m % 2], 16)

                for m in range(SL):
                    load(m, m)
                with sp.Fori(0, LOOP // SL, 1) as i:
                    for m in range(SL):
                        sp.wait_ge(PB.sem, PB.at(i * SL + m, "q"))
                        load(i * SL + (m + SL), m)
                        store(i * SL + m, m)
                for t in range(LOOP, PAIRS):
                    store(t, t % SL)
                for h in range(2):
                    sp.wait_ge(st[h], 16 * PAIRS // 2 + HAD)
                retire(sp, s)

            @block.tensor
            def _(pe):
                PS.give(pe)
                PB.give(pe)

                def front(t, m, k):
                    pe.wait_ge(ld[m], 48 * (k + 1))
                    h = 2 * (m % 2)
                    for n, (name, col) in enumerate((("kr", 64), ("ki", 192))):
                        pe.wait_ge(AS.sem, AS.at(t - 1, name))
                        pe.matmul(pk[:, n, :], tg[:, m, col:col + P], ks[:, m, :], start=True, stop=True)\
                          .then_inc(*PS.inc(name))
                    for n, (name, col, read) in enumerate((("u1", 128, "a"), ("u2", 0, "b"))):
                        pe.wait_ge(VS.sem, VS.at(t - 2, read))
                        pe.matmul(pu[:, h + n, :], tg[:, m, col:col + P], us[:, m, :], start=True, stop=True)\
                          .then_inc(*PS.inc(name))

                def back(t, m):
                    pe.wait_ge(VS.sem, VS.at(t, "p"))
                    pe.wait_ge(AB.sem, AB.at(t - 2, "q"))
                    pe.matmul(pq[:, m % 2, :], tg[:, m, 320:448], a[:, m % 2, :], start=True, stop=True)\
                      .then_inc(*PB.inc("q"))

                rounds(pe, front, back)

            @block.scalar
            def _(act):
                AS.give(act)
                AB.give(act)

                def front(t, m, k):
                    for n, (name, dst, read) in enumerate((("kr", kr, "a"), ("ki", ki, "b"))):
                        act.wait_ge(PS.sem, PS.at(t, name))
                        act.wait_ge(VS.sem, VS.at(t - 2, read))
                        act.activation(dst[:, m % 2, :], pk[:, n, :], ACT.Copy).then_inc(*AS.inc(name))

                def back(t, m, k=None):
                    act.wait_ge(PB.sem, PB.at(t, "q"))
                    act.activation(q[:, m % 2, :], pq[:, m % 2, :], ACT.Copy).then_inc(*AB.inc("q"))

                front(0, 0, 0)
                with act.Fori(0, LOOP // SL, 1) as i:
                    for m in range(SL):
                        front(i * SL + (m + 1), (m + 1) % SL, 0)
                        act.wait_ge(st[m % 2], 16 * (i * (SL // 2) + m // 2) + HAD)
                        back(i * SL + m, m)
                for t in range(LOOP, PAIRS):
                    if t + 1 < PAIRS:
                        front(t + 1, (t + 1) % SL, 0)
                    act.wait_ge(st[t % 2], 16 * (t // 2) + HAD)
                    back(t, t % SL)

            @block.vector
            def _(v):
                VS.give(v)

                def product(t, m):
                    h = m % 2
                    v.wait_ge(AS.sem, AS.at(t, "kr"))
                    v.wait_ge(PS.sem, PS.at(t, "u1"))
                    v.wait_ge(PB.sem, PB.at(t - 2, "q"))
                    v.tensor_tensor(a[:, h, :], pu[:, 2 * h, :], kr[:, h, :], ALU.mult).then_inc(*VS.inc("a"))
                    v.wait_ge(AS.sem, AS.at(t, "ki"))
                    v.wait_ge(PS.sem, PS.at(t, "u2"))
                    v.tensor_tensor(b[:, h, :], pu[:, 2 * h + 1, :], ki[:, h, :], ALU.mult).then_inc(*VS.inc("b"))
                    v.wait_ge(VS.sem, VS.at(t, "b"))
                    v.tensor_tensor(a[:, h, :], a[:, h, :], b[:, h, :], ALU.add).then_inc(*VS.inc("p"))

                with v.Fori(0, PAIRS // SL, 1) as i:
                    for m in range(SL):
                        product(i * SL + m, m)


def phase_hyena_out(nc, d, s):
    with ExitStack() as ctx:
        sb, pb, sem, counted = makers(nc, ctx, s, "hyout")
        q = sb("qall", [P, 2, N2, P])
        x2 = sb("x2", [P, 2, LAT])
        y = sb("y", [P, 2, LAT])
        f2 = sb("f2", [P, K1])
        uc = sb("ucx", [P, 512])
        kc = sb("kc", [P, 2, 512])
        cf = sb("cfx", [P, 512])
        ci = sb("ci", [P, 256])
        xc = sb("xc", [P, CB, P])
        pr = sb("pr", [P, 4, 512])
        yc = sb("yc", [P, CB, P])
        py = pb("py", [P, 4, 512])
        pc = pb("pc", [P, 3, 512])
        ldc, stc = sem("ld_c4"), sem("st_c4")
        ld = [sem(f"ld_q{h}") for h in range(2)]
        st = [sem(f"st_y{h}") for h in range(2)]
        cpe, cdv = sem("ctx_pe"), sem("ctx_dve")
        PS = counted("pe_out", [f"y{g}" for g in range(4)])
        VS = counted("dve_out", [f"y{g}" for g in range(4)])

        with nc.Block() as block:
            @block.sync
            def _(sp):
                had(sp, st)
                for dst, src in ((uc[:], d["uctx"]), (kc[:], d["cspec"].rearrange("a p c -> p a c")), (cf[:], d["cf"]),
                                 (ci[:], d["ci"]), (f2[:], d["f2"]),
                                 (xc[:], d["x2"][:, :, LAT + 2:LAT + 2 + CTX].rearrange("i p c -> p i c"))):
                    sp.dma_start(dst, src).then_inc(ldc, 16)

                def load(i, h):
                    sp.dma_start(q[:, h], d["qspec"][:, :, take(i * P, P)]).then_inc(ld[h], 16)
                    sp.dma_start(x2[:, h, :], d["x2"][take(i, 1), :, 0:LAT]).then_inc(ld[h], 16)

                def store(i, h):
                    sp.wait_ge(VS.sem, VS.at(i, "y3"))
                    sp.dma_start(d["yhy"][:, take(i, 1), 0:LAT], y[:, h, :]).then_inc(st[h], 16)

                load(0, 0)
                load(1, 1)
                for i in range(CB):
                    store(i, i % 2)
                    if i + 2 < CB:
                        load(i + 2, i % 2)
                sp.wait_ge(cdv, 7)
                sp.dma_start(d["yhy"][:, :, LAT:TOK], yc[:]).then_inc(stc, 16)
                sp.wait_ge(stc, 16)
                for h in range(2):
                    sp.wait_ge(st[h], 16 * CB // 2 + HAD)
                retire(sp, s)

            @block.tensor
            def _(pe):
                PS.give(pe)
                pe.wait_ge(ldc, 96)
                for r in range(2):
                    mm = pe.matmul(pc[:, r, :], cf[:, P * r:P * r + P], uc[:], start=True, stop=True)
                mm.then_inc(cpe, 1)
                with pe.Fori(0, CB // 2, 1) as i:
                    for h in range(2):
                        pe.wait_ge(ld[h], 32 * (i + 1))
                        for g in range(4):
                            pe.wait_ge(VS.sem, VS.at(i * 2 + (h - 1), f"y{g}"))
                            for n in range(8):
                                mm = pe.matmul(py[:, g, K1 * n:K1 * n + K1], q[:, h, 8 * g + n, :], f2[:],
                                               start=True, stop=True)
                            mm.then_inc(*PS.inc(f"y{g}"))
                pe.wait_ge(cdv, 6)
                for i in range(CB):
                    for r in range(2):
                        mm = pe.matmul(pc[:, 2, P * i:P * i + P], pr[:, r, P * i:P * i + P], ci[:, P * r:P * r + P],
                                       start=(r == 0), stop=(r == 1))
                mm.then_inc(cpe, 1)

            @block.vector
            def _(v):
                VS.give(v)
                v.wait_ge(cpe, 1)
                v.wait_ge(ldc, 96)
                for n, (r, k) in enumerate(((0, 0), (1, 1), (0, 1), (1, 0))):
                    v.tensor_tensor(pr[:, n, :], pc[:, r, :], kc[:, k, :], ALU.mult).then_inc(cdv, 1)
                v.wait_ge(cdv, 4)
                v.tensor_tensor(pr[:, 0, :], pr[:, 0, :], pr[:, 1, :], ALU.subtract).then_inc(cdv, 1)
                v.wait_ge(cdv, 5)
                v.tensor_tensor(pr[:, 1, :], pr[:, 2, :], pr[:, 3, :], ALU.add).then_inc(cdv, 1)
                with v.Fori(0, CB // 2, 1) as i:
                    for h in range(2):
                        by_n2 = lambda a: a.rearrange("p (a b) -> p b a", b=N2)
                        v.wait_ge(ld[h], 32 * (i + 1))
                        v.wait_ge(st[h], 16 * i + HAD)
                        for g in range(4):
                            v.wait_ge(PS.sem, PS.at(i * 2 + h, f"y{g}"))
                            v.tensor_tensor(by_n2(y[:, h, :])[:, 8 * g:8 * g + 8, :],
                                            py[:, g, :].rearrange("p (b a) -> p b a", a=K1),
                                            by_n2(x2[:, h, :])[:, 8 * g:8 * g + 8, :], ALU.mult)\
                             .then_inc(*VS.inc(f"y{g}"))
                v.wait_ge(cpe, 2)
                v.tensor_tensor(yc[:], pc[:, 2, :].rearrange("p (i c) -> p i c", c=P), xc[:], ALU.mult).then_inc(cdv, 1)


def phase_retention(nc, d, s):
    SL = 4
    LOOP = 12
    with ExitStack() as ctx:
        sb, pb, sem, counted = makers(nc, ctx, s, "retention")
        qkT = sb("qkT5", [P, SL, 2, 512])
        vv = sb("v5", [P, SL, 512])
        gs = sb("gs5", [P, SL, 512])
        sf = sb("sf5", [P, SL, 512])
        kvb = sb("kvb5", [P, SL, 512])
        back_state = sb("back_state", [P, 2, 512])
        dist = sb("dist", [P, 4, P])
        mask = sb("mask", [P, HEADS, P])
        xi = sb("xi", [P, 2, HEADS, P])
        pT = sb("pT", [P, 2, 512])
        qx = sb("qx", [P, 2, 2, 512])
        raw = sb("raw5", [P, 8])
        lg = sb("lg5", [P, 8])
        dec = sb("dec5", [P, 8])
        tmp = sb("tmp5", [P, 5, 8])
        eps = sb("eps5", [P, 1])
        spare = sb("spare", [P, 1])
        stats = sb("stats", [P, 2, HEADS, 6])
        mv = sb("mv", [P, 2, HEADS, 2])
        rstd = sb("rstd5", [P, 2, HEADS])
        on = sb("on", [P, 2, 512])
        y = sb("y5", [P, 2, 512])
        yT = sb("yT", [P, 2, CB, P])
        pS = pb("pS", [P, 2, 512])
        pO = pb("pO", [P, 2, 512])
        pY = pb("pY", [P, 2, 512])
        ldc = sem("ld_c5")
        ld = [sem(f"ld_chunk{m}") for m in range(SL)]
        st = [sem(f"st_yret{h}") for h in range(2)]
        ca, cv, cs = sem("decay_act5"), sem("decay_dve5"), sem("consts5")
        PF = counted("pe_scores", ["s"])
        PO = counted("pe_o", ["o"])
        PY = counted("pe_yT", ["yT"])
        VF = counted("dve_mask", ["p"])
        VB = counted("dve_norm", [f"st{e}" for e in range(HEADS)] + ["spare"] + [f"mv{e}" for e in range(HEADS)] +
                   ["rstd"] + [f"n{e}" for e in range(HEADS)] + ["y"])
        GF = counted("pool_q", ["qf", "qb"])
        GB = counted("pool_state", ["decay", "sum"])
        AB = counted("act_std", ["std"])
        AY = counted("act_yT", ["yT"])
        ROUNDS = NLAT + 1

        def chunk(r):
            return NLAT if isinstance(r, int) and r == NLAT else r * -1 + (NLAT - 1)

        def in_loop(eng, body):
            with eng.Fori(0, LOOP // SL, 1) as i:
                for m in range(SL):
                    body(i * SL + m, m, i)
            for r in range(LOOP, ROUNDS):
                body(r, r % SL, r // SL)

        with nc.Block() as block:
            @block.sync
            def _(sp):
                had(sp, st)
                sp.dma_start(raw[:], d["ret_decay"].partition_broadcast(P)).then_inc(ldc, 16)
                sp.dma_start(dist[:].rearrange("p a b -> p (a b)"), d["dist"]).then_inc(ldc, 16)
                sp.dma_start(back_state[:, 0, :], d["state_b"]).then_inc(ldc, 16)

                def load(r, m, k):
                    t = chunk(r)
                    context = isinstance(r, int) and r == NLAT
                    if not (isinstance(r, int) and r < SL):
                        sp.wait_ge(PO.sem, PO.at(r - SL, "o"))
                        sp.wait_ge(VB.sem, VB.at(r - SL, "y"))
                        sp.wait_ge(GB.sem, GB.at(r - SL, "sum"))
                    sp.dma_start(qkT[:, m].rearrange("p a b -> p (a b)"), d["qkT"][take(t, 1)]).then_inc(ld[m], 16)
                    sp.dma_start(vv[:, m], d["v"][take(t, 1)]).then_inc(ld[m], 16)
                    sp.dma_start(gs[:, m], d["gs"][take(t, 1)]).then_inc(ld[m], 16)
                    if not context:
                        sp.dma_start(sf[:, m], d["state"][take(t, 1)]).then_inc(ld[m], 16)
                        sp.dma_start(kvb[:, m], d["kvb"][take(t, 1)]).then_inc(ld[m], 16)

                for r in range(SL):
                    load(r, r, 0)
                with sp.Fori(1, LOOP // SL + 1, 1) as i:
                    for m in range(SL):
                        load(i * SL + m, m, i)
                load(NLAT, 0, NLAT // SL)
                for h in range(2):
                    sp.wait_ge(st[h], 16 * ((ROUNDS + 1 - h) // 2) + HAD)
                retire(sp, s)

            @block.tensor
            def _(pe):
                PF.give(pe)
                PO.give(pe)
                PY.give(pe)
                pe.wait_ge(ldc, 48)

                def scores(r, m, k):
                    context = isinstance(r, int) and r == NLAT
                    pe.wait_ge(ld[m], 80 * k + (48 if context else 80))
                    pe.wait_ge(VF.sem, VF.at(r - 2, "p"))
                    for e in range(HEADS):
                        cut = slice(P * e, P * e + P)
                        mm = pe.matmul(pS[:, m % 2, cut], qkT[:, m, 1, cut], qkT[:, m, 0, cut], start=True, stop=True)
                    mm.then_inc(*PF.inc("s"))

                def outputs(r, m):
                    context = isinstance(r, int) and r == NLAT
                    h = m % 2
                    pe.wait_ge(VF.sem, VF.at(r, "p"))
                    pe.wait_ge(GF.sem, GF.at(r, "qb"))
                    pe.wait_ge(VB.sem, VB.at(r - 2, "n3"))
                    if not context:
                        pe.wait_ge(GB.sem, GB.at(r - 1, "sum"))
                    for e in range(HEADS):
                        cut = slice(P * e, P * e + P)
                        mm = pe.matmul(pO[:, h, cut], pT[:, h, cut], vv[:, m, cut], start=True, stop=context)
                        if not context:
                            pe.matmul(pO[:, h, cut], qx[:, h, 0, cut], sf[:, m, cut], start=False, stop=False)
                            mm = pe.matmul(pO[:, h, cut], qx[:, h, 1, cut], back_state[:, h, cut],
                                           start=False, stop=True)
                    mm.then_inc(*PO.inc("o"))

                def turn(r, h):
                    pe.wait_ge(VB.sem, VB.at(r, "y"))
                    pe.wait_ge(AY.sem, AY.at(r - 2, "yT"))
                    for e in range(HEADS):
                        cut = slice(P * e, P * e + P)
                        mm = pe.transpose(pY[:, h, cut], y[:, h, cut], s["ident"][:])
                    mm.then_inc(*PY.inc("yT"))

                scores(0, 0, 0)
                scores(1, 1, 0)
                outputs(0, 0)
                with pe.Fori(0, LOOP // SL, 1) as i:
                    for m in range(SL):
                        r, slot = i * SL + (m + 1), (m + 1) % SL
                        scores(i * SL + (m + 2), (m + 2) % SL, i + (m + 2) // SL)
                        turn(i * SL + m, m % 2)
                        outputs(r, slot)
                for r in range(LOOP + 1, ROUNDS):
                    if r + 1 < ROUNDS:
                        scores(r + 1, (r + 1) % SL, (r + 1) // SL)
                    turn(r - 1, (r - 1) % 2)
                    outputs(r, r % SL)
                turn(ROUNDS - 1, (ROUNDS - 1) % 2)

            @block.scalar
            def _(act):
                AB.give(act)
                AY.give(act)
                log_decays_scalar(act, tmp, ca, cv)
                act.wait_ge(cv, 9)
                act.wait_ge(ldc, 48)
                act.activation(dec[:], lg[:], ACT.Exp, scale=float(P)).then_inc(cs, 1)
                for n in range(2):
                    for e in range(HEADS):
                        act.activation(xi[:, n, e, :], dist[:, 2 + n, :], ACT.Exp,
                                       scale=lg[:, 4 * n + e:4 * n + e + 1]).then_inc(cs, 1)
                act.wait_ge(cv, 17)
                act.activation(mask[:], mask[:], ACT.Exp).then_inc(ca, 1)
                act.wait_ge(cv, 19)

                def body(r, m, k):
                    h = m % 2
                    act.wait_ge(VB.sem, VB.at(r, "mv3"))
                    act.activation(rstd[:, h, :], mv[:, h, :, 1], ACT.Sqrt, bias=eps[:]).then_inc(*AB.inc("std"))

                def copy(r, m, k, stored):
                    h = m % 2
                    act.wait_ge(PY.sem, PY.at(r, "yT"))
                    act.wait_ge(st[h], stored + HAD)
                    act.activation(yT[:, h].rearrange("p a b -> p (a b)"), pY[:, h, :], ACT.Copy)\
                       .then_inc(*AY.inc("yT"))
                    act.wait_ge(AY.sem, AY.at(r, "yT"))
                    act.dma_start(d["yret"][:, :, take(chunk(r) * P, P)], yT[:, h]).then_inc(st[h], 16)

                body(0, 0, 0)
                with act.Fori(0, LOOP // SL, 1) as i:
                    for m in range(SL):
                        body(i * SL + (m + 1), (m + 1) % SL, i)
                        copy(i * SL + m, m, i, 16 * (i * 2 + m // 2))
                for r in range(LOOP + 1, ROUNDS + 1):
                    if r < ROUNDS:
                        body(r, r % SL, 0)
                    copy(r - 1, (r - 1) % SL, 0, 16 * ((r - 1) // 2))

            @block.vector
            def _(v):
                VF.give(v)
                VB.give(v)
                v.wait_ge(ldc, 48)
                log_decays_vector(v, lg, raw, tmp, ca, cv)
                v.wait_ge(cv, 9)
                for e in range(HEADS):
                    v.tensor_scalar(mask[:, e, :], dist[:, 0, :], lg[:, e:e + 1], None, ALU.mult).then_inc(cv, 1)
                v.wait_ge(cv, 13)
                for e in range(HEADS):
                    v.scalar_tensor_tensor(mask[:, e, :], dist[:, 1, :], lg[:, 4 + e:5 + e], mask[:, e, :],
                                           ALU.mult, ALU.add).then_inc(cv, 1)
                v.wait_ge(ca, 3)
                v.tensor_tensor(mask[:], mask[:], s["ident"][:].unsqueeze(1).broadcast_to([P, HEADS, P]), ALU.add)\
                 .then_inc(cv, 1)
                v.memset(eps[:], EPS).then_inc(cv, 1)
                v.wait_ge(cv, 19)

                def masked(r, h):
                    v.wait_ge(PF.sem, PF.at(r, "s"))
                    v.wait_ge(PO.sem, PO.at(r - 2, "o"))
                    v.tensor_tensor(pT[:, h, :], pS[:, h, :], mask[:].rearrange("p e c -> p (e c)"), ALU.mult)\
                     .then_inc(*VF.inc("p"))

                def norm(r, m):
                    h = m % 2
                    v.wait_ge(PO.sem, PO.at(r, "o"))
                    v.wait_ge(PY.sem, PY.at(r - 2, "yT"))
                    for e in range(HEADS):
                        v.bn_stats(stats[:, h, e, :], pO[:, h, P * e:P * e + P]).then_inc(*VB.inc(f"st{e}"))
                    v.wait_ge(VB.sem, VB.at(r, "st3"))
                    v.memset(spare[:], 0.0).then_inc(*VB.inc("spare"))
                    for e in range(HEADS):
                        v.bn_aggr(mv[:, h, e, :], stats[:, h, e, :]).then_inc(*VB.inc(f"mv{e}"))
                    v.wait_ge(AB.sem, AB.at(r, "std"))
                    v.reciprocal(rstd[:, h, :], rstd[:, h, :]).then_inc(*VB.inc("rstd"))
                    v.wait_ge(VB.sem, VB.at(r, "rstd"))
                    for e in range(HEADS):
                        cut = slice(P * e, P * e + P)
                        v.tensor_scalar(on[:, h, cut], pO[:, h, cut], mv[:, h, e, 0:1], rstd[:, h, e:e + 1],
                                        ALU.subtract, ALU.mult).then_inc(*VB.inc(f"n{e}"))
                    v.wait_ge(VB.sem, VB.at(r, "n3"))
                    v.tensor_tensor(y[:, h, :], on[:, h, :], gs[:, m, :], ALU.mult).then_inc(*VB.inc("y"))

                masked(0, 0)
                with v.Fori(0, LOOP // SL, 1) as i:
                    for m in range(SL):
                        masked(i * SL + (m + 1), (m + 1) % 2)
                        norm(i * SL + m, m)
                for r in range(LOOP, ROUNDS):
                    if r + 1 < ROUNDS:
                        masked(r + 1, (r + 1) % 2)
                    norm(r, r % SL)

            @block.gpsimd
            def _(g):
                GF.give(g)
                GB.give(g)
                g.wait_ge(cs, 9)
                g.wait_ge(ldc, 48)

                def front(r, m, k):
                    h = m % 2
                    context = isinstance(r, int) and r == NLAT
                    g.wait_ge(ld[m], 80 * k + (48 if context else 80))
                    g.wait_ge(PO.sem, PO.at(r - 2, "o"))
                    for n, name in enumerate(("qf", "qb")):
                        g.tensor_tensor(qx[:, h, n, :], qkT[:, m, 0, :], xi[:, n].rearrange("p e c -> p (e c)"),
                                        ALU.mult).then_inc(*GF.inc(name))

                def state(r, m, k):
                    h = m % 2
                    g.wait_ge(GB.sem, GB.at(r - 1, "sum"))
                    g.wait_ge(PO.sem, PO.at(r - 1, "o"))
                    heads = lambda a: a.rearrange("p (e c) -> p e c", e=HEADS)
                    g.tensor_tensor(heads(back_state[:, 1 - h, :]), heads(back_state[:, h, :]),
                                    dec[:, 4:8].unsqueeze(2).broadcast_to([P, HEADS, P]), ALU.mult)\
                     .then_inc(*GB.inc("decay"))
                    g.wait_ge(GB.sem, GB.at(r, "decay"))
                    g.tensor_tensor(back_state[:, 1 - h, :], back_state[:, 1 - h, :], kvb[:, m, :], ALU.add)\
                     .then_inc(*GB.inc("sum"))

                front(0, 0, 0)
                with g.Fori(0, LOOP // SL, 1) as i:
                    for m in range(SL):
                        front(i * SL + (m + 1), (m + 1) % SL, i + (m + 1) // SL)
                        state(i * SL + m, m, i)
                for r in range(LOOP, NLAT):
                    front(r + 1, (r + 1) % SL, (r + 1) // SL)
                    state(r, r % SL, r // SL)


def phase_merge(nc, d, s):
    with ExitStack() as ctx:
        sb, pb, sem, counted = makers(nc, ctx, s, "merge")
        wg = sb("w_gates", [P, KT, 2 * DM])
        wh = sb("w_hy_o", [P, CB, DM])
        wr = sb("w_ret_o", [P, CB, DM])
        hT = sb("hT6", [P, 2, KT, 512])
        yh = sb("yh", [P, 2, CB, 512])
        yr = sb("yr", [P, 2, CB, 512])
        gate = sb("gate", [P, 2, 2, 512])
        part = sb("part", [P, 2, 512])
        m = sb("m6", [P, 2, 512])
        pg = pb("pg", [P, 2, 2, 512])
        py = pb("py6", [P, 2, 2, 512])
        wld = [sem(f"ld_wg{n}") for n in range(2)]
        wyl = sem("ld_wy")
        ld = [sem(f"ld_blk{h}") for h in range(2)]
        st = [sem(f"st_m{h}") for h in range(2)]
        names = ("gh", "gr", "yh", "yr")
        PS = counted("pe_merge", [f"{n}{c}" for c in range(KT) for n in names])
        AS = counted("act_merge", [f"{n}{c}" for c in range(KT) for n in names[:2]])
        VS = counted("dve_merge", [f"{n}{c}" for c in range(KT) for n in ("a", "b", "m")])

        def last(steps, i, name, c):
            return steps.at(i, f"{name}{c - 2}") if c >= 2 else steps.at(i - 1, f"{name}{c + KT - 2}")

        def in_loop(eng, body):
            with eng.Fori(0, 2, 1) as i:
                for h in range(2):
                    body(i * 2 + h, h, i, 512)
            body(4, 0, 2, CTX)

        with nc.Block() as block:
            @block.sync
            def _(sp):
                had(sp, st)
                def load(b, h, n):
                    cols = bass.ds(b * 512, n)
                    sp.dma_start(hT[:, h, :, 0:n], d["hT"][:, :, cols]).then_inc(ld[h], 16)
                    sp.dma_start(yh[:, h, :, 0:n], d["yhy"][:, :, cols]).then_inc(ld[h], 16)
                    sp.dma_start(yr[:, h, :, 0:n], d["yret"][:, :, cols]).then_inc(ld[h], 16)

                sp.dma_start(wg[:, :, 0:DM], d["w_gates"][:, :, 0:DM]).then_inc(wld[0], 16)
                load(0, 0, 512)
                sp.dma_start(wg[:, :, DM:2 * DM], d["w_gates"][:, :, DM:2 * DM]).then_inc(wld[1], 16)
                sp.dma_start(wh[:], d["w_hy_o"]).then_inc(wyl, 16)
                sp.dma_start(wr[:], d["w_ret_o"]).then_inc(wyl, 16)
                load(1, 1, 512)
                def store(b, n):
                    for c in range(KT):
                        sp.wait_ge(VS.sem, VS.at(b, f"m{c}"))
                        sp.dma_start(d["merged"][:, c, bass.ds(b * 512, n)], m[:, c % 2, 0:n]).then_inc(st[c % 2], 16)

                with sp.Fori(0, 1, 1) as i:
                    for h in range(2):
                        store(i * 2 + h, 512)
                        load(i * 2 + (h + 2), h, 512)
                store(2, 512)
                load(4, 0, CTX)
                store(3, 512)
                store(4, CTX)
                for h in range(2):
                    sp.wait_ge(st[h], 16 * 5 * KT // 2 + HAD)
                retire(sp, s)

            @block.tensor
            def _(pe):
                PS.give(pe)
                pe.wait_ge(wld[0], 16)
                pe.wait_ge(wld[1], 16)
                pe.wait_ge(wyl, 32)

                def body(b, h, k, n):
                    pe.wait_ge(ld[h], 48 * (k + 1))
                    for c in range(KT):
                        p = c % 2
                        for j in range(2):
                            name = names[j]
                            pe.wait_ge(AS.sem, last(AS, b, name, c))
                            for q in range(KT):
                                mm = pe.matmul(pg[:, p, j, 0:n], wg[:, q, DM * j + P * c:DM * j + P * c + P],
                                               hT[:, h, q, 0:n], start=(q == 0), stop=(q == KT - 1))
                            mm.then_inc(*PS.inc(f"{name}{c}"))
                        for j, (w, y) in enumerate(((wh, yh), (wr, yr))):
                            pe.wait_ge(VS.sem, last(VS, b, "ab"[j], c))
                            for q in range(CB):
                                mm = pe.matmul(py[:, p, j, 0:n], w[:, q, P * c:P * c + P], y[:, h, q, 0:n],
                                               start=(q == 0), stop=(q == CB - 1))
                            mm.then_inc(*PS.inc(f"{names[2 + j]}{c}"))

                in_loop(pe, body)

            @block.scalar
            def _(act):
                AS.give(act)

                def body(b, h, k, n):
                    for c in range(KT):
                        for j in range(2):
                            act.wait_ge(VS.sem, last(VS, b, "ab"[j], c))
                            act.wait_ge(PS.sem, PS.at(b, f"{names[j]}{c}"))
                            act.activation(gate[:, c % 2, j, 0:n], pg[:, c % 2, j, 0:n], ACT.Sigmoid)\
                               .then_inc(*AS.inc(f"{names[j]}{c}"))

                in_loop(act, body)

            @block.vector
            def _(v):
                VS.give(v)

                def body(b, h, k, n):
                    for c in range(KT):
                        p = c % 2
                        v.wait_ge(AS.sem, AS.at(b, f"gh{c}"))
                        v.wait_ge(PS.sem, PS.at(b, f"yh{c}"))
                        v.wait_ge(st[p], 16 * (k * 8 + h * 4 + c // 2) + HAD)
                        v.tensor_tensor(m[:, p, 0:n], py[:, p, 0, 0:n], gate[:, p, 0, 0:n], ALU.mult)\
                         .then_inc(*VS.inc(f"a{c}"))
                        v.wait_ge(AS.sem, AS.at(b, f"gr{c}"))
                        v.wait_ge(PS.sem, PS.at(b, f"yr{c}"))
                        v.tensor_tensor(part[:, p, 0:n], py[:, p, 1, 0:n], gate[:, p, 1, 0:n], ALU.mult)\
                         .then_inc(*VS.inc(f"b{c}"))
                        v.wait_ge(VS.sem, VS.at(b, f"b{c}"))
                        v.tensor_tensor(m[:, p, 0:n], m[:, p, 0:n], part[:, p, 0:n], ALU.add)\
                         .then_inc(*VS.inc(f"m{c}"))

                in_loop(v, body)


ROW = DM + NE


def phase_out(nc, d, s):
    LOOP = NLAT - 2
    with ExitStack() as ctx:
        sb, pb, sem, counted = makers(nc, ctx, s, "out")
        wh = sb("w_out_high", [P, KT, DM], F32R)
        wl = sb("w_out_low", [P, KT, DM], F32R)
        w = sb("w_out", [P, KT, DM])
        wr = sb("w_router", [P, KT, NE])
        gate = sb("gate1", [P, 2, DM])
        scale = sb("scale2", [P, 2, DM])
        shift = sb("shift2", [P, 2, DM])
        gn = sb("gn2", [P, DM])
        mh = sb("mT_high", [P, 2, KT, P], F32R)
        ml = sb("mT_low", [P, 2, KT, P], F32R)
        mT = sb("mT", [P, 2, KT, P])
        x = sb("x6", [P, 2, DM])
        t1 = sb("t1", [P, DM])
        junk = sb("junk6", [P, DM])
        row = sb("row", [P, 2, ROW])
        hT = sb("h2T", [P, KT, P])
        ssq = sb("ssq6", [P, 2])
        eps = sb("eps6", [P, 1])
        mx = sb("mx", [P, 2])
        ex = sb("ex", [P, 2, NE])
        sm = sb("sm", [P, 2])
        po = pb("po", [P, 2, DM])
        tp = pb("tp6", [P, DM])
        pr = pb("pr", [P, NE])
        ldw = sem("ld_w6")
        wld = [sem(f"ld_wout{j}") for j in range(2)]
        w_act, w_dve = sem("w_high_ready"), sem("w_split")
        mld = [sem(f"ld_m{h}") for h in range(2)]
        ld = [sem(f"ld_t{h}") for h in range(2)]
        xst = [sem(f"st_x{h}") for h in range(2)]
        rst = [sem(f"st_row{h}") for h in range(2)]
        cv = sem("consts6")
        PF = counted("pe_proj", ["o"])
        PB = counted("pe_rt", ["hT", "r"])
        AF, VF = counted("act_m", ["high"]), counted("dve_m", ["low"])
        AB = counted("act_rt", ["sq", "std", "hT", "ex"])
        VB = counted("dve_rt", ["t1", "x", "rstd", "h2a", "h2", "hT", "mx", "rs", "aff", "row"])

        with nc.Block() as block:
            @block.sync
            def _(sp):
                had(sp, xst, rst)
                def load(t, h, at):
                    sp.wait_ge(VF.sem, VF.at(t - 2, "low"))
                    sp.dma_start(mT[:, h], d["merged"][:, :, take(at, P)]).then_inc(mld[h], 16)

                def load_x(t, h, k):
                    sp.wait_ge(VB.sem, VB.at(t - 2, "h2a"))
                    sp.wait_ge(xst[h], 16 * k + HAD)
                    sp.dma_start(x[:, h, :], d["xs"][take(t, 1)]).then_inc(ld[h], 16)

                def stores(t, h, k, more):
                    at, ahead = (t * P, (t + 2) * P) if isinstance(t, int) else (sp.snap(t * P), sp.snap((t + 2) * P))
                    sp.wait_ge(VB.sem, VB.at(t, "x"))
                    sp.dma_start(d["xacc"][take(at, P), :], x[:, h, :]).then_inc(xst[h], 16)
                    if more:
                        load(t + 2, h, ahead)
                        load_x(t + 2, h, k + 1)
                    sp.wait_ge(VB.sem, VB.at(t, "row"))
                    sp.dma_start(d["h2"][take(at, P), :], row[:, h, :]).then_inc(rst[h], 16)

                load(0, 0, 0)
                for j in range(2):
                    sp.dma_start(w[:, :, 512 * j:512 * j + 512], d["w_out"][:, :, 512 * j:512 * j + 512])\
                      .then_inc(wld[j], 16)
                load(1, 1, P)
                sp.dma_start(wr[:], d["w_router"]).then_inc(ldw, 16)
                sp.dma_start(gn[:], d["norm2_g"].partition_broadcast(P)).then_inc(ldw, 16)
                for n in range(2):
                    for dst, col in ((gate, 2), (shift, 3), (scale, 4)):
                        sp.dma_start(dst[:, n, :], d["mod"][n:n + 1, DM * col:DM * col + DM].partition_broadcast(P))\
                          .then_inc(ldw, 16)
                load_x(0, 0, 0)
                load_x(1, 1, 0)
                with sp.Fori(0, LOOP // 2, 1) as i:
                    for h in range(2):
                        stores(i * 2 + h, h, i, True)
                for t in range(LOOP, NT):
                    stores(t, t % 2, t // 2, t + 2 < NT)
                for h in range(2):
                    sp.wait_ge(xst[h], 16 * ((NT + 1 - h) // 2) + HAD)
                    sp.wait_ge(rst[h], 16 * ((NT + 1 - h) // 2) + HAD)
                retire(sp, s)

            @block.tensor
            def _(pe):
                PF.give(pe)
                PB.give(pe)

                def front(t, h, k):
                    pe.wait_ge(AF.sem, AF.at(t, "high"))
                    pe.wait_ge(VF.sem, VF.at(t, "low"))
                    pe.wait_ge(VB.sem, VB.at(t - 2, "t1"))
                    for j in range(2):
                        pe.wait_ge(w_dve, j + 1)
                        cols = slice(512 * j, 512 * j + 512)
                        for q in range(KT):
                            mm = product(pe, po[:, h, cols], (mh[:, h, q, :], ml[:, h, q, :]), (wh[:, q, cols], wl[:, q, cols]),
                                         q == 0, q == KT - 1)
                    mm.then_inc(*PF.inc("o"))

                def back(t, h):
                    pe.wait_ge(VB.sem, VB.at(t, "h2"))
                    pe.wait_ge(AB.sem, AB.at(t - 1, "hT"))
                    for q in range(KT):
                        mm = pe.transpose(tp[:, P * q:P * q + P], row[:, h, P * q:P * q + P], s["ident"][:])
                    mm.then_inc(*PB.inc("hT"))
                    pe.wait_ge(VB.sem, VB.at(t, "hT"))
                    pe.wait_ge(AB.sem, AB.at(t, "hT"))
                    for q in range(KT):
                        mm = pe.matmul(pr[:], hT[:, q, :], wr[:, q, :], start=(q == 0), stop=(q == KT - 1))
                    mm.then_inc(*PB.inc("r"))

                front(0, 0, 0)
                pe.wait_ge(ldw, 16 * 8)
                with pe.Fori(0, LOOP // 2, 1) as i:
                    for h in range(2):
                        front(i * 2 + (h + 1), 1 - h, i + h)
                        back(i * 2 + h, h)
                for t in range(LOOP, NT):
                    if t + 1 < NT:
                        front(t + 1, (t + 1) % 2, (t + 1) // 2)
                    back(t, t % 2)

            @block.scalar
            def _(act):
                AB.give(act)
                AF.give(act)
                act.wait_ge(cv, 1)

                def front(t, h, k):
                    act.wait_ge(mld[h], 16 * (k + 1))
                    act.wait_ge(PF.sem, PF.at(t - 2, "o"))
                    act.activation(mh[:, h].rearrange("p a b -> p (a b)"),
                                   mT[:, h].rearrange("p a b -> p (a b)"), ACT.Copy).then_inc(*AF.inc("high"))

                def back(t, h, k, more):
                    act.wait_ge(VB.sem, VB.at(t, "x"))
                    act.activation(junk[:], x[:, h, :], ACT.Square, scale=DM ** -0.5, accum_out=ssq[:, h:h + 1])\
                       .then_inc(*AB.inc("sq"))
                    act.wait_ge(AB.sem, AB.at(t, "sq"))
                    act.activation(ssq[:, h:h + 1], ssq[:, h:h + 1], ACT.Sqrt, bias=eps[:]).then_inc(*AB.inc("std"))
                    act.wait_ge(PB.sem, PB.at(t, "hT"))
                    act.wait_ge(PB.sem, PB.at(t - 1, "r"))
                    act.activation(hT[:, 0:4].rearrange("p a b -> p (a b)"), tp[:, 0:512], ACT.Copy)\
                       .then_inc(*AB.inc("hT"))
                    if more:
                        front(t + 2, h, k + 1)
                    act.wait_ge(VB.sem, VB.at(t, "mx"))
                    act.activation(ex[:, h, :], pr[:], ACT.Exp, bias=mx[:, h:h + 1], accum_out=sm[:, h:h + 1])\
                       .then_inc(*AB.inc("ex"))

                front(0, 0, 0)
                front(1, 1, 0)
                for j in range(2):
                    act.wait_ge(wld[j], 16)
                    act.activation(wh[:, :, 512 * j:512 * j + 512], w[:, :, 512 * j:512 * j + 512], ACT.Copy)\
                       .then_inc(w_act, 1)
                with act.Fori(0, LOOP // 2, 1) as i:
                    for h in range(2):
                        back(i * 2 + h, h, i, True)
                for t in range(LOOP, NT):
                    back(t, t % 2, t // 2, t + 2 < NT)

            @block.vector
            def _(v):
                VB.give(v)
                v.memset(eps[:], EPS).then_inc(cv, 1)

                def front(t, h):
                    v.wait_ge(AF.sem, AF.at(t, "high"))
                    v.tensor_tensor(ml[:, h].rearrange("p a b -> p (a b)"), mT[:, h].rearrange("p a b -> p (a b)"), mh[:, h].rearrange("p a b -> p (a b)").bitcast(F32),
                                    ALU.subtract).then_inc(*VF.inc("low"))

                VF.give(v)
                front(0, 0)
                front(1, 1)
                for j in range(2):
                    v.wait_ge(w_act, j + 1)
                    v.tensor_tensor(wl[:, :, 512 * j:512 * j + 512], w[:, :, 512 * j:512 * j + 512], wh[:, :, 512 * j:512 * j + 512].bitcast(F32), ALU.subtract)\
                     .then_inc(w_dve, 1)
                v.wait_ge(ldw, 16 * 8)
                v.scalar_tensor_tensor(scale[:], scale[:], 1.0, gn[:].unsqueeze(1).broadcast_to([P, 2, DM]),
                                       ALU.add, ALU.mult).then_inc(cv, 1)
                v.wait_ge(cv, 2)

                def back(t, h, k, n, more):
                    v.wait_ge(PF.sem, PF.at(t, "o"))
                    v.tensor_tensor(t1[:], po[:, h, :], gate[:, n, :], ALU.mult).then_inc(*VB.inc("t1"))
                    v.wait_ge(ld[h], 16 * (k + 1))
                    v.wait_ge(VB.sem, VB.at(t, "t1"))
                    v.tensor_tensor(x[:, h, :], x[:, h, :], t1[:], ALU.add).then_inc(*VB.inc("x"))
                    v.wait_ge(AB.sem, AB.at(t, "std"))
                    v.reciprocal(ssq[:, h:h + 1], ssq[:, h:h + 1]).then_inc(*VB.inc("rstd"))
                    v.wait_ge(rst[h], 16 * k + HAD)
                    v.wait_ge(VB.sem, VB.at(t, "rstd"))
                    v.scalar_tensor_tensor(row[:, h, 0:DM], x[:, h, :], ssq[:, h:h + 1], scale[:, n, :],
                                           ALU.mult, ALU.mult).then_inc(*VB.inc("h2a"))
                    v.wait_ge(VB.sem, VB.at(t, "h2a"))
                    v.tensor_tensor(row[:, h, 0:DM], row[:, h, 0:DM], shift[:, n, :], ALU.add).then_inc(*VB.inc("h2"))
                    v.wait_ge(PB.sem, PB.at(t, "hT"))
                    v.wait_ge(PB.sem, PB.at(t - 1, "r"))
                    v.tensor_copy(hT[:, 4:8].rearrange("p a b -> p (a b)"), tp[:, 512:DM]).then_inc(*VB.inc("hT"))
                    if more:
                        front(t + 2, h)
                    v.wait_ge(PB.sem, PB.at(t, "r"))
                    v.tensor_reduce(mx[:, h:h + 1], pr[:], AX.X, ALU.max, negate=True).then_inc(*VB.inc("mx"))
                    v.wait_ge(AB.sem, AB.at(t, "ex"))
                    v.reciprocal(sm[:, h:h + 1], sm[:, h:h + 1]).then_inc(*VB.inc("rs"))
                    v.wait_ge(VB.sem, VB.at(t, "rs"))
                    v.tensor_scalar(s["aff"][:, take(t, 1), :].squeeze(1) if isinstance(t, int) else
                                    s["aff"][:, take(t, 1), :], ex[:, h, :], sm[:, h:h + 1], None, ALU.mult)\
                     .then_inc(*VB.inc("aff"))
                    v.tensor_scalar(row[:, h, DM:ROW], ex[:, h, :], sm[:, h:h + 1], None, ALU.mult)\
                     .then_inc(*VB.inc("row"))

                with v.Fori(0, LOOP // 2, 1) as i:
                    for h in range(2):
                        back(i * 2 + h, h, i, 0, True)
                for t in range(LOOP, NT):
                    back(t, t % 2, t // 2, int(t == NLAT), t + 2 < NT)


SLOTS = CAP + CCAP
GROUPS = [(0, P), (P, P), (CAP, CCAP)]
CTX_LO = CAP + 2 * CCAP
HID = CTX_LO + CCAP + CAP


def phase_experts(nc, d, s):
    BITS = 30
    with ExitStack() as ctx:
        sb, pb, sem, counted = makers(nc, ctx, s, "experts")
        wg = sb("wg", [P, 4, KT, 256])
        wu = sb("wu", [P, 4, KT, 256])
        wdh = sb("w_down_high", [P, 4, 2, DM], F32R)
        wdl = sb("w_down_low", [P, 4, 2, DM], F32R)
        raw = sb("w_down_row", [P, DM])
        caps = sb("caps", [P, 2])
        slot = sb("slot", [P, CAP])
        thr = sb("thr", [P, 2], I32)
        cand = sb("cand", [P, 2], I32)
        bit = sb("bit", [P, 2], I32)
        cnt = sb("cnt", [P, 2])
        met = sb("met", [P, 2], I32)
        need = sb("need", [P, 2])
        pos = sb("pos", [P, 3, P])
        ends = sb("ends", [P, 2])
        below = sb("below", [P, NLAT, CAP], BF16)
        below_c = sb("below_c", [P, CCAP], BF16)
        ones = sb("ones", [P, 1], BF16)
        ids = sb("ids", [P, 2, 3], I32)
        sids = sb("sids", [P, 2, 3], I32)
        vals = sb("vals", [P, 2, 3])
        xs = sb("xg", [P, 3, ROW])
        xT = sb("xT9", [P, KT, SLOTS])
        act_g = sb("act_g", [P, SLOTS])
        full = sb("full", [P, SLOTS])
        hid = sb("hid", [P, KT, HID], F32R)
        clow = sb("clow", [CCAP, 512])
        ye = sb("ye", [P, 3, DM])
        arr, prob, over, tie, scan = (ye[:].rearrange("p a b -> p (a b)")[:, 3 * P * n:3 * P * n + 3 * P]
                                      .rearrange("p (a b) -> p a b", b=P) for n in range(5))
        seg = ye[:].rearrange("p a b -> p (a b)")[:, 15 * P:17 * P]
        gate2 = sb("gate2", [P, 2, DM])
        pg = pb("pg9", [P, 2, 512])
        pu = pb("pu9", [P, 2, 512])
        px = pb("px9", [P, 2, 512])
        pi = pb("pi9", [P, 512])

        ldc = sem("ld_c9")
        gld = [sem(f"ld_g{j}") for j in range(4)]
        uld = [sem(f"ld_u{j}") for j in range(4)]
        rld = sem("ld_d")
        ga = sem("gather")
        sc = [sem(f"added{h}") for h in range(2)]
        pc = sem("pool_spare")
        CG, CP = counted("pool_gather", ["carry"]), counted("pool_add", ["before", "added"])
        spare = sb("spare9", [P, 4])
        R0 = counted("dve_arrange", ["zero", "a0", "a1", "ac", "prob", "thr", "bit"])
        RB = counted("dve_bits", ["cand", "cl", "cc", "met", "bit", "thr"])
        R1 = counted("dve_slots", ["gl", "gc", "need", "tl", "tc", "s0", "s1", "e0", "e1", "lim", "k0", "k1",
                                          "sel", "p0", "p1", "f0", "f1", "off", "q0", "q1", "pos", "ones"])
        QB = counted("pe_bits", ["sum"])
        Q1 = counted("pe_route", ["prob", "above", "ahead", "slots", "pos"])
        PG = counted("pe_gu", [f"{n}{f}" for f in range(KT) for n in "gu"])
        PI = counted("pe_ids", ["ids"])
        PX = counted("pe_xT", [f"x{k}" for k in range(KT)])
        PD = counted("pe_dn", [f"d{n}" for n in range(6)])
        AG = counted("act_g", [f"g{f}" for f in range(KT)])
        AX = counted("act_xT", [f"x{k}" for k in range(KT)])
        VG = counted("dve_hid", [f"{n}{f}" for f in range(KT) for n in "mlh"])
        AH = counted("act_hid", [f"h{f}" for f in range(KT)])
        AW, VW = counted("act_wd", [f"w{f}" for f in range(KT)]), counted("dve_wd", [f"w{f}" for f in range(KT)])
        AC, VC = counted("act_ctx", ["c0", "c1"]), counted("dve_ctx", ["sum0", "sum1"])
        empty = sem("empty")
        VM = counted("dve_below", [f"m{n}" for n in range(NLAT)] + ["mc"])
        VI = counted("dve_ids", ["i0", "i2"])
        VX = counted("dve_keep", ["s0", "s2", "v0", "v2"])
        VD = counted("dve_dn", [f"d{n}" for n in range(6)])
        LOOP = NE - 2

        def experts(eng, body):
            with eng.Fori(0, LOOP // 2, 1) as i:
                for h in range(2):
                    body(i * 2 + h, h, i, True, True)
            for e in range(LOOP, NE):
                body(e, e % 2, e // 2, e + 1 < NE, e + 2 < NE)

        with nc.Block() as block:
            @block.sync
            def _(sp):
                for dst, src in ((seg, d["seg"]), (caps[:], d["caps"]), (slot[:], d["slot"])):
                    sp.dma_start(dst, src).then_inc(ldc, 16)
                for n in range(2):
                    sp.dma_start(gate2[:, n, :], d["mod"][n:n + 1, 5 * DM:6 * DM].partition_broadcast(P)).then_inc(ldc, 16)

                def load_gate_up(e, j):
                    sp.dma_start(wg[:, j], d["w_gate"][take(e, 1), j]).then_inc(gld[j], 16)
                    sp.dma_start(wu[:, j], d["w_up"][take(e, 1), j]).then_inc(uld[j], 16)

                def loads(e, more):
                    for f in range(KT):
                        sp.wait_ge(VW.sem, VW.at(e, f"w{f - 1}") if f else VW.at(e - 1, f"w{KT - 1}"))
                        sp.dma_start(raw[:].unsqueeze(1), d["w_down"][take(e, 1), f // 2, :, f % 2, :].rearrange("e p c -> p e c"))\
                          .then_inc(rld, 16)
                        if more and f >= 2 and f % 2 == 0:
                            sp.wait_ge(PG.sem, PG.at(e, f"u{f - 1}"))
                            load_gate_up(e + 1, f // 2 - 1)
                    if more:
                        sp.wait_ge(PG.sem, PG.at(e, f"u{KT - 1}"))
                        load_gate_up(e + 1, 3)

                for j in range(4):
                    load_gate_up(0, j)
                with sp.Fori(0, NE - 1, 1) as e:
                    loads(e, True)
                loads(NE - 1, False)
                sp.wait_ge(VW.sem, VW.at(NE - 1, f"w{KT - 1}"))
                retire(sp, s)

            @block.tensor
            def _(pe):
                for steps in (PG, PI, PX, PD):
                    steps.give(pe)
                for steps in (QB, Q1):
                    steps.give(pe)
                pe.wait_ge(R0.sem, R0.at(0, "ac"))
                for n in range(3):
                    mm = pe.transpose(px[:, 0, P * n:P * n + P], arr[:, n, :], s["ident"][:])
                mm.then_inc(*Q1.inc("prob"))
                pe.wait_ge(ldc, 80)
                with pe.Fori(0, BITS, 1) as i:
                    pe.wait_ge(RB.sem, RB.at(i, "cc"))
                    pe.matmul(pi[:, 0:2], seg[:, 0:P], cnt[:], start=True, stop=True).then_inc(*QB.inc("sum"))
                for name, ready, half, src in (("above", "gc", 0, cnt), ("ahead", "e1", 1, ends), ("slots", "f1", 1, ends)):
                    pe.wait_ge(R1.sem, R1.at(0, ready))
                    pe.matmul(pi[:, 0:2], seg[:, P * half:P * half + P], src[:], start=True, stop=True)\
                      .then_inc(*Q1.inc(name))
                pe.wait_ge(R1.sem, R1.at(0, "q1"))
                for n in range(3):
                    mm = pe.transpose(px[:, 1, P * n:P * n + P], scan[:, n, :], s["ident"][:])
                mm.then_inc(*Q1.inc("pos"))
                pe.wait_ge(R1.sem, R1.at(0, "ones"))

                def index(e):
                    pe.wait_ge(VM.sem, VM.at(e, "mc"))
                    pe.wait_ge(VI.sem, VI.at(e - 1, "i2"))
                    for half in range(2):
                        for n in range(NLAT):
                            pe.matmul(pi[:, half:half + 1], below[:, n, P * half:P * half + P], ones[:],
                                      start=(n == 0), stop=(n == NLAT - 1))
                    pe.matmul(pi[0:CCAP, 2:3], below_c[:], ones[:], start=True, stop=True).then_inc(*PI.inc("ids"))

                def turn(e):
                    pe.wait_ge(ga, e * 48 + 48)
                    for q in range(KT):
                        pe.wait_ge(AX.sem, AX.at(e, f"x{q - 2}") if q >= 2 else AX.at(e - 1, f"x{q + KT - 2}"))
                        if q < 2:
                            pe.wait_ge(VD.sem, VD.at(e - 2, f"d{4 + q}"))
                        for n, (at, m) in enumerate(GROUPS):
                            mm = pe.transpose(px[:, q % 2, at:at + m], xs[0:m, n, P * q:P * q + P],
                                              s["ident"][0:m, 0:m])
                        mm.then_inc(*PX.inc(f"x{q}"))

                def gate_up(e, h, k):
                    for f in range(KT):
                        j, c = f // 2, f % 2
                        if c == 0:
                            pe.wait_ge(gld[j], (k * 2 + h) * 16 + 16)
                            pe.wait_ge(uld[j], (k * 2 + h) * 16 + 16)
                        if f == 0:
                            pe.wait_ge(AX.sem, AX.at(e, f"x{KT - 1}"))
                        for w, p, name, steps in ((wg, pg, "g", AG), (wu, pu, "u", VG)):
                            free = {"g": "g", "u": "m"}[name]
                            pe.wait_ge(steps.sem, steps.at(e, f"{free}{f - 2}") if f >= 2 else
                                       steps.at(e - 1, f"{free}{f + KT - 2}"))
                            for q in range(KT):
                                mm = pe.matmul(p[:, f % 2, 0:SLOTS], w[:, j, q, P * c:P * c + P], xT[:, q, :],
                                               start=(q == 0), stop=(q == KT - 1))
                            mm.then_inc(*PG.inc(f"{name}{f}"))

                def down(e, h, k, more):
                    pe.wait_ge(VW.sem, VW.at(e, f"w{KT - 1}"))
                    pe.wait_ge(VG.sem, VG.at(e, f"h{KT - 1}"))
                    for n in range(6):
                        (at, m), c = GROUPS[n // 2], n % 2
                        if n < 2 and more:
                            pe.wait_ge(AX.sem, AX.at(e + 1, f"x{KT - 2 + n}"))
                        if n >= 2:
                            pe.wait_ge(VD.sem, VD.at(e, f"d{n - 2}"))
                        elif not more:
                            pe.wait_ge(VD.sem, VD.at(e - 1, f"d{4 + n}"))
                        for f in range(KT):
                            high, low = (x[:, f // 2, f % 2, 512 * c:512 * c + 512] for x in (wdh, wdl))
                            first, last = f == 0, f == KT - 1
                            if n < 4:
                                rows = hid[:, f, at:at + m], hid[:, f, CTX_LO + CCAP + at:CTX_LO + CCAP + at + m]
                                mm = product(pe, px[0:m, n % 2, :], rows, (high, low), first, last)
                            else:
                                rows = hid[:, f, CAP:CTX_LO + CCAP]
                                pe.matmul(px[0:3 * CCAP, n % 2, :], rows, high, start=first, stop=False)
                                mm = pe.matmul(px[0:3 * CCAP, n % 2, :], rows, low, start=False, stop=last)
                        mm.then_inc(*PD.inc(f"d{n}"))

                index(0)
                turn(0)
                index(1)
                pe.wait_ge(empty, 1)

                def body(e, h, k, one, two):
                    gate_up(e, h, k)
                    if two:
                        index(e + 2)
                    if one:
                        turn(e + 1)
                    down(e, h, k, one)

                experts(pe, body)

            @block.scalar
            def _(act):
                AG.give(act)
                AX.give(act)

                for steps in (AH, AW, AC):
                    steps.give(act)

                def turned(e):
                    act.wait_ge(PG.sem, PG.at(e - 1, f"u{KT - 1}"))
                    for q in range(KT):
                        act.wait_ge(PX.sem, PX.at(e, f"x{q}"))
                        act.activation(xT[:, q, :], px[:, q % 2, 0:SLOTS], ACT.Copy).then_inc(*AX.inc(f"x{q}"))

                turned(0)

                def body(e, h, k, one, two):
                    for f in range(KT):
                        act.wait_ge(PG.sem, PG.at(e, f"g{f}"))
                        act.wait_ge(VG.sem, VG.at(e, f"m{f - 1}") if f else VG.at(e - 1, f"m{KT - 1}"))
                        act.activation(act_g[:], pg[:, f % 2, 0:SLOTS], ACT.Silu).then_inc(*AG.inc(f"g{f}"))
                        act.wait_ge(VG.sem, VG.at(e, f"m{f}"))
                        if f == 0:
                            act.wait_ge(PD.sem, PD.at(e - 1, "d5"))
                        act.activation(hid[:, f, 0:SLOTS], full[:], ACT.Copy).then_inc(*AH.inc(f"h{f}"))
                        act.wait_ge(rld, e * (16 * KT) + 16 * (f + 1))
                        act.activation(wdh[:, f // 2, f % 2, :], raw[:], ACT.Copy).then_inc(*AW.inc(f"w{f}"))
                    if one:
                        turned(e + 1)
                    for c in range(2):
                        act.wait_ge(PD.sem, PD.at(e, f"d{4 + c}"))
                        act.wait_ge(VD.sem, VD.at(e, "d4") if c else VD.at(e - 1, "d5"))
                        act.activation(clow[:], px[2 * CCAP:3 * CCAP, c, :], ACT.Copy).then_inc(*AC.inc(f"c{c}"))

                experts(act, body)

            @block.vector
            def _(v):
                for steps in (VG, VM, VI, VX, VD, VW, VC):
                    steps.give(v)
                for steps in (R0, RB, R1):
                    steps.give(v)
                v.memset(hid[:, :, SLOTS:CTX_LO].bitcast(F32), 0.0).then_inc(empty, 1)
                v.memset(arr[:], 0.0).then_inc(*R0.inc("zero"))
                v.wait_ge(R0.sem, R0.at(0, "zero"))
                lat = s["aff"][:, 0:NLAT, :].rearrange("p (g b) e -> p b e g", b=2)
                for b in range(2):
                    v.tensor_copy(arr[:, b, :].rearrange("p (e g) -> p e g", g=8), lat[:, b]).then_inc(*R0.inc(f"a{b}"))
                v.tensor_copy(arr[:, 2, 0:P:8], s["aff"][:, NLAT, :]).then_inc(*R0.inc("ac"))
                v.wait_ge(Q1.sem, Q1.at(0, "prob"))
                v.tensor_copy(prob[:].rearrange("p a b -> p (a b)"), px[:, 0, 0:3 * P]).then_inc(*R0.inc("prob"))
                v.memset(thr[:], 0).then_inc(*R0.inc("thr"))
                v.memset(bit[:], 1 << (BITS - 1)).then_inc(*R0.inc("bit"))
                v.wait_ge(R0.sem, R0.at(0, "bit"))
                v.wait_ge(ldc, 80)
                parts = lambda a, n: a[:, 0:2, :] if n == 0 else a[:, 2, :]
                with v.Fori(0, BITS, 1) as i:
                    v.wait_ge(RB.sem, RB.at(i - 1, "thr"))
                    v.tensor_tensor(cand[:], thr[:], bit[:], ALU.bitwise_or).then_inc(*RB.inc("cand"))
                    v.wait_ge(RB.sem, RB.at(i, "cand"))
                    for n, name in enumerate(("cl", "cc")):
                        v.tensor_scalar(parts(over, n), parts(prob, n), cand[:, n:n + 1].bitcast(F32), 0.0, ALU.is_ge,
                                        ALU.add, accum_out=cnt[:, n:n + 1]).then_inc(*RB.inc(name))
                    v.wait_ge(QB.sem, QB.at(i, "sum"))
                    v.tensor_tensor(met[:], pi[:, 0:2], caps[:], ALU.is_ge).then_inc(*RB.inc("met"))
                    v.wait_ge(RB.sem, RB.at(i, "met"))
                    v.tensor_single_scalar(bit[:], bit[:], 1, ALU.logical_shift_right).then_inc(*RB.inc("bit"))
                    v.copy_predicated(thr[:], met[:], cand[:]).then_inc(*RB.inc("thr"))
                v.wait_ge(RB.sem, RB.at(BITS - 1, "thr"))
                t = lambda n: thr[:, n:n + 1].bitcast(F32)
                done = lambda name: v.wait_ge(R1.sem, R1.at(0, name))
                for n, name in enumerate(("gl", "gc")):
                    v.tensor_scalar(parts(over, n), parts(prob, n), t(n), 0.0, ALU.is_gt, ALU.add,
                                    accum_out=cnt[:, n:n + 1]).then_inc(*R1.inc(name))
                v.wait_ge(Q1.sem, Q1.at(0, "above"))
                v.tensor_tensor(need[:], caps[:], pi[:, 0:2], ALU.subtract).then_inc(*R1.inc("need"))
                for n, name in enumerate(("tl", "tc")):
                    v.tensor_scalar(parts(tie, n), parts(prob, n), t(n), None, ALU.is_equal).then_inc(*R1.inc(name))
                flat = lambda a, n: a[:].rearrange("p a b -> p (a b)")[:, 0:256] if n == 0 else a[:, 2, :]

                def running(src, a, b):
                    for n in range(2):
                        v.tensor_tensor_scan(flat(scan, n), flat(src, n), flat(src, n), 0.0, ALU.add, ALU.bypass)\
                         .then_inc(*R1.inc(f"{a}{n}"))
                    done(f"{a}1")
                    for n in range(2):
                        v.tensor_copy(ends[:, n:n + 1], scan[:, 1 + n, P - 1:P]).then_inc(*R1.inc(f"{b}{n}"))

                done("tc")
                running(tie, "s", "e")
                v.wait_ge(Q1.sem, Q1.at(0, "ahead"))
                v.tensor_tensor(need[:], need[:], pi[:, 0:2], ALU.subtract).then_inc(*R1.inc("lim"))
                done("lim")
                for n in range(2):
                    v.scalar_tensor_tensor(flat(tie, n), flat(scan, n), need[:, n:n + 1], flat(tie, n), ALU.is_le,
                                           ALU.mult).then_inc(*R1.inc(f"k{n}"))
                done("k1")
                v.tensor_tensor(tie[:], tie[:], over[:], ALU.add).then_inc(*R1.inc("sel"))
                done("sel")
                running(tie, "p", "f")
                v.wait_ge(Q1.sem, Q1.at(0, "slots"))
                v.tensor_copy(need[:], pi[:, 0:2]).then_inc(*R1.inc("off"))
                done("off")
                for n in range(2):
                    v.tensor_scalar(flat(scan, n), flat(scan, n), need[:, n:n + 1], None, ALU.add)\
                     .then_inc(*R1.inc(f"q{n}"))
                v.wait_ge(Q1.sem, Q1.at(0, "pos"))
                v.tensor_copy(pos[:].rearrange("p a b -> p (a b)"), px[:, 1, 0:3 * P]).then_inc(*R1.inc("pos"))
                v.memset(ones[:], 1.0).then_inc(*R1.inc("ones"))
                done("ones")

                def passed(e, n):
                    g, b = n // 2, n % 2
                    v.tensor_scalar(below[:, n, :], slot[:], pos[:, b, take(e * 8 + g, 1)], None, ALU.is_ge)\
                     .then_inc(*VM.inc(f"m{n}"))

                def passed_context(e):
                    v.tensor_scalar(below_c[:], slot[:, 0:CCAP], pos[:, 2, take(e * 8, 1)], None, ALU.is_ge)\
                     .then_inc(*VM.inc("mc"))

                def numbers(e, h, k):
                    v.wait_ge(PI.sem, PI.at(e, "ids"))
                    if not (isinstance(k, int) and k == 0):
                        v.wait_ge(ga, e * 48 - 48)
                    v.tensor_copy(ids[:, h, 0:2], pi[:, 0:2]).then_inc(*VI.inc("i0"))
                    v.tensor_scalar(ids[0:CCAP, h, 2:3], pi[0:CCAP, 2:3], float(LAT), None, ALU.add)\
                     .then_inc(*VI.inc("i2"))

                for e in range(2):
                    v.wait_ge(PI.sem, PI.at(e - 1, "ids"))
                    for n in range(NLAT):
                        passed(e, n)
                    passed_context(e)
                    numbers(e, e, 0)

                def body(e, h, k, one, two):
                    v.wait_ge(ga, e * 48 + 48)
                    v.wait_ge(CP.sem, CP.at(e - 2, "added"))
                    v.wait_ge(VI.sem, VI.at(e, "i2"))
                    v.tensor_copy(sids[:, h, 0:2], ids[:, h, 0:2]).then_inc(*VX.inc("s0"))
                    v.tensor_copy(sids[0:CCAP, h, 2:3], ids[0:CCAP, h, 2:3]).then_inc(*VX.inc("s2"))
                    v.tensor_copy(vals[:, h, 0:2], xs[:, 0:2, take(e + DM, 1)].rearrange("p a b -> p (a b)"))\
                     .then_inc(*VX.inc("v0"))
                    v.tensor_copy(vals[0:CCAP, h, 2:3], xs[0:CCAP, 2, take(e + DM, 1)]).then_inc(*VX.inc("v2"))
                    for f in range(KT):
                        v.wait_ge(AG.sem, AG.at(e, f"g{f}"))
                        v.wait_ge(PG.sem, PG.at(e, f"u{f}"))
                        if f == 0:
                            v.wait_ge(PD.sem, PD.at(e - 1, "d5"))
                        v.wait_ge(VG.sem, VG.at(e, f"h{f - 1}") if f else VG.at(e - 1, f"h{KT - 1}"))
                        v.tensor_tensor(full[:], pu[:, f % 2, 0:SLOTS], act_g[:], ALU.mult)\
                         .then_inc(*VG.inc(f"m{f}"))
                        v.wait_ge(VG.sem, VG.at(e, f"m{f}"))
                        v.wait_ge(AH.sem, AH.at(e, f"h{f}"))
                        for name, (at, n), to in (("l", (0, CAP), CTX_LO + CCAP), ("h", (CAP, CCAP), CTX_LO)):
                            v.tensor_tensor(hid[:, f, to:to + n], full[:, at:at + n],
                                            hid[:, f, at:at + n].bitcast(F32), ALU.subtract).then_inc(*VG.inc(f"{name}{f}"))
                        v.wait_ge(AW.sem, AW.at(e, f"w{f}"))
                        v.tensor_tensor(wdl[:, f // 2, f % 2, :], raw[:], wdh[:, f // 2, f % 2, :].bitcast(F32),
                                        ALU.subtract).then_inc(*VW.inc(f"w{f}"))
                        if two:
                            if f == 0:
                                v.wait_ge(PI.sem, PI.at(e + 1, "ids"))
                            passed(e + 2, 2 * f)
                            passed(e + 2, 2 * f + 1)
                    if two:
                        passed_context(e + 2)
                        numbers(e + 2, h, k + 1)
                    v.wait_ge(CP.sem, CP.at(e - 1, "added"))
                    v.wait_ge(VX.sem, VX.at(e, "v2"))
                    for n in range(6):
                        g, c = n // 2, n % 2
                        m = GROUPS[g][1]
                        v.wait_ge(PD.sem, PD.at(e, f"d{n}"))
                        rows = px[0:m, c, :]
                        if g == 2:
                            v.wait_ge(AC.sem, AC.at(e, f"c{c}"))
                            v.tensor_tensor(clow[:], px[0:m, c, :], clow[:], ALU.add).then_inc(*VC.inc(f"sum{c}"))
                            v.wait_ge(VC.sem, VC.at(e, f"sum{c}"))
                            rows = clow[:]
                        v.scalar_tensor_tensor(ye[0:m, g, 512 * c:512 * c + 512], rows, vals[0:m, h, g:g + 1],
                                               gate2[0:m, g // 2, 512 * c:512 * c + 512], ALU.mult, ALU.mult)\
                         .then_inc(*VD.inc(f"d{n}"))

                experts(v, body)

            @block.gpsimd
            def _(g):
                g.memset(spare[:], 0.0).then_inc(pc, 1)
                g.wait_ge(pc, 1)

                CG.give(g)
                CP.give(g)

                def carry(steps, name, column):
                    g.tensor_tensor(spare[:, column:column + 1], spare[:, 0:1], spare[:, 0:1], ALU.add)\
                     .then_inc(*steps.inc(name))

                def gather(e, h):
                    g.wait_ge(VI.sem, VI.at(e, "i2"))
                    g.wait_ge(PX.sem, PX.at(e - 1, f"x{KT - 1}"))
                    g.wait_ge(VX.sem, VX.at(e - 1, "v2"))
                    g.wait_ge(CG.sem, CG.at(e - 1, "carry"))
                    carry(CG, "carry", 1)
                    for n, (at, m) in enumerate(GROUPS):
                        g.indirect_dma_start(xs[0:m, n, :], None, d["h2"],
                                             bass.IndirectOffsetOnAxis(ap=ids[0:m, h, n:n + 1], axis=0)).then_inc(ga, 16)

                gather(0, 0)

                def body(e, h, k, one, two):
                    if one:
                        gather(e + 1, 1 - h)
                    g.wait_ge(VD.sem, VD.at(e, "d5"))
                    g.wait_ge(CP.sem, CP.at(e - 1, "added"))
                    carry(CP, "before", 2)
                    for n, (at, m) in enumerate(GROUPS):
                        g.indirect_dma_start(d["xacc"], bass.IndirectOffsetOnAxis(ap=sids[0:m, h, n:n + 1], axis=0),
                                             ye[0:m, n, :], None, compute_op=ALU.add).then_inc(sc[h], 16)
                    g.wait_ge(sc[h], 48 * (k + 1))
                    carry(CP, "added", 3)

                experts(g, body)
                for h in range(2):
                    g.wait_ge(sc[h], 48 * NE // 2)


def phase_final(nc, d, s):
    SL = 4
    with ExitStack() as ctx:
        sb, pb, sem, counted = makers(nc, ctx, s, "final")
        x = sb("xf", [P, SL, DM])
        y = sb("yf", [P, SL, DM])
        junk = sb("junkf", [P, DM])
        gf = sb("gf", [P, DM])
        rstd = sb("rstdf", [P, SL])
        eps = sb("epsf", [P, 1])
        ldc, cv = sem("ld_cf"), sem("consts_f")
        ld = [sem(f"ld_f{m}") for m in range(SL)]
        st = [sem(f"st_f{m}") for m in range(SL)]
        AS = counted("act_final", ["sq", "std"])
        VS = counted("dve_final", ["rstd", "y"])

        def in_loop(eng, body):
            with eng.Fori(0, NLAT // SL, 1) as i:
                for m in range(SL):
                    body(i * SL + m, m, i)
            body(NLAT, 0, NLAT // SL)

        with nc.Block() as block:
            @block.sync
            def _(sp):
                had(sp, st)
                def load(t, m):
                    sp.dma_start(x[:, m], d["xacc"][take(t * P, P), :]).then_inc(ld[m], 16)

                def store(t, m):
                    at = t * P if isinstance(t, int) else sp.snap(t * P)
                    sp.wait_ge(VS.sem, VS.at(t, "y"))
                    sp.dma_start(d["y_sample"][take(at, P), :], y[:, m]).then_inc(st[m], 16)

                sp.dma_start(gf[:], d["norm_f_g"].partition_broadcast(P)).then_inc(ldc, 16)
                for m in range(SL):
                    load(m, m)
                with sp.Fori(0, NLAT // SL - 1, 1) as i:
                    for m in range(SL):
                        store(i * SL + m, m)
                        load(i * SL + (m + SL), m)
                for t in range(NLAT - SL, NLAT):
                    store(t, t % SL)
                    if t == NLAT - SL:
                        load(NLAT, 0)
                sp.wait_ge(VS.sem, VS.at(NLAT, "y"))
                sp.dma_start(d["y_prompt"], y[:, 0]).then_inc(st[0], 16)
                for m in range(SL):
                    sp.wait_ge(st[m], 16 * (NLAT // SL + (m == 0)) + HAD)
                retire(sp, s)

            @block.scalar
            def _(act):
                AS.give(act)
                act.wait_ge(cv, 1)

                def body(t, m, k):
                    act.wait_ge(ld[m], 16 * (k + 1))
                    act.wait_ge(VS.sem, VS.at(t - SL // 2, "y") if False else VS.at(t - 2, "y"))
                    act.activation(junk[:], x[:, m], ACT.Square, scale=DM ** -0.5, accum_out=rstd[:, m:m + 1])\
                       .then_inc(*AS.inc("sq"))
                    act.wait_ge(AS.sem, AS.at(t, "sq"))
                    act.activation(rstd[:, m:m + 1], rstd[:, m:m + 1], ACT.Sqrt, bias=eps[:]).then_inc(*AS.inc("std"))

                in_loop(act, body)

            @block.vector
            def _(v):
                VS.give(v)
                v.memset(eps[:], EPS).then_inc(cv, 1)
                v.wait_ge(ldc, 16)

                def body(t, m, k):
                    v.wait_ge(AS.sem, AS.at(t, "std"))
                    v.reciprocal(rstd[:, m:m + 1], rstd[:, m:m + 1]).then_inc(*VS.inc("rstd"))
                    v.wait_ge(st[m], 16 * k + HAD)
                    v.wait_ge(VS.sem, VS.at(t, "rstd"))
                    v.scalar_tensor_tensor(y[:, m], x[:, m], rstd[:, m:m + 1], gf[:], ALU.mult, ALU.mult)\
                     .then_inc(*VS.inc("y"))

                in_loop(v, body)


PHASES = [phase_filters, phase_tokens, phase_hyena_in, phase_spectrum, phase_hyena_out, phase_retention,
          phase_merge, phase_out, phase_experts, phase_final]

SCRATCH = {
    "mod": (2, 6 * DM), "kspec": (P, N2, DH), "cspec": (2, P, DH),
    "hT": (P, KT, TOK), "state": (NLAT, P, 512), "v": (NT, P, 512), "gs": (NT, P, 512), "qkT": (NT, P, 1024),
    "kvb": (NLAT, P, 512), "x2": (CB, P, TOK + 2), "uspec": (P, N2, DH), "uctx": (P, DH), "qspec": (P, N2, DH),
    "yhy": (P, CB, TOK), "yret": (P, CB, TOK), "merged": (P, KT, TOK), "xacc": (TOK, DM), "h2": (TOK, ROW),
}
OUTPUTS = {"y_prompt": (CTX, DM), "y_sample": (LAT, DM), "new_f": (HEADS, HD, HD), "new_b": (HEADS, HD, HD)}


def build(nc, d):
    with ExitStack() as ctx:
        s = persistent(nc, ctx)
        for phase in PHASES:
            s["own"], s["stack"] = [], ExitStack()
            phase(nc, d, s)
            s["last_stack"].close()
            s["last"], s["last_stack"] = s["own"], s["stack"]
        s["last_stack"].close()


def kernel(**inputs):
    import concourse.bacc as bacc
    from concourse.bass_utils import run_bass_kernel_spmd

    arrays = {**layout({k: np.asarray(v) for k, v in inputs.items()}), **constants()}
    nc = bacc.Bacc("TRN2", target_bir_lowering=False, num_devices=1)
    d = {k: nc.dram_tensor(f"in_{k}", a.shape, F32, kind="ExternalInput").ap() for k, a in arrays.items()}
    for k, shape in SCRATCH.items():
        d[k] = nc.dram_tensor(f"scratch_{k}", shape, F32, kind="Internal").ap()
    for k, shape in OUTPUTS.items():
        d[k] = nc.dram_tensor(f"out_{k}", shape, F32, kind="ExternalOutput").ap()
    build(nc, d)
    r = run_bass_kernel_spmd(nc, [{f"in_{k}": a for k, a in arrays.items()}], core_ids=[0]).results[0]
    state = (1, 1, HEADS, HD, HD)
    return (r["out_y_prompt"].reshape(1, CTX, DM), r["out_y_sample"].reshape(1, LAT, DM),
            r["out_new_f"].reshape(state), r["out_new_b"].reshape(state))
```

```python
import numpy as np
import concourse.bass as bass
from concourse import mybir
from contextlib import ExitStack

F32 = mybir.dt.float32
I32 = mybir.dt.int32
BF16 = mybir.dt.bfloat16
F32R = mybir.dt.float32r
ALU = mybir.AluOpType
ACT = mybir.ActivationFunctionType
AX = mybir.AxisListType

P = 128
DM = 1024
KT = DM // P
LAT, CTX = 2048, 128
NLAT = LAT // P
NT = NLAT + 1
TOK = LAT + CTX
DH = 512
CB = DH // P
HEADS, HD = 4, 128
NE, CAP, CCAP = 16, 2 * LAT // 16, 2 * CTX // 16
FH = 64
N2, K1 = 32, 64
PAIRS = K1 // 2
EPS = 1e-6
GRID_W = 64


class Steps:

    def __init__(self, sem, steps):
        self.sem = sem
        self.steps, self.k, self.next = list(steps), len(steps), 0
        assert len(set(self.steps)) == self.k

    def give(self, eng):
        eng.sem_inc(self.sem, 2 * self.k)

    def at(self, rnd, step):
        return (rnd + 2) * self.k + self.steps.index(step) + 1

    def inc(self, step):
        assert self.steps[self.next % self.k] == step, (self.steps[self.next % self.k], step)
        self.next += 1
        return self.sem, 1


def in_turn(eng, rounds, looped, front, back):
    front(0, 0)
    with eng.Fori(0, looped // 2, 1) as i:
        for h in range(2):
            front(i * 2 + (h + 1), 1 - h)
            back(i * 2 + h, h)
    for t in range(looped, rounds):
        if t + 1 < rounds:
            front(t + 1, (t + 1) % 2)
        back(t, t % 2)


def product(pe, out, lhs, rhs, start, stop):
    pe.matmul(out, lhs[0], rhs[0], start=start, stop=False)
    pe.matmul(out, lhs[0], rhs[1], start=False, stop=False)
    return pe.matmul(out, lhs[1], rhs[0], start=False, stop=stop)


def makers(nc, ctx, s, phase):
    sb = lambda n, sh, dt=F32: ctx.enter_context(nc.sbuf_tensor(f"{phase}_{n}", sh, dt))
    pb = lambda n, sh: ctx.enter_context(nc.psum_tensor(f"{phase}_{n}", sh, F32))

    def sem(n):
        s["own"].append(s["stack"].enter_context(nc.semaphore(f"{phase}_{n}")))
        return s["own"][-1]

    return sb, pb, sem, lambda n, steps: Steps(sem(n), steps)


HAD = 16


def had(sp, *sems):
    for each in sems:
        for sem in each if isinstance(each, list) else [each]:
            sp.sem_inc(sem, HAD)


def retire(sp, s):
    for sem in s["last"]:
        sp.sem_clear(sem)


def take(v, k):
    return bass.ds(v, k)


def constants():
    f8 = np.float64
    c = {}
    c["ident"] = np.eye(P)

    def position_features(pos, L):
        t = pos / (L - 1)
        ang = (2 * np.pi * pos / L)[:, None] * np.linspace(1e-4, 15, 16)[None, :]
        return np.concatenate([t[:, None], np.cos(ang), -np.sin(ang)], axis=1).T, t

    n2, j = np.meshgrid(np.arange(N2), np.arange(K1), indexing="ij")
    ahead, behind = (32 * j + n2).ravel().astype(f8), (LAT - 32 * j - n2).ravel().astype(f8)
    zf, tf = position_features(ahead, LAT)
    zb, tb = position_features(behind, LAT)
    cf, ctf = position_features(np.arange(CTX, dtype=f8), CTX)
    cb, ctb = position_features(CTX - np.arange(CTX, dtype=f8), CTX)
    c["z"] = np.concatenate([np.concatenate([zf, cf], 1), np.concatenate([zb, cb], 1)], 0)
    negt = np.zeros((P, N2 + 2))
    negt[:64, :N2] = -tf.reshape(N2, K1).T
    negt[64:, :N2] = -tb.reshape(N2, K1).T
    negt[:, N2], negt[:, N2 + 1] = -ctf, -ctb
    c["negt"] = negt
    n1, k1 = np.arange(P)[:, None], np.arange(K1)[None, :]
    ph = -2 * np.pi * n1 * (k1 + 0.5) / P
    f1 = np.stack([np.cos(ph), np.sin(ph)], axis=2).reshape(P, P)
    f1[64:] *= -1.0
    c["f1"] = f1
    up = np.zeros((P, 2, P))
    up[:64, 0], up[64:, 1] = f1[:64], f1[:64]
    c["f1u"] = up.reshape(P, 2 * P)
    n2, k2 = np.arange(N2), np.arange(N2)
    tg = np.zeros((PAIRS, P, 448))
    for p in range(PAIRS):
        for b in range(2):
            kk = 2 * p + b
            ph = -2 * np.pi * (n2[:, None] * (kk + 0.5) / 4096 + n2[:, None] * k2[None, :] / N2)
            cs, sn = np.cos(ph), np.sin(ph)
            re = np.concatenate([cs, -sn], 0)
            im = np.concatenate([sn, cs], 0)
            rows = slice(64 * b, 64 * b + 64)
            for s, m in ((0, -im), (64, re), (128, re), (192, im), (256, im)):
                tg[p, rows, s + 32 * b:s + 32 * b + 32] = m
            ics, isn = cs.T, -sn.T
            tg[p, 32 * b:32 * b + 32, 320 + 64 * b:320 + 64 * b + 64] = np.concatenate([ics, isn], 1)
            tg[p, 64 + 32 * b:96 + 32 * b, 320 + 64 * b:320 + 64 * b + 64] = np.concatenate([-isn, ics], 1)
    c["tg"] = tg
    n1, k1 = np.arange(K1)[None, :], np.arange(K1)[:, None]
    ph = 2 * np.pi * n1 * (k1 + 0.5) / P
    c["f2"] = (np.stack([np.cos(ph), -np.sin(ph)], axis=1) * (2.0 / 4096)).reshape(P, K1)
    n, k = np.arange(256)[:, None], np.arange(P)[None, :]
    ph = -2 * np.pi * n * (k + 0.5) / 256
    cc = np.concatenate([np.cos(ph), np.sin(ph)], 1)
    cc[128:] *= -1.0
    c["cf"] = np.concatenate([cc[:128], cc[128:]], 1)
    ph = 2 * np.pi * np.arange(P)[None, :] * (np.arange(P)[:, None] + 0.5) / 256
    c["ci"] = np.concatenate([np.cos(ph), -np.sin(ph)], 1) * (2.0 / 256)
    inv = 10000.0 ** (-np.arange(32) / 32.0)
    pos = np.arange(LAT)
    ar, ac = (pos // GRID_W)[:, None] * inv, (pos % GRID_W)[:, None] * inv
    cos = np.concatenate([np.cos(ar), np.cos(ar), np.cos(ac), np.cos(ac)], 1)
    sin = np.concatenate([-np.sin(ar), np.sin(ar), -np.sin(ac), np.sin(ac)], 1)
    cos = np.concatenate([cos, np.ones((CTX, P))])
    sin = np.concatenate([sin, np.zeros((CTX, P))])
    c["rope"] = np.concatenate([cos, sin, cos * HD ** -0.5, sin * HD ** -0.5], 1).reshape(NT, P, 512)
    j, i = np.arange(P)[:, None], np.arange(P)[None, :]
    c["dist"] = np.concatenate([np.maximum(i - j, 0), np.maximum(j - i, 0),
                                np.broadcast_to(i + 1, (P, P)), np.broadcast_to(P - i, (P, P))], 1)
    c["expo"] = np.concatenate([P - 1 - j, j], 1)
    q = np.arange(P)
    c["seg"] = np.concatenate([(q[:, None] // 8 == q[None, :] // 8), (q[:, None] // 8 == q[None, :] // 8) &
                               (q[:, None] < q[None, :])], 1)
    c["caps"] = np.broadcast_to(np.array([CAP, CCAP]), (P, 2))
    c["slot"] = np.broadcast_to(np.arange(CAP), (P, CAP))
    return {k: np.ascontiguousarray(v, dtype=np.float32) for k, v in c.items()}


TWO_PI_A, TWO_PI_B = 6.28125, 1.93500518798828125e-3
TWO_PI_C = 2 * np.pi - TWO_PI_A - TWO_PI_B
ROUND = 1.5 * 2.0 ** 23


def phase_filters(nc, d, s):
    CH = 12
    with ExitStack() as ctx:
        sb, pb, sem, counted = makers(nc, ctx, s, "filters")
        wm = sb("wm", [P, 2, KT, 512])
        cond = sb("cond", [P, KT, 2])
        scond = sb("scond", [P, KT, 2])
        bmod = sb("bmod", [2, 6 * DM])
        g1n = sb("g1n", [P, KT])
        mrow = sb("mrow", [2, 6 * DM])
        zt = sb("zt", [66, TOK])
        w1 = sb("w1", [66, P])
        w2 = sb("w2", [P, P])
        fcol = sb("fcol", [P, 3])
        fb = sb("fb", [P, 2])
        w3 = sb("w3", [P, DH])
        dec = sb("dec", [P, 3, DH])
        negt = sb("negt", [P, N2 + 2])
        bias0 = sb("bias0", [1, DH])
        f1 = sb("f1", [P, P])
        cf = sb("cf", [P, 512])
        arg = sb("arg", [P, TOK])
        rnd = sb("rnd", [P, TOK])
        hid1 = sb("hid1", [P, TOK])
        hid2 = sb("hid2", [P, N2 + 2, P])
        hs = sb("hs", [P, 2, P])
        env = sb("env", [P, 2, DH])
        taps = sb("taps", [P, 2, DH])
        spec = sb("spec", [P, 2, DH])
        pa = pb("pa", [P, 5, 512])
        pm = pb("pm", [P, 2, 512])
        pmt = pb("pmt", [P, P])

        ld, lc = sem("ld_filter"), sem("ld_cond")
        wld = [sem("wmod0"), sem("wmod1")]
        silu, bar, modpe, modcol, modt, modr = (sem(x) for x in
                                                ("silu_c", "clear", "mod_pe", "mod_col", "mod_t", "mod_r"))
        sin_pe, sin_act, sin_dve = sem("sin_pe"), sem("sin_act"), sem("sin_dve")
        wfree = sem("wmod_used")
        ast = counted("act_taps", ["hid", "env"])
        pst = counted("pe_taps", ["taps", "spec"])
        vst = counted("dve_taps", ["taps", "spec"])
        sst = [sem("spec_out0"), sem("spec_out1")]
        outs = sem("mod_out")
        cspec = sem("ctx_spec")

        AHEAD = 4

        def groups(eng, taps, chunk):
            taps(0)
            with eng.Fori(0, (CH - AHEAD) // 2, 1) as i:
                for h in range(2):
                    taps(i * 2 + (h + 1))
                    chunk(i * 2 + (AHEAD + h), h)
            with eng.Fori(CH - AHEAD + 1, N2 // 2, 1) as i:
                taps(i)

        with nc.Block() as block:
            @block.sync
            def _(sp):
                had(sp, modcol, sst)
                sp.dma_start(cond[:], d["cond"]).then_inc(lc, 16)
                sp.dma_start(bmod[:], d["b_mod"].partition_broadcast(2)).then_inc(lc, 16)
                sp.dma_start(g1n[:], d["norm1_g"]).then_inc(lc, 16)
                sp.dma_start(s["ident"][:], d["ident"]).then_inc(lc, 16)
                for dst, src in ((zt, "z"), (w1, "f_w1"), (w2, "f_w2"), (fcol, "f_col"), (w3, "f_w3"),
                                 (negt, "negt"), (f1, "f1"), (cf, "cf")):
                    if src in ("f_w1", "f_w2"):
                        continue
                    sp.dma_start(dst[:], d[src]).then_inc(ld, 16)
                sp.dma_start(bias0[:], d["hy_bias"]).then_inc(ld, 16)
                sp.wait_ge(bar, 3)
                for h, (r1, r2) in enumerate(((0, 0), (33, 64))):
                    sp.dma_start(w1[r1:r1 + 33, 64 * h:64 * h + 64], d["f_w1"]).then_inc(ld, 16)
                    sp.dma_start(w2[r2:r2 + 64, 64 * h:64 * h + 64], d["f_w2"]).then_inc(ld, 16)
                for n, (lo, hi) in enumerate(((0, 64), (0, 128), (0, 128))):
                    if n == 0:
                        for h in range(2):
                            sp.dma_start(dec[64 * h:64 * h + 64, 0, :],
                                         d["decay"][h:h + 1, :].partition_broadcast(64)).then_inc(ld, 16)
                    else:
                        sp.dma_start(dec[:, n, :], d["decay"][n - 1:n, :].partition_broadcast(P)).then_inc(ld, 16)
                for h in range(2):
                    sp.dma_start(wm[:, h], d["w_mod"][h:h + 1]).then_inc(wld[h], 16)
                def chunk(t, h):
                    sp.wait_ge(wfree, t + -1)
                    sp.dma_start(wm[:, h], d["w_mod"][take(t, 1)]).then_inc(wld[h], 16)

                def store(i):
                    for h in range(2):
                        t = i * 2 + h
                        sp.wait_ge(vst.sem, vst.at(t, "spec"))
                        sp.dma_start(d["kspec"][:, take(t, 1), :], spec[:, h, :]).then_inc(sst[h], 16)

                for t in range(2, AHEAD + 2):
                    chunk(t, t % 2)
                store(0)
                with sp.Fori(0, (CH - AHEAD) // 2 - 1, 1) as i:
                    for h in range(2):
                        store(i * 2 + (h + 1))
                        chunk(i * 2 + (AHEAD + 2 + h), h)
                with sp.Fori(CH - AHEAD - 1, N2 // 2, 1) as i:
                    store(i)
                sp.wait_ge(cspec, 2)
                sp.dma_start(d["cspec"].rearrange("a p c -> p a c"), spec[:]).then_inc(outs, 16)
                sp.wait_ge(modcol, CH + HAD)
                sp.dma_start(d["mod"], mrow[:]).then_inc(outs, 16)
                sp.wait_ge(outs, 32)
                retire(sp, s)

            @block.tensor
            def _(pe):
                pst.give(pe)
                pe.wait_ge(ld, 16 * 15)
                for b in range(5):
                    n = min(512, TOK - 512 * b)
                    mm = pe.matmul(pa[:, b, 0:n], w1[:], zt[:, 512 * b:512 * b + n], start=True, stop=True)
                mm.then_inc(sin_pe, 1)

                def mod(t, h, after=True):
                    pe.wait_ge(wld[h], (t // 2) * 16 + 16 if isinstance(t, int) else (t - h) * 8 + 16)
                    if after:
                        pe.wait_ge(modcol, t + (HAD - 1))
                    for k in range(KT):
                        mm = pe.matmul(pm[0:2, h, :], scond[:, k, :], wm[:, h, k, :],
                                       start=(k == 0), stop=(k == KT - 1))
                    mm.then_inc(wfree, 1)

                pe.wait_ge(silu, 1)
                for t in range(2):
                    mod(t, t % 2, False)
                pe.wait_ge(sin_act, 2)
                for b in range(5):
                    n = min(512, TOK - 512 * b)
                    mm = pe.matmul(pa[:, b, 0:n], w2[:], hid1[:, 512 * b:512 * b + n], start=True, stop=True)
                mm.then_inc(sin_pe, 1)

                def taps_mm(t, h):
                    pe.wait_ge(ast.sem, ast.at(t, "hid"))
                    pe.wait_ge(vst.sem, vst.at(t - 2, "taps"))
                    pe.matmul(pa[:, h, :], hs[:, h, :], w3[:], start=True, stop=True).then_inc(*pst.inc("taps"))

                def spec_mm(t, h):
                    pe.wait_ge(vst.sem, vst.at(t, "taps"))
                    pe.wait_ge(vst.sem, vst.at(t - 2, "spec"))
                    pe.matmul(pa[:, 2 + h, :], f1[:], taps[:, h, :], start=True, stop=True)\
                      .then_inc(*pst.inc("spec"))

                def pair(i):
                    for h in range(2):
                        taps_mm(i * 2 + h, h)
                        spec_mm(i * 2 + h, h)

                for t in range(2, AHEAD):
                    mod(t, t % 2)
                groups(pe, pair, mod)
                for h in range(2):
                    pe.wait_ge(ast.sem, ast.at(N2 + h, "hid"))
                    pe.wait_ge(vst.sem, vst.at(N2 + h - 2, "taps"))
                    pe.matmul(pa[:, h, :], hs[:, h, :], w3[:], start=True, stop=True).then_inc(*pst.inc("taps"))
                    pe.wait_ge(vst.sem, vst.at(N2 + h - 2, "spec"))
                    pe.wait_ge(vst.sem, vst.at(N2 + h, "taps"))
                    for r in range(2):
                        mm = pe.matmul(pa[:, 2 + r, :], cf[:, 256 * h + P * r:256 * h + P * r + P], taps[:, h, :],
                                       start=(h == 0), stop=(h == 1))
                    mm.then_inc(*pst.inc("spec"))
                pe.wait_ge(modcol, CH + HAD)
                for m in range(2 * KT):
                    mm = pe.transpose(pmt[:, 2 * m:2 * m + 2], mrow[:, P * m:P * m + P], s["ident"][0:2, 0:2])
                mm.then_inc(modt, 1)

            @block.scalar
            def _(act):
                ast.give(act)
                act.wait_ge(lc, 64)
                act.activation(scond[:], cond[:], ACT.Silu).then_inc(silu, 1)
                act.wait_ge(bar, 4)
                for layer in range(2):
                    act.wait_ge(sin_pe, layer + 1)
                    act.activation(arg[:], pa[:].rearrange("p a b -> p (a b)")[:, 0:TOK], ACT.Identity,
                                   bias=fb[:, layer:layer + 1], scale=fcol[:, 1:2]).then_inc(sin_act, 1)
                    act.wait_ge(sin_dve, 5 * (layer + 1))
                    if layer == 0:
                        act.activation(hid1[:], arg[:], ACT.Sin).then_inc(sin_act, 1)
                    else:
                        for h in range(2):
                            a = arg[64 * h:64 * h + 64, 0:LAT].rearrange("p (a b) -> p a b", b=K1)
                            act.activation(hid2[64 * h:64 * h + 64, 0:N2, 64 * h:64 * h + 64], a, ACT.Sin)\
                               .then_inc(sin_act, 1)
                            act.activation(hid2[64 * h:64 * h + 64, N2 + h, :],
                                           arg[64 * h:64 * h + 64, LAT:TOK], ACT.Sin).then_inc(sin_act, 1)
                act.wait_ge(bar, 9)

                def group(t, h, direction):
                    act.wait_ge(pst.sem, pst.at(t - 2, "taps"))
                    act.activation(hs[:, h, :], hid2[:, take(t, 1), :], ACT.Copy).then_inc(*ast.inc("hid"))
                    act.wait_ge(vst.sem, vst.at(t - 2, "taps"))
                    act.activation(env[:, h, :], dec[:, direction, :], ACT.Exp, scale=negt[:, take(t, 1)])\
                       .then_inc(*ast.inc("env"))

                with act.Fori(0, N2 // 2, 1) as i:
                    for h in range(2):
                        group(i * 2 + h, h, 0)
                for h in range(2):
                    group(N2 + h, h, 1 + h)

            @block.vector
            def _(v):
                vst.give(v)
                v.memset(w1[:], 0.0).then_inc(bar, 1)
                v.memset(w2[:], 0.0).then_inc(bar, 1)
                v.memset(hid2[:], 0.0).then_inc(bar, 1)
                v.wait_ge(ld, 16 * 15)
                v.tensor_tensor(fb[:], fcol[:, 0:3:2], fcol[:, 1:2].broadcast_to([P, 2]), ALU.mult).then_inc(bar, 1)
                def columns(t, h):
                    v.wait_ge(wfree, t + 1)
                    v.tensor_tensor(mrow[:, take(t * 512, 512)], pm[0:2, h, :], bmod[:, take(t * 512, 512)], ALU.add)\
                     .then_inc(modcol, 1)

                n = 0
                for layer in range(2):
                    v.wait_ge(sin_act, 2 * layer + 1)
                    v.tensor_scalar(rnd[:], arg[:], float(1 / (2 * np.pi)), ROUND, ALU.mult, ALU.add)\
                     .then_inc(sin_dve, 1)
                    v.wait_ge(sin_dve, n + 1)
                    v.tensor_scalar(rnd[:], rnd[:], -ROUND, None, ALU.add).then_inc(sin_dve, 1)
                    for m, part in enumerate((TWO_PI_A, TWO_PI_B, TWO_PI_C)):
                        v.wait_ge(sin_dve, n + 2 + m)
                        if m < 2:
                            v.scalar_tensor_tensor(arg[:], rnd[:], -part, arg[:], ALU.mult, ALU.add)\
                             .then_inc(sin_dve, 1)
                        else:
                            v.scalar_tensor_tensor(rnd[:], rnd[:], -part, arg[:], ALU.mult, ALU.add)\
                             .then_inc(bar, 1)
                            v.wait_ge(bar, 5 + layer)
                            v.tensor_scalar(arg[:], rnd[:], 3.1415925, -3.1415925, ALU.min, ALU.max)\
                             .then_inc(sin_dve, 1)
                    n += 5
                    for t in range(2 * layer, 2 * layer + 2):
                        columns(t, t % 2)
                v.wait_ge(sin_act, 7)
                v.memset(hid2[64:P, 0, 64:65], 0.0).then_inc(bar, 1)
                v.memset(hid2[64:P, N2 + 1, 0:1], 0.0).then_inc(bar, 1)
                v.scalar_tensor_tensor(dec[:], dec[:], -1.0, dec[:], ALU.mult, ALU.max).then_inc(bar, 1)

                def taps_of(t, h):
                    v.wait_ge(pst.sem, pst.at(t, "taps"))
                    v.wait_ge(ast.sem, ast.at(t, "env"))
                    v.wait_ge(pst.sem, pst.at(t - 2, "spec"))
                    v.tensor_tensor(taps[:, h, :], pa[:, h, :], env[:, h, :], ALU.mult)\
                     .then_inc(*vst.inc("taps"))

                def tap_zero(t, h):
                    v.wait_ge(pst.sem, pst.at(t, "taps"))
                    v.wait_ge(ast.sem, ast.at(t, "env"))
                    v.wait_ge(pst.sem, pst.at(t - 2, "spec"))
                    v.tensor_tensor(taps[:, h, :], pa[:, h, :], env[:, h, :], ALU.mult).then_inc(bar, 1)

                def spec_of(t, h, k):
                    v.wait_ge(pst.sem, pst.at(t, "spec"))
                    v.wait_ge(sst[h], k * 16 + HAD)
                    v.tensor_copy(spec[:, h, :], pa[:, 2 + h, :]).then_inc(*vst.inc("spec"))

                def skip_weight(count):
                    v.wait_ge(bar, count)
                    v.tensor_tensor(taps[0:1, 0, :], taps[0:1, 0, :], bias0[:], ALU.add)\
                     .then_inc(*vst.inc("taps"))

                def pair(i):
                    if isinstance(i, int) and i == 0:
                        tap_zero(0, 0)
                        skip_weight(10)
                        spec_of(0, 0, 0)
                        taps_of(1, 1)
                        spec_of(1, 1, 0)
                        return
                    for h in range(2):
                        taps_of(i * 2 + h, h)
                        spec_of(i * 2 + h, h, i)

                groups(v, pair, columns)
                tap_zero(N2, 0)
                skip_weight(11)
                v.wait_ge(sst[0], N2 * 8 + HAD)
                v.wait_ge(sst[1], N2 * 8 + HAD)
                v.wait_ge(pst.sem, pst.at(N2, "spec"))
                v.engine_nop().then_inc(*vst.inc("spec"))
                taps_of(N2 + 1, 1)
                v.wait_ge(pst.sem, pst.at(N2 + 1, "spec"))
                for r in range(2):
                    v.tensor_copy(spec[:, r, :], pa[:, 2 + r, :]).then_inc(cspec, 1)

                v.wait_ge(modt, 1)
                v.tensor_copy(s["shift1"][:], pmt[:, 0:2 * KT].rearrange("p (a b) -> p a b", b=2)).then_inc(modr, 1)
                v.scalar_tensor_tensor(s["scale1"][:], pmt[:, 2 * KT:4 * KT].rearrange("p (a b) -> p a b", b=2), 1.0,
                                       g1n[:].unsqueeze(2).broadcast_to([P, KT, 2]), ALU.add, ALU.mult)\
                 .then_inc(modr, 1)


def layout(x):
    c = np.ascontiguousarray
    o = {}
    o["xs"] = c(np.concatenate([x["x_sample"][0], x["x_prompt"][0]], 0).reshape(NT, P, DM))
    col = lambda v: c(v.reshape(-1, P).T)
    o["cond"] = c(np.stack([col(x["c"][0]), col(x["c_ctx"])], 2))
    o["w_mod"] = c(x["w_mod"][0].reshape(KT, P, 12, 512).transpose(2, 1, 0, 3))
    o["b_mod"] = c(x["b_mod"])
    o["norm1_g"] = col(x["norm1_g"][0])
    w = x["w_in"][0].reshape(KT, P, 5632)
    o["w_hy"] = c(w[:, :, :1536].reshape(KT, P, 3, CB, P).transpose(3, 1, 2, 0, 4))
    o["w_qkvg"] = c(w[:, :, 1536:3584].reshape(KT, P, 4, 512).transpose(2, 1, 0, 3))
    o["w_gates"] = c(w[:, :, 3584:].transpose(1, 0, 2))
    o["conv"] = c(np.concatenate([x["hy_conv_w"][0], x["hy_conv_b"]], 0).reshape(4, 3, CB, P).transpose(2, 3, 1, 0))
    o["f_w1"], o["f_w2"] = c(x["hy_f_w1"][0]), c(x["hy_f_w2"][0])
    o["f_col"] = c(np.tile(np.stack([x["hy_f_b1"][0], x["hy_f_freq"][0], x["hy_f_b2"][0]], 1), (2, 1)))
    o["f_w3"] = c(x["hy_f_w3"][0].reshape(FH, 2, DH).transpose(1, 0, 2).reshape(P, DH))
    o["decay"] = c(x["hy_decay"][0].reshape(2, DH))
    o["hy_bias"] = c(x["hy_bias"])
    o["ret_decay"] = c(np.concatenate([x["ret_decay_fwd"], x["ret_decay_bwd"]], 1))
    o["ret_gn_g"] = c(x["ret_gn_g"])
    o["state_f"] = c(x["state_ret_fwd"][0, 0].transpose(1, 0, 2).reshape(P, 512))
    o["state_b"] = c(x["state_ret_bwd"][0, 0].transpose(1, 0, 2).reshape(P, 512))
    o["w_hy_o"] = c(x["w_hy_o"][0].reshape(CB, P, DM).transpose(1, 0, 2))
    o["w_ret_o"] = c(x["w_ret_o"][0].reshape(CB, P, DM).transpose(1, 0, 2))
    o["w_out"] = c(x["w_out"][0].reshape(KT, P, DM).transpose(1, 0, 2))
    o["norm2_g"] = c(x["norm2_g"])
    o["norm_f_g"] = c(x["norm_f_g"].reshape(1, DM))
    o["w_router"] = c(x["w_router"][0].reshape(KT, P, NE).transpose(1, 0, 2))
    o["w_gate"] = c(x["w_e_gate"][0].reshape(NE, KT, P, 4, 256).transpose(0, 3, 2, 1, 4))
    o["w_up"] = c(x["w_e_up"][0].reshape(NE, KT, P, 4, 256).transpose(0, 3, 2, 1, 4))
    o["w_down"] = c(x["w_e_down"][0].reshape(NE, 4, 2, P, DM).transpose(0, 1, 3, 2, 4))
    return o


def persistent(nc, ctx):
    sb = lambda n, sh, dt=F32: ctx.enter_context(nc.sbuf_tensor(n, sh, dt))
    return {
        "own": [], "last": [], "stack": ExitStack(), "last_stack": ExitStack(),
        "ident": sb("ident", [P, P]),
        "scale1": sb("scale1", [P, KT, 2]),
        "shift1": sb("shift1", [P, KT, 2]),
        "aff": sb("aff", [P, NT, NE]),
    }


def log_decays_vector(v, lg, raw, tmp, done_a, done_v):
    a, y, w, r, e = (tmp[:, n, :] for n in range(5))
    v.scalar_tensor_tensor(a, raw[:], -1.0, raw[:], ALU.mult, ALU.max).then_inc(done_v, 1)
    v.wait_ge(done_a, 1)
    v.tensor_scalar(w, y, 1.0, None, ALU.add).then_inc(done_v, 1)
    v.wait_ge(done_a, 2)
    v.tensor_scalar(a, w, -1.0, 1e-30, ALU.add, ALU.max).then_inc(done_v, 1)
    v.wait_ge(done_v, 3)
    v.reciprocal(e, a).then_inc(done_v, 1)
    v.wait_ge(done_v, 4)
    v.tensor_tensor(e, e, r, ALU.mult).then_inc(done_v, 1)
    v.tensor_scalar(a, w, 1.0, None, ALU.is_equal).then_inc(done_v, 1)
    v.wait_ge(done_v, 6)
    v.tensor_tensor(e, e, a, ALU.add).then_inc(done_v, 1)
    v.wait_ge(done_v, 7)
    v.tensor_tensor(e, e, y, ALU.mult).then_inc(done_v, 1)
    v.wait_ge(done_v, 8)
    v.scalar_tensor_tensor(lg[:], raw[:], 0.0, e, ALU.min, ALU.subtract).then_inc(done_v, 1)


def log_decays_scalar(act, tmp, done_a, done_v):
    a, y, w, r = (tmp[:, n, :] for n in range(4))
    act.wait_ge(done_v, 1)
    act.activation(y, a, ACT.Exp, scale=-1.0).then_inc(done_a, 1)
    act.wait_ge(done_v, 2)
    act.activation(r, w, ACT.Ln).then_inc(done_a, 1)


def phase_tokens(nc, d, s):
    with ExitStack() as ctx:
        sb, pb, sem, counted = makers(nc, ctx, s, "tokens")
        wh = sb("w_high", [P, 4, KT, 512], F32R)
        wl = sb("w_low", [P, 4, KT, 512], F32R)
        x = sb("x", [P, 2, DM])
        ssq = sb("ssq", [P, 2])
        rstd = sb("rstd", [P, 2])
        eps = sb("eps", [P, 1])
        xn = sb("xn", [P, DM])
        hT = sb("hT", [P, KT, P])
        hh = sb("h_high", [P, 2, KT, P], F32R)
        hl = sb("h_low", [P, 2, KT, P], F32R)
        rope = sb("rope", [P, 2, 4, P])
        cosm = sb("cosm", [P, 512])
        qk = sb("qk", [P, 2, 512])
        sinm = sb("sinm", [P, 512])
        qkT = sb("qkT", [P, 2, 2, 512])
        vs = sb("vs", [P, 2, 512])
        vz = sb("vz", [P, 2, 512])
        gs = sb("gs", [P, 2, 512])
        gn = sb("gn", [P, 512])
        state = sb("state", [P, 2, 512])
        kvb = sb("kvb", [P, 2, 512])
        kvf = sb("kvf", [P, 512])
        raw = sb("raw", [P, 8])
        lg = sb("lg", [P, 8])
        tmp = sb("tmp", [P, 5, 8])
        expo = sb("expo", [P, 2])
        zeta = sb("zeta", [P, 8])
        dec = sb("dec", [P, 8])
        tp = pb("tp", [P, KT * P])
        pq = [pb(f"p{n}", [P, 512]) for n in "qkvg"]
        qt = [pb(f"pt{n}", [P, 512]) for n in "qk"]

        ldw, ldc = [sem(f"ld_w{n}") for n in range(3)], sem("ld_c")
        w_act, w_dve = sem("w_high_ready"), sem("w_split")
        staged = [qkT[:, 0].rearrange("p a b -> p (a b)"), qkT[:, 1].rearrange("p a b -> p (a b)"),
                  kvb[:].rearrange("p a b -> p (a b)")]
        PIECES = [(n, k) for n in range(4) for k in range(0, KT, 2)]
        xld = [sem(f"ld_x{h}") for h in range(2)]
        rld = [sem(f"ld_rope{h}") for h in range(2)]
        hst = sem("st_h")
        qst = [sem(f"st_qk{h}") for h in range(2)]
        vst = [sem(f"st_v{h}") for h in range(2)]
        sst = [sem(f"st_state{h}") for h in range(2)]
        kst = [sem(f"st_kvb{h}") for h in range(2)]
        fin = sem("st_final")
        ca, cv, cs = sem("decay_act"), sem("decay_dve"), sem("consts")
        AF = counted("act_front", ["square", "sqrt", "xn"] + [f"h{k}" for k in range(KT // 2)] + ["high"])
        VF = counted("dve_front", ["rstd"] + [f"h{k}" for k in range(KT // 2, KT)] + ["low"])
        PF = counted("pe_front", ["xT"])
        PB = counted("pe_back", ["q", "k", "v", "g", "qkT", "kvf", "kvb"])
        AB = counted("act_back", ["v", "silu", "qT", "kT", "kvb"])
        VB = counted("dve_back", ["qc", "qs1", "qs2", "q", "kc", "ks1", "ks2", "k",
                                         "s0", "s1", "s2", "s3"])
        GB = counted("pool_back", ["vzf", "vzb", "gs"])
        LOOP = NLAT - 2

        with nc.Block() as block:
            @block.sync
            def _(sp):
                had(sp, hst, qst, vst, kst, sst)
                sp.dma_start(raw[:], d["ret_decay"].partition_broadcast(P)).then_inc(ldc, 16)
                sp.dma_start(expo[:], d["expo"]).then_inc(ldc, 16)
                sp.dma_start(gn[:], d["ret_gn_g"].partition_broadcast(P)).then_inc(ldc, 16)
                sp.dma_start(state[:, 0, :], d["state_f"]).then_inc(ldc, 16)

                def load_x(t, h):
                    sp.wait_ge(AF.sem, AF.at(t - 2, "xn"))
                    sp.dma_start(x[:, h, :], d["xs"][take(t, 1)]).then_inc(xld[h], 16)

                def load_rope(t, h):
                    sp.wait_ge(VB.sem, VB.at(t - 2, "k"))
                    sp.dma_start(rope[:, h].rearrange("p a b -> p (a b)"), d["rope"][take(t, 1)])\
                      .then_inc(rld[h], 16)

                def stores(t, h, more):
                    context = isinstance(t, int) and t == NLAT
                    sp.wait_ge(AF.sem, AF.at(t, "h3"))
                    sp.wait_ge(VF.sem, VF.at(t, "h7"))
                    sp.dma_start(d["hT"][:, :, take(t * P, P)], hT[:]).then_inc(hst, 16)
                    if more:
                        load_x(t + 2, h)
                    if not context:
                        sp.wait_ge(VB.sem, VB.at(t - 1, "s3"))
                        sp.dma_start(d["state"][take(t, 1)], state[:, h, :]).then_inc(sst[h], 16)
                    if more:
                        load_rope(t + 2, h)
                    sp.wait_ge(AB.sem, AB.at(t, "v"))
                    sp.dma_start(d["v"][take(t, 1)], vs[:, h, :]).then_inc(vst[h], 16)
                    sp.wait_ge(GB.sem, GB.at(t, "gs"))
                    sp.dma_start(d["gs"][take(t, 1)], gs[:, h, :]).then_inc(vst[h], 16)
                    sp.wait_ge(AB.sem, AB.at(t, "kT"))
                    sp.dma_start(d["qkT"][take(t, 1)], qkT[:, h].rearrange("p a b -> p (a b)")).then_inc(qst[h], 16)
                    sp.wait_ge(AB.sem, AB.at(t, "kvb"))
                    if context:
                        sp.dma_start(d["new_b"].rearrange("e p c -> p e c"),
                                     kvb[:, h, :].rearrange("p (e c) -> p e c", e=HEADS)).then_inc(kst[h], 16)
                        sp.wait_ge(VB.sem, VB.at(t, "s3"))
                        sp.dma_start(d["new_f"].rearrange("e p c -> p e c"),
                                     kvf[:].rearrange("p (e c) -> p e c", e=HEADS)).then_inc(fin, 16)
                    else:
                        sp.dma_start(d["kvb"][take(t, 1)], kvb[:, h, :]).then_inc(kst[h], 16)

                load_x(0, 0)
                load_x(1, 1)
                load_rope(0, 0)
                load_rope(1, 1)
                for m, (n, k) in enumerate(PIECES):
                    if m >= 3:
                        sp.wait_ge(w_dve, m - 2)
                    sp.dma_start(staged[m % 3].rearrange("p (a b) -> p a b", b=512), d["w_qkvg"][n, :, k:k + 2, :])\
                      .then_inc(ldw[m % 3], 16)
                sp.wait_ge(ldc, 64)
                with sp.Fori(0, LOOP // 2, 1) as i:
                    for h in range(2):
                        stores(i * 2 + h, h, True)
                for t in range(LOOP, NT):
                    stores(t, t % 2, t + 2 < NT)
                for h in range(2):
                    rounds = (NT + 1 - h) // 2
                    sp.wait_ge(qst[h], 16 * rounds + HAD)
                    sp.wait_ge(vst[h], 32 * rounds + HAD)
                    sp.wait_ge(kst[h], 16 * rounds + HAD)
                    sp.wait_ge(sst[h], 16 * (NLAT // 2) + HAD)
                sp.wait_ge(hst, 16 * NT + HAD)
                sp.wait_ge(fin, 16)
                retire(sp, s)

            @block.tensor
            def _(pe):
                PF.give(pe)
                PB.give(pe)

                def front(t, h):
                    pe.wait_ge(AF.sem, AF.at(t, "xn"))
                    pe.wait_ge(AF.sem, AF.at(t - 1, "h3"))
                    pe.wait_ge(VF.sem, VF.at(t - 1, "h7"))
                    for k in range(KT):
                        mm = pe.transpose(tp[:, P * k:P * k + P], xn[:, P * k:P * k + P], s["ident"][:])
                    mm.then_inc(*PF.inc("xT"))

                def project(t, h, n, name):
                    pe.wait_ge(w_dve, 4 * n + 4)
                    for k in range(KT):
                        mm = product(pe, pq[n][:], (hh[:, h, k, :], hl[:, h, k, :]), (wh[:, n, k, :], wl[:, n, k, :]),
                                     k == 0, k == KT - 1)
                    mm.then_inc(*PB.inc(name))

                def back_1(t, h):
                    pe.wait_ge(AF.sem, AF.at(t, "high"))
                    pe.wait_ge(VF.sem, VF.at(t, "low"))
                    pe.wait_ge(VB.sem, VB.at(t - 1, "q"))
                    project(t, h, 0, "q")
                    pe.wait_ge(VB.sem, VB.at(t - 1, "k"))
                    project(t, h, 1, "k")

                def back_2(t, h):
                    pe.wait_ge(VB.sem, VB.at(t - 1, "s3"))
                    project(t, h, 2, "v")
                    pe.wait_ge(AB.sem, AB.at(t - 1, "kvb"))
                    project(t, h, 3, "g")
                    pe.wait_ge(VB.sem, VB.at(t, "k"))
                    pe.wait_ge(AB.sem, AB.at(t - 1, "kT"))
                    for n in range(2):
                        for e in range(HEADS):
                            mm = pe.transpose(qt[n][:, P * e:P * e + P], qk[:, n, P * e:P * e + P], s["ident"][:])
                    mm.then_inc(*PB.inc("qkT"))
                    for n, name in enumerate(("kvf", "kvb")):
                        pe.wait_ge(GB.sem, GB.at(t, ("vzf", "vzb")[n]))
                        pe.wait_ge(AB.sem, AB.at(t, ("v", "silu")[n]))
                        for e in range(HEADS):
                            mm = pe.matmul(pq[2 + n][:, P * e:P * e + P], qk[:, 1, P * e:P * e + P],
                                           vz[:, n, P * e:P * e + P], start=True, stop=True)
                        mm.then_inc(*PB.inc(name))

                front(0, 0)
                with pe.Fori(0, LOOP // 2, 1) as i:
                    for h in range(2):
                        back_1(i * 2 + h, h)
                        front(i * 2 + (h + 1), 1 - h)
                        back_2(i * 2 + h, h)
                for t in range(LOOP, NT):
                    back_1(t, t % 2)
                    if t + 1 < NT:
                        front(t + 1, (t + 1) % 2)
                    back_2(t, t % 2)

            @block.scalar
            def _(act):
                AF.give(act)
                AB.give(act)
                log_decays_scalar(act, tmp, ca, cv)
                act.wait_ge(cv, 9)
                for n in range(2):
                    act.activation(zeta[:, 4 * n:4 * n + 4], lg[:, 4 * n:4 * n + 4], ACT.Exp, scale=expo[:, n:n + 1])\
                       .then_inc(cs, 1)
                act.activation(dec[:], lg[:], ACT.Exp, scale=float(P)).then_inc(cs, 1)
                act.wait_ge(cs, 4)

                def front(t, h, cond, k):
                    act.wait_ge(xld[h], 16 * (k + 1))
                    act.wait_ge(PF.sem, PF.at(t - 1, "xT"))
                    act.wait_ge(AF.sem, AF.at(t - 1, "xn"))
                    act.activation(xn[:], x[:, h, :], ACT.Square, scale=DM ** -0.5, accum_out=ssq[:, h:h + 1])\
                       .then_inc(*AF.inc("square"))
                    act.wait_ge(AF.sem, AF.at(t, "square"))
                    act.activation(rstd[:, h:h + 1], ssq[:, h:h + 1], ACT.Sqrt, bias=eps[:]).then_inc(*AF.inc("sqrt"))
                    act.wait_ge(VF.sem, VF.at(t, "rstd"))
                    act.activation(xn[:], x[:, h, :], ACT.Copy, scale=rstd[:, h:h + 1]).then_inc(*AF.inc("xn"))
                    act.wait_ge(PF.sem, PF.at(t, "xT"))
                    act.wait_ge(hst, 16 * t + HAD)
                    act.wait_ge(VF.sem, VF.at(t - 1, "low"))
                    for m in range(KT // 2):
                        act.activation(hT[:, m, :], tp[:, P * m:P * m + P], ACT.Identity,
                                       bias=s["shift1"][:, m, cond:cond + 1], scale=s["scale1"][:, m, cond:cond + 1])\
                           .then_inc(*AF.inc(f"h{m}"))
                    act.wait_ge(AF.sem, AF.at(t, "h3"))
                    act.wait_ge(VF.sem, VF.at(t, "h7"))
                    act.wait_ge(PB.sem, PB.at(t - 2, "g"))
                    act.activation(hh[:, h].rearrange("p a b -> p (a b)"), hT[:].rearrange("p a b -> p (a b)"),
                                   ACT.Copy).then_inc(*AF.inc("high"))

                def back_1(t, h, k):
                    act.wait_ge(PB.sem, PB.at(t, "v"))
                    act.wait_ge(vst[h], 32 * k + HAD)
                    act.wait_ge(GB.sem, GB.at(t - 2, "vzb"))
                    act.activation(vs[:, h, :], pq[2][:], ACT.Copy).then_inc(*AB.inc("v"))
                    act.wait_ge(PB.sem, PB.at(t, "g"))
                    act.activation(gs[:, h, :], pq[3][:], ACT.Silu).then_inc(*AB.inc("silu"))
                    act.wait_ge(PB.sem, PB.at(t, "qkT"))
                    act.wait_ge(qst[h], 16 * k + HAD)
                    for n, name in enumerate(("qT", "kT")):
                        act.activation(qkT[:, h, n, :], qt[n][:], ACT.Copy).then_inc(*AB.inc(name))
                    act.wait_ge(PB.sem, PB.at(t, "kvb"))
                    act.wait_ge(kst[h], 16 * k + HAD)
                    act.activation(kvb[:, h, :], pq[3][:], ACT.Copy).then_inc(*AB.inc("kvb"))

                front(0, 0, 0, 0)
                for m, (n, k) in enumerate(PIECES):
                    act.wait_ge(ldw[m % 3], 16 * (m // 3 + 1))
                    act.activation(wh[:, n, k:k + 2].rearrange("p a b -> p (a b)"), staged[m % 3], ACT.Copy)\
                       .then_inc(w_act, 1)
                with act.Fori(0, LOOP // 2, 1) as i:
                    front(i * 2 + 1, 1, 0, i)
                    back_1(i * 2, 0, i)
                    front(i * 2 + 2, 0, 0, i + 1)
                    back_1(i * 2 + 1, 1, i)
                for t in range(LOOP, NT):
                    if t + 1 < NT:
                        front(t + 1, (t + 1) % 2, int(t + 1 == NT - 1), (t + 1) // 2)
                    back_1(t, t % 2, t // 2)

            @block.vector
            def _(v):
                VF.give(v)
                VB.give(v)
                v.memset(eps[:], EPS).then_inc(cs, 1)
                v.wait_ge(ldc, 64)
                log_decays_vector(v, lg, raw, tmp, ca, cv)
                v.wait_ge(cs, 4)

                def front(t, h, cond, k):
                    v.wait_ge(PF.sem, PF.at(t, "xT"))
                    v.wait_ge(hst, 16 * t + HAD)
                    v.wait_ge(AF.sem, AF.at(t - 1, "high"))
                    for m in range(KT // 2, KT):
                        v.tensor_scalar(hT[:, m, :], tp[:, P * m:P * m + P], s["scale1"][:, m, cond:cond + 1],
                                        s["shift1"][:, m, cond:cond + 1], ALU.mult, ALU.add).then_inc(*VF.inc(f"h{m}"))
                    v.wait_ge(AF.sem, AF.at(t, "high"))
                    v.wait_ge(VF.sem, VF.at(t, "h7"))
                    v.wait_ge(PB.sem, PB.at(t - 2, "g"))
                    v.tensor_tensor(hl[:, h].rearrange("p a b -> p (a b)"), hT[:].rearrange("p a b -> p (a b)"),
                                    hh[:, h].rearrange("p a b -> p (a b)").bitcast(F32), ALU.subtract)\
                     .then_inc(*VF.inc("low"))

                def norm(t, h):
                    v.wait_ge(AF.sem, AF.at(t, "sqrt"))
                    v.reciprocal(rstd[:, h:h + 1], rstd[:, h:h + 1]).then_inc(*VF.inc("rstd"))

                def turn(t, h, k, n, name):
                    v.wait_ge(PB.sem, PB.at(t, name))
                    if n == 0:
                        v.wait_ge(rld[h], 16 * (k + 1))
                    v.wait_ge(PB.sem, PB.at(t - 1, "kvb" if n else "qkT"))
                    v.wait_ge(VB.sem, VB.at(t, "q") if n else VB.at(t - 1, "k"))
                    heads = lambda a: a.rearrange("p (e c) -> p e c", e=HEADS)
                    v.tensor_tensor(heads(cosm[:]), heads(pq[n][:]),
                                    rope[:, h, 2 * n, :].unsqueeze(1).broadcast_to([P, HEADS, P]), ALU.mult)\
                     .then_inc(*VB.inc(name + "c"))
                    part = lambda a: a.rearrange("p (e g u c) -> p e g u c", e=HEADS, g=2, u=2)
                    sin = rope[:, h, 2 * n + 1, :].rearrange("p (g u c) -> p g u c", g=2, u=2)
                    for u in range(2):
                        v.tensor_tensor(part(sinm[:])[:, :, :, u, :], part(pq[n][:])[:, :, :, 1 - u, :],
                                        sin[:, :, u, :].unsqueeze(1).broadcast_to([P, HEADS, 2, 32]), ALU.mult)\
                         .then_inc(*VB.inc(f"{name}s{u + 1}"))
                    v.wait_ge(VB.sem, VB.at(t, name + "s2"))
                    v.tensor_tensor(qk[:, n, :], cosm[:], sinm[:], ALU.add).then_inc(*VB.inc(name))

                def back_1(t, h, k):
                    turn(t, h, k, 0, "q")
                    turn(t, h, k, 1, "k")

                def back_2(t, h, k):
                    v.wait_ge(PB.sem, PB.at(t, "kvf"))
                    context = isinstance(t, int) and t == NLAT
                    if not context:
                        v.wait_ge(sst[1 - h], 16 * (k + h) + HAD)
                    for e in range(HEADS):
                        cut = slice(P * e, P * e + P)
                        if context:
                            v.tensor_copy(kvf[:, cut], pq[2][:, cut]).then_inc(*VB.inc(f"s{e}"))
                        else:
                            v.wait_ge(VB.sem, VB.at(t - 1, f"s{e}"))
                            v.scalar_tensor_tensor(state[:, 1 - h, cut], state[:, h, cut], dec[:, e:e + 1],
                                                   pq[2][:, cut], ALU.mult, ALU.add).then_inc(*VB.inc(f"s{e}"))

                norm(0, 0)
                front(0, 0, 0, 0)
                for m, (n, k) in enumerate(PIECES):
                    v.wait_ge(w_act, m + 1)
                    flat = lambda a: a[:, n, k:k + 2].rearrange("p a b -> p (a b)")
                    v.tensor_tensor(flat(wl), staged[m % 3], flat(wh).bitcast(F32), ALU.subtract).then_inc(w_dve, 1)
                with v.Fori(0, LOOP // 2, 1) as i:
                    for h in range(2):
                        norm(i * 2 + (h + 1), 1 - h)
                        back_1(i * 2 + h, h, i)
                        front(i * 2 + (h + 1), 1 - h, 0, i + h)
                        back_2(i * 2 + h, h, i)
                for t in range(LOOP, NT):
                    if t + 1 < NT:
                        norm(t + 1, (t + 1) % 2)
                    back_1(t, t % 2, t // 2)
                    if t + 1 < NT:
                        front(t + 1, (t + 1) % 2, int(t + 1 == NLAT), (t + 1) // 2)
                    back_2(t, t % 2, t // 2)

            @block.gpsimd
            def _(g):
                GB.give(g)
                g.wait_ge(cs, 4)
                g.wait_ge(ldc, 64)

                def back(t, h, k):
                    g.wait_ge(AB.sem, AB.at(t, "v"))
                    g.wait_ge(PB.sem, PB.at(t - 1, "kvb"))
                    for n, name in enumerate(("vzf", "vzb")):
                        g.tensor_tensor(vz[:, n, :].rearrange("p (e c) -> p e c", e=HEADS),
                                        vs[:, h, :].rearrange("p (e c) -> p e c", e=HEADS),
                                        zeta[:, 4 * n:4 * n + 4].unsqueeze(2).broadcast_to([P, HEADS, P]), ALU.mult)\
                         .then_inc(*GB.inc(name))
                    g.wait_ge(AB.sem, AB.at(t, "silu"))
                    g.tensor_tensor(gs[:, h, :], gs[:, h, :], gn[:], ALU.mult).then_inc(*GB.inc("gs"))

                with g.Fori(0, NLAT // 2, 1) as i:
                    for h in range(2):
                        back(i * 2 + h, h, i)
                back(NLAT, 0, NLAT // 2)


ZW = TOK + 4
SPANS = [(512 * b, min(512, TOK - 512 * b)) for b in range(5)]


def place_of(token):
    return token + 1 if token < LAT else token + 3


def phase_hyena_in(nc, d, s):
    GR = N2 // 4
    with ExitStack() as ctx:
        sb, pb, sem, counted = makers(nc, ctx, s, "hyin")
        hh = sb("hT_high", [P, KT, TOK], F32R)
        hl = sb("hT_low", [P, KT, TOK], F32R)
        raw = sb("w_hy", [P, KT, P])
        wh = sb("w_high", [P, 2, KT, P], F32R)
        wl = sb("w_low", [P, 2, KT, P], F32R)
        conv = sb("conv", [P, CB, 3, 4])
        z = sb("z", [P, ZW])
        c = sb("c", [P, 2, ZW])
        u = sb("u", [P, TOK])
        f1 = sb("f1u", [P, 2 * P])
        ut = sb("ut", [P, 2, 256])
        us = sb("us", [P, 2, 4, P])
        uc = sb("uc", [P, P])
        HALF = KT // 2
        staged = [c[:, 0, :], c[:, 1, :], z[:], u[:]]
        PIECES = [(b, HALF * g) for b in range(len(SPANS)) for g in range(2)]

        def piece(m):
            b, k = PIECES[m]
            at, n = SPANS[b]
            return (staged[m % 4][:, 0:HALF * n].rearrange("p (k n) -> p k n", k=HALF),
                    lambda a: a[:, k:k + HALF, at:at + n])

        pz = pb("pz", [P, 5, 512])
        pt = pb("pt", [P, 2, 512])
        ps = pb("ps", [P, 512])
        hld = [sem(f"ld_h{b}") for b in range(4)]
        wld = sem("ld_why")
        h_act, h_dve = sem("h_high_ready"), sem("h_split")
        AW, VW = (counted(f"{n}_w_hy", [f"w{m}" for m in range(3)]) for n in ("act", "dve"))
        ldc = sem("ld_hyc")
        xst = sem("st_x2")
        ust = [sem(f"st_u{h}") for h in range(2)]
        cst = sem("st_uctx")
        pads = sem("pads")
        zs = [[f"z{m}{b}" for b in range(5)] for m in range(3)]
        tail = ["T0"] + sum([[f"T{g + 1}", f"S{g}"] for g in range(GR - 1)], []) + ["TC", f"S{GR - 1}"]
        PS = counted("pe_hy", sum(zs, []) + tail)
        AS = counted("act_hy", sum([zs[m] + [f"c{m}"] for m in range(3)], []) + [f"S{g}" for g in range(GR)])
        VS = counted("dve_hy", ["a0", "b0", "a1", "b1", "ul", "u"] + [f"T{g}" for g in range(GR)] + ["TC", "a2", "b2"])

        with nc.Block() as block:
            @block.sync
            def _(sp):
                had(sp, xst, cst, ust)
                sp.dma_start(conv[:], d["conv"].rearrange("i p z k -> p i z k")).then_inc(ldc, 16)
                sp.dma_start(f1[:], d["f1u"]).then_inc(ldc, 16)

                def weights(i, m):
                    sp.wait_ge(VW.sem, VW.at(i, f"w{m - 1}") if m else VW.at(i - 1, "w2"))
                    sp.dma_start(raw[:], d["w_hy"][i, :, m]).then_inc(wld, 16)

                weights(0, 0)
                for m, (b, k) in enumerate(PIECES):
                    if m >= 4:
                        sp.wait_ge(h_dve, m - 3)
                    at, n = SPANS[b]
                    sp.dma_start(piece(m)[0], d["hT"][:, k:k + HALF, at:at + n]).then_inc(hld[m % 4], 16)
                for i in range(CB):
                    weights(i, 1)
                    weights(i, 2)
                    if i + 1 < CB:
                        weights(i + 1, 0)
                    for g in range(GR):
                        sp.wait_ge(AS.sem, AS.at(i, f"S{g}"))
                        sp.dma_start(d["uspec"][:, 4 * g:4 * g + 4, P * i:P * i + P], us[:, g % 2]).then_inc(ust[g % 2], 16)
                    sp.wait_ge(VS.sem, VS.at(i, "TC"))
                    sp.dma_start(d["uctx"][:, P * i:P * i + P], uc[:]).then_inc(cst, 16)
                    sp.wait_ge(VS.sem, VS.at(i, "b2"))
                    sp.dma_start(d["x2"][i], c[:, 0, 1:ZW - 1]).then_inc(xst, 16)
                sp.wait_ge(xst, 16 * CB + HAD)
                sp.wait_ge(cst, 16 * CB + HAD)
                for h in range(2):
                    sp.wait_ge(ust[h], 16 * CB * GR // 2 + HAD)
                retire(sp, s)

            @block.tensor
            def _(pe):
                PS.give(pe)
                pe.wait_ge(ldc, 32)

                def block_of(i, h, k):
                    for m in range(3):
                        slot = (3 * h + m) % 2
                        pe.wait_ge(VW.sem, VW.at(i, f"w{m}"))
                        for b, (at, n) in enumerate(SPANS):
                            if m == 0:
                                pe.wait_ge(h_dve, 2 * b + 2)
                            if m == 0:
                                pe.wait_ge(AS.sem, AS.at(i - 1, zs[2][b]))
                            else:
                                pe.wait_ge(AS.sem, AS.at(i, zs[m - 1][b]))
                            for q in range(KT):
                                mm = product(pe, pz[:, b, 0:n], (wh[:, slot, q, :], wl[:, slot, q, :]),
                                             (hh[:, q, at:at + n], hl[:, q, at:at + n]), q == 0, q == KT - 1)
                            mm.then_inc(*PS.inc(zs[m][b]))
                    pe.wait_ge(VS.sem, VS.at(i, "u"))

                    def turn(g):
                        if g < 2:
                            pe.wait_ge(VS.sem, VS.at(i - 1, f"T{g + GR - 2}" if g else "TC"))
                        else:
                            pe.wait_ge(VS.sem, VS.at(i, f"T{g - 2}"))
                        for q in range(2):
                            at = K1 * (4 * g + 2 * q)
                            mm = pe.transpose(pt[:, g % 2, P * q:P * q + P], u[:, at:at + P], s["ident"][:])
                        mm.then_inc(*PS.inc(f"T{g}"))

                    def stage(g):
                        pe.wait_ge(VS.sem, VS.at(i, f"T{g}"))
                        pe.wait_ge(AS.sem, AS.at(i, f"S{g - 1}") if g else AS.at(i - 1, f"S{GR - 1}"))
                        for r in range(2):
                            mm = pe.matmul(ps[:].rearrange("p (q r c) -> p q r c", r=2, c=P)[:, :, r, :],
                                           f1[:, P * r:P * r + P], ut[:, g % 2, :].rearrange("p (q c) -> p q c", c=P),
                                           start=True, stop=True)
                        mm.then_inc(*PS.inc(f"S{g}"))

                    turn(0)
                    for g in range(GR - 1):
                        turn(g + 1)
                        stage(g)
                    pe.wait_ge(VS.sem, VS.at(i, f"T{GR - 2}"))
                    pe.transpose(pt[:, 0, 0:P], u[:, LAT:TOK], s["ident"][:]).then_inc(*PS.inc("TC"))
                    stage(GR - 1)

                with pe.Fori(0, CB // 2, 1) as i:
                    for h in range(2):
                        block_of(i * 2 + h, h, i)

            @block.scalar
            def _(act):
                AS.give(act)
                AW.give(act)
                act.wait_ge(ldc, 32)

                def split(i, m):
                    slot = (3 * i + m) % 2
                    act.wait_ge(wld, i * 48 + 16 * (m + 1))
                    act.wait_ge(PS.sem, PS.at(i, "z04") if m == 2 else PS.at(i - 1, zs[m + 1][4]))
                    act.activation(wh[:, slot].rearrange("p a b -> p (a b)"), raw[:].rearrange("p a b -> p (a b)"),
                                   ACT.Copy).then_inc(*AW.inc(f"w{m}"))

                def block_of(i):
                    for m in range(3):
                        if m < 2:
                            split(i, m + 1)
                        elif i + 1 < CB:
                            split(i + 1, 0)
                        for b, (at, n) in enumerate(SPANS):
                            act.wait_ge(PS.sem, PS.at(i, zs[m][b]))
                            if b == 0:
                                act.wait_ge(VS.sem, VS.at(i, f"b{m - 1}") if m else VS.at(i - 1, "b2"))
                            act.activation(z[:, place_of(at):place_of(at) + n], pz[:, b, 0:n], ACT.Copy)\
                               .then_inc(*AS.inc(zs[m][b]))
                        act.wait_ge(AS.sem, AS.at(i, zs[m][4]))
                        if m == 0:
                            act.wait_ge(xst, i * 16 + HAD)
                        else:
                            act.wait_ge(VS.sem, VS.at(i - 1, "u") if m == 1 else VS.at(i, "u"))
                        act.activation(c[:, m % 2, 1:ZW - 1], z[:, 1:ZW - 1], ACT.Identity,
                                       bias=conv[:, take(i, 1), m, 3], scale=conv[:, take(i, 1), m, 1])\
                           .then_inc(*AS.inc(f"c{m}"))
                    for g in range(GR):
                        act.wait_ge(PS.sem, PS.at(i, f"S{g}"))
                        act.wait_ge(ust[g % 2], 16 * (i * (GR // 2) + g // 2) + HAD)
                        act.activation(us[:, g % 2].rearrange("p a b -> p (a b)"), ps[:], ACT.Copy)\
                           .then_inc(*AS.inc(f"S{g}"))

                split(0, 0)
                for m in range(len(PIECES)):
                    act.wait_ge(hld[m % 4], 16 * (m // 4 + 1))
                    src, at = piece(m)
                    act.activation(at(hh), src, ACT.Copy).then_inc(h_act, 1)
                act.wait_ge(h_dve, len(PIECES))
                act.wait_ge(pads, 1)
                for i in range(CB):
                    block_of(i)

            @block.vector
            def _(v):
                VS.give(v)
                VW.give(v)
                v.wait_ge(ldc, 32)

                def split(i, m):
                    slot = (3 * i + m) % 2
                    v.wait_ge(AW.sem, AW.at(i, f"w{m}"))
                    flat = lambda a: a.rearrange("p a b -> p (a b)")
                    v.tensor_tensor(flat(wl[:, slot]), flat(raw[:]), flat(wh[:, slot]).bitcast(F32), ALU.subtract)\
                     .then_inc(*VW.inc(f"w{m}"))

                def block_of(i):
                    def convolve(m):
                        v.wait_ge(AS.sem, AS.at(i, f"c{m}"))
                        for step, (tap, off) in (("a", (0, 0)), ("b", (2, 2))):
                            if step == "b":
                                v.wait_ge(VS.sem, VS.at(i, f"a{m}"))
                            v.scalar_tensor_tensor(c[:, m % 2, 1:ZW - 1], z[:, off:off + ZW - 2],
                                                   conv[:, take(i, 1), m, tap], c[:, m % 2, 1:ZW - 1],
                                                   ALU.mult, ALU.add).then_inc(*VS.inc(f"{step}{m}"))

                    split(i, 1)
                    convolve(0)
                    split(i, 2)
                    convolve(1)
                    v.wait_ge(VS.sem, VS.at(i, "b1"))
                    v.wait_ge(PS.sem, PS.at(i - 1, "TC"))
                    by_n2 = lambda m: c[:, m, 1:1 + LAT].rearrange("p (a b) -> p b a", b=N2)
                    v.tensor_tensor(u[:, 0:LAT].rearrange("p (b a) -> p b a", b=N2), by_n2(0), by_n2(1), ALU.mult)\
                     .then_inc(*VS.inc("ul"))
                    at = place_of(LAT)
                    v.tensor_tensor(u[:, LAT:TOK], c[:, 0, at:at + CTX], c[:, 1, at:at + CTX], ALU.mult)\
                     .then_inc(*VS.inc("u"))
                    if i + 1 < CB:
                        split(i + 1, 0)
                    for g in range(GR):
                        v.wait_ge(PS.sem, PS.at(i, f"T{g}"))
                        v.wait_ge(PS.sem, PS.at(i, f"S{g - 2}") if g >= 2 else PS.at(i - 1, f"S{g + GR - 2}"))
                        v.tensor_copy(ut[:, g % 2, :], pt[:, g % 2, 0:256]).then_inc(*VS.inc(f"T{g}"))
                    v.wait_ge(PS.sem, PS.at(i, "TC"))
                    v.wait_ge(cst, 16 * i + HAD)
                    v.tensor_copy(uc[:], pt[:, 0, 0:P]).then_inc(*VS.inc("TC"))
                    convolve(2)

                split(0, 0)
                for m in range(len(PIECES)):
                    v.wait_ge(h_act, m + 1)
                    src, at = piece(m)
                    v.tensor_tensor(at(hl), src, at(hh).bitcast(F32), ALU.subtract).then_inc(h_dve, 1)
                v.wait_ge(h_dve, len(PIECES))
                for at in (0, LAT + 1, LAT + 2, ZW - 1):
                    mm = v.memset(z[:, at:at + 1], 0.0)
                mm.then_inc(pads, 1)
                for i in range(CB):
                    block_of(i)


def phase_spectrum(nc, d, s):
    SL = 4
    LOOP = PAIRS - SL
    with ExitStack() as ctx:
        sb, pb, sem, counted = makers(nc, ctx, s, "spectrum")
        ks = sb("ks", [P, SL, 512])
        us = sb("us2", [P, SL, 512])
        tg = sb("tg", [P, SL, 448])
        kr = sb("kr", [P, 2, 512])
        ki = sb("ki", [P, 2, 512])
        a = sb("prod_a", [P, 2, 512])
        b = sb("prod_b", [P, 2, 512])
        q = sb("q", [P, 2, 512])
        pk = pb("pk", [P, 2, 512])
        pu = pb("pu", [P, 4, 512])
        pq = pb("pq", [P, 2, 512])
        ld = [sem(f"ld_pair{n}") for n in range(SL)]
        st = [sem(f"st_pair{n}") for n in range(2)]
        PS = counted("pe_sp", ["kr", "ki", "u1", "u2"])
        PB = counted("pe_sp_back", ["q"])
        AS = counted("act_sp", ["kr", "ki"])
        AB = counted("act_sp_back", ["q"])
        VS = counted("dve_sp", ["a", "b", "p"])
        pairs = lambda name: d[name].rearrange("(a r) n c -> a (r n) c", r=4)

        def rounds(eng, front, back):
            front(0, 0, 0)
            with eng.Fori(0, LOOP // SL, 1) as i:
                for m in range(SL):
                    front(i * SL + (m + 1), (m + 1) % SL, i + (m + 1) // SL)
                    back(i * SL + m, m)
            for t in range(LOOP, PAIRS):
                if t + 1 < PAIRS:
                    front(t + 1, (t + 1) % SL, (t + 1) // SL)
                back(t, t % SL)

        with nc.Block() as block:
            @block.sync
            def _(sp):
                had(sp, st)
                def load(t, m):
                    sp.dma_start(ks[:, m], pairs("kspec")[take(t, 1)]).then_inc(ld[m], 16)
                    sp.dma_start(us[:, m], pairs("uspec")[take(t, 1)]).then_inc(ld[m], 16)
                    sp.dma_start(tg[:, m], d["tg"][take(t, 1)]).then_inc(ld[m], 16)

                def store(t, m):
                    sp.wait_ge(AB.sem, AB.at(t, "q"))
                    sp.dma_start(pairs("qspec")[take(t, 1)], q[:, m % 2]).then_inc(st[m % 2], 16)

                for m in range(SL):
                    load(m, m)
                with sp.Fori(0, LOOP // SL, 1) as i:
                    for m in range(SL):
                        sp.wait_ge(PB.sem, PB.at(i * SL + m, "q"))
                        load(i * SL + (m + SL), m)
                        store(i * SL + m, m)
                for t in range(LOOP, PAIRS):
                    store(t, t % SL)
                for h in range(2):
                    sp.wait_ge(st[h], 16 * PAIRS // 2 + HAD)
                retire(sp, s)

            @block.tensor
            def _(pe):
                PS.give(pe)
                PB.give(pe)

                def front(t, m, k):
                    pe.wait_ge(ld[m], 48 * (k + 1))
                    h = 2 * (m % 2)
                    for n, (name, col) in enumerate((("kr", 64), ("ki", 192))):
                        pe.wait_ge(AS.sem, AS.at(t - 1, name))
                        pe.matmul(pk[:, n, :], tg[:, m, col:col + P], ks[:, m, :], start=True, stop=True)\
                          .then_inc(*PS.inc(name))
                    for n, (name, col, read) in enumerate((("u1", 128, "a"), ("u2", 0, "b"))):
                        pe.wait_ge(VS.sem, VS.at(t - 2, read))
                        pe.matmul(pu[:, h + n, :], tg[:, m, col:col + P], us[:, m, :], start=True, stop=True)\
                          .then_inc(*PS.inc(name))

                def back(t, m):
                    pe.wait_ge(VS.sem, VS.at(t, "p"))
                    pe.wait_ge(AB.sem, AB.at(t - 2, "q"))
                    pe.matmul(pq[:, m % 2, :], tg[:, m, 320:448], a[:, m % 2, :], start=True, stop=True)\
                      .then_inc(*PB.inc("q"))

                rounds(pe, front, back)

            @block.scalar
            def _(act):
                AS.give(act)
                AB.give(act)

                def front(t, m, k):
                    for n, (name, dst, read) in enumerate((("kr", kr, "a"), ("ki", ki, "b"))):
                        act.wait_ge(PS.sem, PS.at(t, name))
                        act.wait_ge(VS.sem, VS.at(t - 2, read))
                        act.activation(dst[:, m % 2, :], pk[:, n, :], ACT.Copy).then_inc(*AS.inc(name))

                def back(t, m, k=None):
                    act.wait_ge(PB.sem, PB.at(t, "q"))
                    act.activation(q[:, m % 2, :], pq[:, m % 2, :], ACT.Copy).then_inc(*AB.inc("q"))

                front(0, 0, 0)
                with act.Fori(0, LOOP // SL, 1) as i:
                    for m in range(SL):
                        front(i * SL + (m + 1), (m + 1) % SL, 0)
                        act.wait_ge(st[m % 2], 16 * (i * (SL // 2) + m // 2) + HAD)
                        back(i * SL + m, m)
                for t in range(LOOP, PAIRS):
                    if t + 1 < PAIRS:
                        front(t + 1, (t + 1) % SL, 0)
                    act.wait_ge(st[t % 2], 16 * (t // 2) + HAD)
                    back(t, t % SL)

            @block.vector
            def _(v):
                VS.give(v)

                def product(t, m):
                    h = m % 2
                    v.wait_ge(AS.sem, AS.at(t, "kr"))
                    v.wait_ge(PS.sem, PS.at(t, "u1"))
                    v.wait_ge(PB.sem, PB.at(t - 2, "q"))
                    v.tensor_tensor(a[:, h, :], pu[:, 2 * h, :], kr[:, h, :], ALU.mult).then_inc(*VS.inc("a"))
                    v.wait_ge(AS.sem, AS.at(t, "ki"))
                    v.wait_ge(PS.sem, PS.at(t, "u2"))
                    v.tensor_tensor(b[:, h, :], pu[:, 2 * h + 1, :], ki[:, h, :], ALU.mult).then_inc(*VS.inc("b"))
                    v.wait_ge(VS.sem, VS.at(t, "b"))
                    v.tensor_tensor(a[:, h, :], a[:, h, :], b[:, h, :], ALU.add).then_inc(*VS.inc("p"))

                with v.Fori(0, PAIRS // SL, 1) as i:
                    for m in range(SL):
                        product(i * SL + m, m)


def phase_hyena_out(nc, d, s):
    with ExitStack() as ctx:
        sb, pb, sem, counted = makers(nc, ctx, s, "hyout")
        q = sb("qall", [P, 2, N2, P])
        x2 = sb("x2", [P, 2, LAT])
        y = sb("y", [P, 2, LAT])
        f2 = sb("f2", [P, K1])
        uc = sb("ucx", [P, 512])
        kc = sb("kc", [P, 2, 512])
        cf = sb("cfx", [P, 512])
        ci = sb("ci", [P, 256])
        xc = sb("xc", [P, CB, P])
        pr = sb("pr", [P, 4, 512])
        yc = sb("yc", [P, CB, P])
        py = pb("py", [P, 4, 512])
        pc = pb("pc", [P, 3, 512])
        ldc, stc = sem("ld_c4"), sem("st_c4")
        ld = [sem(f"ld_q{h}") for h in range(2)]
        st = [sem(f"st_y{h}") for h in range(2)]
        cpe, cdv = sem("ctx_pe"), sem("ctx_dve")
        PS = counted("pe_out", [f"y{g}" for g in range(4)])
        VS = counted("dve_out", [f"y{g}" for g in range(4)])

        with nc.Block() as block:
            @block.sync
            def _(sp):
                had(sp, st)
                for dst, src in ((uc[:], d["uctx"]), (kc[:], d["cspec"].rearrange("a p c -> p a c")), (cf[:], d["cf"]),
                                 (ci[:], d["ci"]), (f2[:], d["f2"]),
                                 (xc[:], d["x2"][:, :, LAT + 2:LAT + 2 + CTX].rearrange("i p c -> p i c"))):
                    sp.dma_start(dst, src).then_inc(ldc, 16)

                def load(i, h):
                    sp.dma_start(q[:, h], d["qspec"][:, :, take(i * P, P)]).then_inc(ld[h], 16)
                    sp.dma_start(x2[:, h, :], d["x2"][take(i, 1), :, 0:LAT]).then_inc(ld[h], 16)

                def store(i, h):
                    sp.wait_ge(VS.sem, VS.at(i, "y3"))
                    sp.dma_start(d["yhy"][:, take(i, 1), 0:LAT], y[:, h, :]).then_inc(st[h], 16)

                load(0, 0)
                load(1, 1)
                for i in range(CB):
                    store(i, i % 2)
                    if i + 2 < CB:
                        load(i + 2, i % 2)
                sp.wait_ge(cdv, 7)
                sp.dma_start(d["yhy"][:, :, LAT:TOK], yc[:]).then_inc(stc, 16)
                sp.wait_ge(stc, 16)
                for h in range(2):
                    sp.wait_ge(st[h], 16 * CB // 2 + HAD)
                retire(sp, s)

            @block.tensor
            def _(pe):
                PS.give(pe)
                pe.wait_ge(ldc, 96)
                for r in range(2):
                    mm = pe.matmul(pc[:, r, :], cf[:, P * r:P * r + P], uc[:], start=True, stop=True)
                mm.then_inc(cpe, 1)
                with pe.Fori(0, CB // 2, 1) as i:
                    for h in range(2):
                        pe.wait_ge(ld[h], 32 * (i + 1))
                        for g in range(4):
                            pe.wait_ge(VS.sem, VS.at(i * 2 + (h - 1), f"y{g}"))
                            for n in range(8):
                                mm = pe.matmul(py[:, g, K1 * n:K1 * n + K1], q[:, h, 8 * g + n, :], f2[:],
                                               start=True, stop=True)
                            mm.then_inc(*PS.inc(f"y{g}"))
                pe.wait_ge(cdv, 6)
                for i in range(CB):
                    for r in range(2):
                        mm = pe.matmul(pc[:, 2, P * i:P * i + P], pr[:, r, P * i:P * i + P], ci[:, P * r:P * r + P],
                                       start=(r == 0), stop=(r == 1))
                mm.then_inc(cpe, 1)

            @block.vector
            def _(v):
                VS.give(v)
                v.wait_ge(cpe, 1)
                v.wait_ge(ldc, 96)
                for n, (r, k) in enumerate(((0, 0), (1, 1), (0, 1), (1, 0))):
                    v.tensor_tensor(pr[:, n, :], pc[:, r, :], kc[:, k, :], ALU.mult).then_inc(cdv, 1)
                v.wait_ge(cdv, 4)
                v.tensor_tensor(pr[:, 0, :], pr[:, 0, :], pr[:, 1, :], ALU.subtract).then_inc(cdv, 1)
                v.wait_ge(cdv, 5)
                v.tensor_tensor(pr[:, 1, :], pr[:, 2, :], pr[:, 3, :], ALU.add).then_inc(cdv, 1)
                with v.Fori(0, CB // 2, 1) as i:
                    for h in range(2):
                        by_n2 = lambda a: a.rearrange("p (a b) -> p b a", b=N2)
                        v.wait_ge(ld[h], 32 * (i + 1))
                        v.wait_ge(st[h], 16 * i + HAD)
                        for g in range(4):
                            v.wait_ge(PS.sem, PS.at(i * 2 + h, f"y{g}"))
                            v.tensor_tensor(by_n2(y[:, h, :])[:, 8 * g:8 * g + 8, :],
                                            py[:, g, :].rearrange("p (b a) -> p b a", a=K1),
                                            by_n2(x2[:, h, :])[:, 8 * g:8 * g + 8, :], ALU.mult)\
                             .then_inc(*VS.inc(f"y{g}"))
                v.wait_ge(cpe, 2)
                v.tensor_tensor(yc[:], pc[:, 2, :].rearrange("p (i c) -> p i c", c=P), xc[:], ALU.mult).then_inc(cdv, 1)


def phase_retention(nc, d, s):
    SL = 4
    LOOP = 12
    with ExitStack() as ctx:
        sb, pb, sem, counted = makers(nc, ctx, s, "retention")
        qkT = sb("qkT5", [P, SL, 2, 512])
        vv = sb("v5", [P, SL, 512])
        gs = sb("gs5", [P, SL, 512])
        sf = sb("sf5", [P, SL, 512])
        kvb = sb("kvb5", [P, SL, 512])
        back_state = sb("back_state", [P, 2, 512])
        dist = sb("dist", [P, 4, P])
        mask = sb("mask", [P, HEADS, P])
        xi = sb("xi", [P, 2, HEADS, P])
        pT = sb("pT", [P, 2, 512])
        qx = sb("qx", [P, 2, 2, 512])
        raw = sb("raw5", [P, 8])
        lg = sb("lg5", [P, 8])
        dec = sb("dec5", [P, 8])
        tmp = sb("tmp5", [P, 5, 8])
        eps = sb("eps5", [P, 1])
        spare = sb("spare", [P, 1])
        stats = sb("stats", [P, 2, HEADS, 6])
        mv = sb("mv", [P, 2, HEADS, 2])
        rstd = sb("rstd5", [P, 2, HEADS])
        on = sb("on", [P, 2, 512])
        y = sb("y5", [P, 2, 512])
        yT = sb("yT", [P, 2, CB, P])
        pS = pb("pS", [P, 2, 512])
        pO = pb("pO", [P, 2, 512])
        pY = pb("pY", [P, 2, 512])
        ldc = sem("ld_c5")
        ld = [sem(f"ld_chunk{m}") for m in range(SL)]
        st = [sem(f"st_yret{h}") for h in range(2)]
        ca, cv, cs = sem("decay_act5"), sem("decay_dve5"), sem("consts5")
        PF = counted("pe_scores", ["s"])
        PO = counted("pe_o", ["o"])
        PY = counted("pe_yT", ["yT"])
        VF = counted("dve_mask", ["p"])
        VB = counted("dve_norm", [f"st{e}" for e in range(HEADS)] + ["spare"] + [f"mv{e}" for e in range(HEADS)] +
                   ["rstd"] + [f"n{e}" for e in range(HEADS)] + ["y"])
        GF = counted("pool_q", ["qf", "qb"])
        GB = counted("pool_state", ["decay", "sum"])
        AB = counted("act_std", ["std"])
        AY = counted("act_yT", ["yT"])
        ROUNDS = NLAT + 1

        def chunk(r):
            return NLAT if isinstance(r, int) and r == NLAT else r * -1 + (NLAT - 1)

        def in_loop(eng, body):
            with eng.Fori(0, LOOP // SL, 1) as i:
                for m in range(SL):
                    body(i * SL + m, m, i)
            for r in range(LOOP, ROUNDS):
                body(r, r % SL, r // SL)

        with nc.Block() as block:
            @block.sync
            def _(sp):
                had(sp, st)
                sp.dma_start(raw[:], d["ret_decay"].partition_broadcast(P)).then_inc(ldc, 16)
                sp.dma_start(dist[:].rearrange("p a b -> p (a b)"), d["dist"]).then_inc(ldc, 16)
                sp.dma_start(back_state[:, 0, :], d["state_b"]).then_inc(ldc, 16)

                def load(r, m, k):
                    t = chunk(r)
                    context = isinstance(r, int) and r == NLAT
                    if not (isinstance(r, int) and r < SL):
                        sp.wait_ge(PO.sem, PO.at(r - SL, "o"))
                        sp.wait_ge(VB.sem, VB.at(r - SL, "y"))
                        sp.wait_ge(GB.sem, GB.at(r - SL, "sum"))
                    sp.dma_start(qkT[:, m].rearrange("p a b -> p (a b)"), d["qkT"][take(t, 1)]).then_inc(ld[m], 16)
                    sp.dma_start(vv[:, m], d["v"][take(t, 1)]).then_inc(ld[m], 16)
                    sp.dma_start(gs[:, m], d["gs"][take(t, 1)]).then_inc(ld[m], 16)
                    if not context:
                        sp.dma_start(sf[:, m], d["state"][take(t, 1)]).then_inc(ld[m], 16)
                        sp.dma_start(kvb[:, m], d["kvb"][take(t, 1)]).then_inc(ld[m], 16)

                for r in range(SL):
                    load(r, r, 0)
                with sp.Fori(1, LOOP // SL + 1, 1) as i:
                    for m in range(SL):
                        load(i * SL + m, m, i)
                load(NLAT, 0, NLAT // SL)
                for h in range(2):
                    sp.wait_ge(st[h], 16 * ((ROUNDS + 1 - h) // 2) + HAD)
                retire(sp, s)

            @block.tensor
            def _(pe):
                PF.give(pe)
                PO.give(pe)
                PY.give(pe)
                pe.wait_ge(ldc, 48)

                def scores(r, m, k):
                    context = isinstance(r, int) and r == NLAT
                    pe.wait_ge(ld[m], 80 * k + (48 if context else 80))
                    pe.wait_ge(VF.sem, VF.at(r - 2, "p"))
                    for e in range(HEADS):
                        cut = slice(P * e, P * e + P)
                        mm = pe.matmul(pS[:, m % 2, cut], qkT[:, m, 1, cut], qkT[:, m, 0, cut], start=True, stop=True)
                    mm.then_inc(*PF.inc("s"))

                def outputs(r, m):
                    context = isinstance(r, int) and r == NLAT
                    h = m % 2
                    pe.wait_ge(VF.sem, VF.at(r, "p"))
                    pe.wait_ge(GF.sem, GF.at(r, "qb"))
                    pe.wait_ge(VB.sem, VB.at(r - 2, "n3"))
                    if not context:
                        pe.wait_ge(GB.sem, GB.at(r - 1, "sum"))
                    for e in range(HEADS):
                        cut = slice(P * e, P * e + P)
                        mm = pe.matmul(pO[:, h, cut], pT[:, h, cut], vv[:, m, cut], start=True, stop=context)
                        if not context:
                            pe.matmul(pO[:, h, cut], qx[:, h, 0, cut], sf[:, m, cut], start=False, stop=False)
                            mm = pe.matmul(pO[:, h, cut], qx[:, h, 1, cut], back_state[:, h, cut],
                                           start=False, stop=True)
                    mm.then_inc(*PO.inc("o"))

                def turn(r, h):
                    pe.wait_ge(VB.sem, VB.at(r, "y"))
                    pe.wait_ge(AY.sem, AY.at(r - 2, "yT"))
                    for e in range(HEADS):
                        cut = slice(P * e, P * e + P)
                        mm = pe.transpose(pY[:, h, cut], y[:, h, cut], s["ident"][:])
                    mm.then_inc(*PY.inc("yT"))

                scores(0, 0, 0)
                scores(1, 1, 0)
                outputs(0, 0)
                with pe.Fori(0, LOOP // SL, 1) as i:
                    for m in range(SL):
                        r, slot = i * SL + (m + 1), (m + 1) % SL
                        scores(i * SL + (m + 2), (m + 2) % SL, i + (m + 2) // SL)
                        outputs(r, slot)
                        turn(i * SL + m, m % 2)
                for r in range(LOOP + 1, ROUNDS):
                    if r + 1 < ROUNDS:
                        scores(r + 1, (r + 1) % SL, (r + 1) // SL)
                    outputs(r, r % SL)
                    turn(r - 1, (r - 1) % 2)
                turn(ROUNDS - 1, (ROUNDS - 1) % 2)

            @block.scalar
            def _(act):
                AB.give(act)
                AY.give(act)
                log_decays_scalar(act, tmp, ca, cv)
                act.wait_ge(cv, 9)
                act.wait_ge(ldc, 48)
                act.activation(dec[:], lg[:], ACT.Exp, scale=float(P)).then_inc(cs, 1)
                for n in range(2):
                    for e in range(HEADS):
                        act.activation(xi[:, n, e, :], dist[:, 2 + n, :], ACT.Exp,
                                       scale=lg[:, 4 * n + e:4 * n + e + 1]).then_inc(cs, 1)
                act.wait_ge(cv, 17)
                act.activation(mask[:], mask[:], ACT.Exp).then_inc(ca, 1)
                act.wait_ge(cv, 19)

                def body(r, m, k):
                    h = m % 2
                    act.wait_ge(VB.sem, VB.at(r, "mv3"))
                    act.activation(rstd[:, h, :], mv[:, h, :, 1], ACT.Sqrt, bias=eps[:]).then_inc(*AB.inc("std"))

                def copy(r, m, k, stored):
                    h = m % 2
                    act.wait_ge(PY.sem, PY.at(r, "yT"))
                    act.wait_ge(st[h], stored + HAD)
                    act.activation(yT[:, h].rearrange("p a b -> p (a b)"), pY[:, h, :], ACT.Copy)\
                       .then_inc(*AY.inc("yT"))
                    act.wait_ge(AY.sem, AY.at(r, "yT"))
                    act.dma_start(d["yret"][:, :, take(chunk(r) * P, P)], yT[:, h]).then_inc(st[h], 16)

                body(0, 0, 0)
                with act.Fori(0, LOOP // SL, 1) as i:
                    for m in range(SL):
                        body(i * SL + (m + 1), (m + 1) % SL, i)
                        copy(i * SL + m, m, i, 16 * (i * 2 + m // 2))
                for r in range(LOOP + 1, ROUNDS + 1):
                    if r < ROUNDS:
                        body(r, r % SL, 0)
                    copy(r - 1, (r - 1) % SL, 0, 16 * ((r - 1) // 2))

            @block.vector
            def _(v):
                VF.give(v)
                VB.give(v)
                v.wait_ge(ldc, 48)
                log_decays_vector(v, lg, raw, tmp, ca, cv)
                v.wait_ge(cv, 9)
                for e in range(HEADS):
                    v.tensor_scalar(mask[:, e, :], dist[:, 0, :], lg[:, e:e + 1], None, ALU.mult).then_inc(cv, 1)
                v.wait_ge(cv, 13)
                for e in range(HEADS):
                    v.scalar_tensor_tensor(mask[:, e, :], dist[:, 1, :], lg[:, 4 + e:5 + e], mask[:, e, :],
                                           ALU.mult, ALU.add).then_inc(cv, 1)
                v.wait_ge(ca, 3)
                v.tensor_tensor(mask[:], mask[:], s["ident"][:].unsqueeze(1).broadcast_to([P, HEADS, P]), ALU.add)\
                 .then_inc(cv, 1)
                v.memset(eps[:], EPS).then_inc(cv, 1)
                v.wait_ge(cv, 19)

                def masked(r, h):
                    v.wait_ge(PF.sem, PF.at(r, "s"))
                    v.wait_ge(PO.sem, PO.at(r - 2, "o"))
                    v.tensor_tensor(pT[:, h, :], pS[:, h, :], mask[:].rearrange("p e c -> p (e c)"), ALU.mult)\
                     .then_inc(*VF.inc("p"))

                def norm(r, m):
                    h = m % 2
                    v.wait_ge(PO.sem, PO.at(r, "o"))
                    v.wait_ge(PY.sem, PY.at(r - 2, "yT"))
                    for e in range(HEADS):
                        v.bn_stats(stats[:, h, e, :], pO[:, h, P * e:P * e + P]).then_inc(*VB.inc(f"st{e}"))
                    v.wait_ge(VB.sem, VB.at(r, "st3"))
                    v.memset(spare[:], 0.0).then_inc(*VB.inc("spare"))
                    for e in range(HEADS):
                        v.bn_aggr(mv[:, h, e, :], stats[:, h, e, :]).then_inc(*VB.inc(f"mv{e}"))
                    v.wait_ge(AB.sem, AB.at(r, "std"))
                    v.reciprocal(rstd[:, h, :], rstd[:, h, :]).then_inc(*VB.inc("rstd"))
                    v.wait_ge(VB.sem, VB.at(r, "rstd"))
                    for e in range(HEADS):
                        cut = slice(P * e, P * e + P)
                        v.tensor_scalar(on[:, h, cut], pO[:, h, cut], mv[:, h, e, 0:1], rstd[:, h, e:e + 1],
                                        ALU.subtract, ALU.mult).then_inc(*VB.inc(f"n{e}"))
                    v.wait_ge(VB.sem, VB.at(r, "n3"))
                    v.tensor_tensor(y[:, h, :], on[:, h, :], gs[:, m, :], ALU.mult).then_inc(*VB.inc("y"))

                masked(0, 0)
                with v.Fori(0, LOOP // SL, 1) as i:
                    for m in range(SL):
                        masked(i * SL + (m + 1), (m + 1) % 2)
                        norm(i * SL + m, m)
                for r in range(LOOP, ROUNDS):
                    if r + 1 < ROUNDS:
                        masked(r + 1, (r + 1) % 2)
                    norm(r, r % SL)

            @block.gpsimd
            def _(g):
                GF.give(g)
                GB.give(g)
                g.wait_ge(cs, 9)
                g.wait_ge(ldc, 48)

                def front(r, m, k):
                    h = m % 2
                    context = isinstance(r, int) and r == NLAT
                    g.wait_ge(ld[m], 80 * k + (48 if context else 80))
                    g.wait_ge(PO.sem, PO.at(r - 2, "o"))
                    for n, name in enumerate(("qf", "qb")):
                        g.tensor_tensor(qx[:, h, n, :], qkT[:, m, 0, :], xi[:, n].rearrange("p e c -> p (e c)"),
                                        ALU.mult).then_inc(*GF.inc(name))

                def state(r, m, k):
                    h = m % 2
                    g.wait_ge(GB.sem, GB.at(r - 1, "sum"))
                    g.wait_ge(PO.sem, PO.at(r - 1, "o"))
                    heads = lambda a: a.rearrange("p (e c) -> p e c", e=HEADS)
                    g.tensor_tensor(heads(back_state[:, 1 - h, :]), heads(back_state[:, h, :]),
                                    dec[:, 4:8].unsqueeze(2).broadcast_to([P, HEADS, P]), ALU.mult)\
                     .then_inc(*GB.inc("decay"))
                    g.wait_ge(GB.sem, GB.at(r, "decay"))
                    g.tensor_tensor(back_state[:, 1 - h, :], back_state[:, 1 - h, :], kvb[:, m, :], ALU.add)\
                     .then_inc(*GB.inc("sum"))

                front(0, 0, 0)
                with g.Fori(0, LOOP // SL, 1) as i:
                    for m in range(SL):
                        front(i * SL + (m + 1), (m + 1) % SL, i + (m + 1) // SL)
                        state(i * SL + m, m, i)
                for r in range(LOOP, NLAT):
                    front(r + 1, (r + 1) % SL, (r + 1) // SL)
                    state(r, r % SL, r // SL)


def phase_merge(nc, d, s):
    HC = KT // 2
    ROUNDS = 2 * len(SPANS)
    with ExitStack() as ctx:
        sb, pb, sem, counted = makers(nc, ctx, s, "merge")
        raw = sb("w_gates", [P, KT, 2, P])
        wh = sb("w_gates_high", [P, HC, KT, 2, P], F32R)
        wl = sb("w_gates_low", [P, HC, KT, 2, P], F32R)
        wy = sb("w_y", [P, HC, 2, CB, P])
        hT = sb("hT6", [P, KT, 512])
        hh = sb("hT_high", [P, KT, 512], F32R)
        hl = sb("hT_low", [P, KT, 512], F32R)
        y = sb("y6", [P, 2, 2, CB, 512])
        yc = sb("y_context", [P, 2, CB, CTX])
        gate = sb("gate", [P, 2, 2, 512])
        part = sb("part", [P, 2, 512])
        m = sb("m6", [P, 2, 512])
        pg = pb("pg", [P, 2, 2, 512])
        py = pb("py6", [P, 2, 2, 512])
        gld = sem("ld_gates")
        wld = [sem(f"ld_wy{c}") for c in range(HC)]
        hld = sem("ld_hT")
        yld = [sem(f"ld_y{h}") for h in range(2)] + [sem("ld_yc")]
        st = [sem(f"st_m{h}") for h in range(2)]
        w_act, w_dve = sem("w_high_ready"), sem("w_split")
        names = ("gh", "gr", "yh", "yr")
        PS = counted("pe_merge", [f"{n}{c}" for c in range(HC) for n in names])
        AH = counted("act_split", [f"h{q}" for q in range(KT)])
        VH = counted("dve_split", [f"h{q}" for q in range(KT)])
        AS = counted("act_merge", [f"{n}{c}" for c in range(HC) for n in names[:2]])
        VS = counted("dve_merge", [f"{n}{c}" for c in range(HC) for n in ("a", "b", "m")])

        def last(steps, r, name, c):
            return steps.at(r, f"{name}{c - 2}") if c >= 2 else steps.at(r - 1, f"{name}{c + HC - 2}")

        def rounds(eng, body):
            for half in range(2):
                with eng.Fori(0, 2, 1) as i:
                    for h in range(2):
                        body(i * 2 + (5 * half + h), half, h, i, 512)
                body(5 * half + 4, half, 2, 0, CTX)

        with nc.Block() as block:
            @block.sync
            def _(sp):
                had(sp, st)

                def load_hT(r):
                    at, n = SPANS[r % 5]
                    if r:
                        sp.wait_ge(VH.sem, VH.at(r - 1, f"h{KT - 1}"))
                    sp.dma_start(hT[:, :, 0:n], d["hT"][:, :, at:at + n]).then_inc(hld, 16)

                def load_y(b):
                    at, n = SPANS[b]
                    for j, src in enumerate(("yhy", "yret")):
                        sp.dma_start(yc[:, j] if b == 4 else y[:, b % 2, j], d[src][:, :, at:at + n])\
                          .then_inc(yld[2 if b == 4 else b % 2], 16)

                def gate_columns(c):
                    if c:
                        sp.wait_ge(w_dve, c)
                    for j in range(2):
                        sp.dma_start(raw[:, :, j, :], d["w_gates"][:, :, DM * j + P * c:DM * j + P * c + P])\
                          .then_inc(gld, 16)

                def projections(c):
                    if c >= HC:
                        sp.wait_ge(PS.sem, PS.at(4, f"yr{c - HC}"))
                    for j, src in enumerate(("w_hy_o", "w_ret_o")):
                        sp.dma_start(wy[:, c % HC, j], d[src][:, :, P * c:P * c + P]).then_inc(wld[c % HC], 16)

                load_hT(0)
                gate_columns(0)
                projections(0)
                load_y(0)
                for c in range(1, HC):
                    gate_columns(c)
                    projections(c)
                load_y(1)
                load_y(4)
                for r in range(ROUNDS):
                    half, b = r // 5, r % 5
                    at, n = SPANS[b]
                    if r + 1 < ROUNDS:
                        load_hT(r + 1)
                    for c in range(HC):
                        if r == 4:
                            if c + 1 < HC:
                                gate_columns(HC + c + 1)
                            projections(HC + c)
                        sp.wait_ge(VS.sem, VS.at(r, f"m{c}"))
                        sp.dma_start(d["merged"][:, HC * half + c, at:at + n], m[:, c % 2, 0:n]).then_inc(st[c % 2], 16)
                    if b < 4 and not (half == 1 and b > 1):
                        load_y((b + 2) % 4)
                    if r == 3:
                        gate_columns(HC)
                for h in range(2):
                    sp.wait_ge(st[h], 16 * ROUNDS * HC // 2 + HAD)
                retire(sp, s)

            @block.tensor
            def _(pe):
                PS.give(pe)

                def body(r, half, h, k, n):
                    for c in range(HC):
                        p = c % 2
                        pe.wait_ge(w_dve, HC * half + c + 1)
                        for j in range(2):
                            name = names[j]
                            pe.wait_ge(AS.sem, last(AS, r, name, c))
                            for q in range(KT):
                                if c == 0 and j == 0:
                                    pe.wait_ge(VH.sem, VH.at(r, f"h{q}"))
                                mm = product(pe, pg[:, p, j, 0:n], (wh[:, c, q, j, :], wl[:, c, q, j, :]),
                                             (hh[:, q, 0:n], hl[:, q, 0:n]), q == 0, q == KT - 1)
                            mm.then_inc(*PS.inc(f"{name}{c}"))
                        pe.wait_ge(wld[c], 32 * (half + 1))
                        if c == 0:
                            pe.wait_ge(yld[h], k * 32 + (64 * half + 32) if h < 2 else 32)
                        for j in range(2):
                            pe.wait_ge(VS.sem, last(VS, r, "ab"[j], c))
                            for q in range(CB):
                                mm = pe.matmul(py[:, p, j, 0:n], wy[:, c, j, q, :], yc[:, j, q, :] if h == 2 else y[:, h, j, q, :],
                                               start=(q == 0), stop=(q == CB - 1))
                            mm.then_inc(*PS.inc(f"{names[2 + j]}{c}"))

                rounds(pe, body)

            @block.scalar
            def _(act):
                AS.give(act)
                AH.give(act)

                def split_rows(r, n):
                    act.wait_ge(hld, r * 16 + 16)
                    act.wait_ge(PS.sem, PS.at(r - 1, f"gr{HC - 1}"))
                    for q in range(KT):
                        act.activation(hh[:, q, 0:n], hT[:, q, 0:n], ACT.Copy).then_inc(*AH.inc(f"h{q}"))

                def split_weights(c):
                    act.wait_ge(gld, 32 * (c + 1))
                    act.activation(wh[:, c % HC].rearrange("p a b c -> p (a b c)"), raw[:].rearrange("p a b c -> p (a b c)"),
                                   ACT.Copy).then_inc(w_act, 1)

                def body(r, half, h, k, n):
                    for c in range(HC):
                        for j in range(2):
                            act.wait_ge(VS.sem, last(VS, r, "ab"[j], c))
                            act.wait_ge(PS.sem, PS.at(r, f"{names[j]}{c}"))
                            act.activation(gate[:, c % 2, j, 0:n], pg[:, c % 2, j, 0:n], ACT.Sigmoid)\
                               .then_inc(*AS.inc(f"{names[j]}{c}"))
                        if half == 0 and h == 2 and c + 1 < HC:
                            split_weights(HC + c)
                    if not (half == 1 and h == 2):
                        split_rows(r + 1, 512)
                    if half == 0 and h == 2:
                        split_weights(KT - 1)

                split_rows(0, 512)
                for c in range(HC):
                    split_weights(c)
                rounds(act, body)

            @block.vector
            def _(v):
                VS.give(v)
                VH.give(v)

                def split_rows(r):
                    v.wait_ge(PS.sem, PS.at(r - 1, f"gr{HC - 1}"))
                    for q in range(KT):
                        v.wait_ge(AH.sem, AH.at(r, f"h{q}"))
                        v.tensor_tensor(hl[:, q, :], hT[:, q, :], hh[:, q, :].bitcast(F32), ALU.subtract)\
                         .then_inc(*VH.inc(f"h{q}"))

                def split_weights(c):
                    v.wait_ge(w_act, c + 1)
                    flat = lambda a: a.rearrange("p a b c -> p (a b c)")
                    v.tensor_tensor(flat(wl[:, c % HC]), flat(raw[:]), flat(wh[:, c % HC]).bitcast(F32), ALU.subtract)\
                     .then_inc(w_dve, 1)

                def body(r, half, h, k, n):
                    for c in range(HC):
                        p = c % 2
                        if half == 0 and h == 2 and c + 1 < HC:
                            split_weights(HC + c)
                        if c == HC - 1 and not (half == 1 and h == 2):
                            split_rows(r + 1)
                        if c == HC - 1 and half == 0 and h == 2:
                            split_weights(KT - 1)
                        v.wait_ge(AS.sem, AS.at(r, f"gh{c}"))
                        v.wait_ge(PS.sem, PS.at(r, f"yh{c}"))
                        v.wait_ge(st[p], r * 32 + (16 * (c // 2) + HAD))
                        v.tensor_tensor(m[:, p, 0:n], py[:, p, 0, 0:n], gate[:, p, 0, 0:n], ALU.mult)\
                         .then_inc(*VS.inc(f"a{c}"))
                        v.wait_ge(AS.sem, AS.at(r, f"gr{c}"))
                        v.wait_ge(PS.sem, PS.at(r, f"yr{c}"))
                        v.tensor_tensor(part[:, p, 0:n], py[:, p, 1, 0:n], gate[:, p, 1, 0:n], ALU.mult)\
                         .then_inc(*VS.inc(f"b{c}"))
                        v.wait_ge(VS.sem, VS.at(r, f"b{c}"))
                        v.tensor_tensor(m[:, p, 0:n], m[:, p, 0:n], part[:, p, 0:n], ALU.add)\
                         .then_inc(*VS.inc(f"m{c}"))

                split_rows(0)
                for c in range(HC):
                    split_weights(c)
                rounds(v, body)


ROW = DM + NE


def phase_out(nc, d, s):
    LOOP = NLAT - 2
    with ExitStack() as ctx:
        sb, pb, sem, counted = makers(nc, ctx, s, "out")
        wh = sb("w_out_high", [P, KT, DM], F32R)
        wl = sb("w_out_low", [P, KT, DM], F32R)
        w = sb("w_out", [P, KT, DM])
        wr = sb("w_router", [P, KT, NE])
        gate = sb("gate1", [P, 2, DM])
        scale = sb("scale2", [P, 2, DM])
        shift = sb("shift2", [P, 2, DM])
        gn = sb("gn2", [P, DM])
        mh = sb("mT_high", [P, 2, KT, P], F32R)
        ml = sb("mT_low", [P, 2, KT, P], F32R)
        mT = sb("mT", [P, 2, KT, P])
        x = sb("x6", [P, 2, DM])
        t1 = sb("t1", [P, DM])
        junk = sb("junk6", [P, DM])
        row = sb("row", [P, 2, ROW])
        hT = sb("h2T", [P, 2, KT, P])
        ssq = sb("ssq6", [P, 2])
        eps = sb("eps6", [P, 1])
        mx = sb("mx", [P, 2])
        ex = sb("ex", [P, 2, NE])
        sm = sb("sm", [P, 2])
        po = pb("po", [P, 2, DM])
        tp = pb("tp6", [P, DM])
        pr = pb("pr", [P, NE])
        ldw = sem("ld_w6")
        PIECES = [(512 * j, k) for j in range(2) for k in range(0, KT, 2)]
        wld = [sem(f"ld_wout{j}") for j in range(len(PIECES))]
        w_act, w_dve = sem("w_high_ready"), sem("w_split")
        mld = [sem(f"ld_m{h}") for h in range(2)]
        ld = [sem(f"ld_t{h}") for h in range(2)]
        xst = [sem(f"st_x{h}") for h in range(2)]
        rst = [sem(f"st_row{h}") for h in range(2)]
        cv = sem("consts6")
        PF = counted("pe_proj", ["o"])
        PB, PR = counted("pe_turn", ["hT"]), counted("pe_router", ["r"])
        AF, VF = counted("act_m", ["high"]), counted("dve_m", ["low"])
        AB, AR = counted("act_rows", ["sq", "std", "hT"]), counted("act_router", ["ex"])
        VB = counted("dve_rows", ["t1", "x", "rstd", "h2a", "h2", "hT"])
        VR = counted("dve_router", ["mx", "rs", "aff", "row"])

        with nc.Block() as block:
            @block.sync
            def _(sp):
                had(sp, xst, rst)
                def load(t, h, at):
                    sp.wait_ge(VF.sem, VF.at(t - 2, "low"))
                    sp.dma_start(mT[:, h], d["merged"][:, :, take(at, P)]).then_inc(mld[h], 16)

                def load_x(t, h, k):
                    sp.wait_ge(VB.sem, VB.at(t - 2, "h2a"))
                    sp.wait_ge(xst[h], 16 * k + HAD)
                    sp.dma_start(x[:, h, :], d["xs"][take(t, 1)]).then_inc(ld[h], 16)

                def stores(t, h, k, more):
                    at, ahead = (t * P, (t + 2) * P) if isinstance(t, int) else (sp.snap(t * P), sp.snap((t + 2) * P))
                    if more:
                        load(t + 2, h, ahead)
                    sp.wait_ge(VB.sem, VB.at(t, "x"))
                    sp.dma_start(d["xacc"][take(at, P), :], x[:, h, :]).then_inc(xst[h], 16)
                    if more:
                        load_x(t + 2, h, k + 1)

                def store_row(t, h):
                    at = t * P if isinstance(t, int) else sp.snap(t * P)
                    sp.wait_ge(VR.sem, VR.at(t, "row"))
                    sp.dma_start(d["h2"][take(at, P), :], row[:, h, :]).then_inc(rst[h], 16)

                load(0, 0, 0)
                for j, (c, k) in enumerate(PIECES):
                    sp.dma_start(w[:, k:k + 2, c:c + 512], d["w_out"][:, k:k + 2, c:c + 512]).then_inc(wld[j], 16)
                load(1, 1, P)
                sp.dma_start(wr[:], d["w_router"]).then_inc(ldw, 16)
                sp.dma_start(gn[:], d["norm2_g"].partition_broadcast(P)).then_inc(ldw, 16)
                for n in range(2):
                    for dst, col in ((gate, 2), (shift, 3), (scale, 4)):
                        sp.dma_start(dst[:, n, :], d["mod"][n:n + 1, DM * col:DM * col + DM].partition_broadcast(P))\
                          .then_inc(ldw, 16)
                load_x(0, 0, 0)
                load_x(1, 1, 0)
                stores(0, 0, 0, True)
                with sp.Fori(0, LOOP // 2, 1) as i:
                    for h in range(2):
                        stores(i * 2 + (h + 1), 1 - h, i + h, True)
                        store_row(i * 2 + h, h)
                for t in range(LOOP + 1, NT + 1):
                    if t < NT:
                        stores(t, t % 2, t // 2, t + 2 < NT)
                    store_row(t - 1, (t - 1) % 2)
                for h in range(2):
                    sp.wait_ge(xst[h], 16 * ((NT + 1 - h) // 2) + HAD)
                    sp.wait_ge(rst[h], 16 * ((NT + 1 - h) // 2) + HAD)
                retire(sp, s)

            @block.tensor
            def _(pe):
                PF.give(pe)
                PB.give(pe)
                PR.give(pe)

                def front(t, h, k):
                    pe.wait_ge(AF.sem, AF.at(t, "high"))
                    pe.wait_ge(VF.sem, VF.at(t, "low"))
                    pe.wait_ge(VB.sem, VB.at(t - 2, "t1"))
                    for j in range(2):
                        cols = slice(512 * j, 512 * j + 512)
                        for q in range(KT):
                            if q % 2 == 0:
                                pe.wait_ge(w_dve, 4 * j + q // 2 + 1)
                            mm = product(pe, po[:, h, cols], (mh[:, h, q, :], ml[:, h, q, :]), (wh[:, q, cols], wl[:, q, cols]),
                                         q == 0, q == KT - 1)
                    mm.then_inc(*PF.inc("o"))

                def turn(t, h):
                    pe.wait_ge(VB.sem, VB.at(t, "h2"))
                    pe.wait_ge(AB.sem, AB.at(t - 1, "hT"))
                    pe.wait_ge(VB.sem, VB.at(t - 1, "hT"))
                    for q in range(KT):
                        mm = pe.transpose(tp[:, P * q:P * q + P], row[:, h, P * q:P * q + P], s["ident"][:])
                    mm.then_inc(*PB.inc("hT"))

                def router(t, h):
                    pe.wait_ge(VB.sem, VB.at(t, "hT"))
                    pe.wait_ge(AB.sem, AB.at(t, "hT"))
                    pe.wait_ge(AR.sem, AR.at(t - 1, "ex"))
                    for q in range(KT):
                        mm = pe.matmul(pr[:], hT[:, h, q, :], wr[:, q, :], start=(q == 0), stop=(q == KT - 1))
                    mm.then_inc(*PR.inc("r"))

                front(0, 0, 0)
                pe.wait_ge(ldw, 16 * 8)
                front(1, 1, 0)
                turn(0, 0)
                with pe.Fori(0, LOOP // 2, 1) as i:
                    for h in range(2):
                        front(i * 2 + (h + 2), h, i + 1)
                        router(i * 2 + h, h)
                        turn(i * 2 + (h + 1), 1 - h)
                for t in range(LOOP, NT):
                    if t + 2 < NT:
                        front(t + 2, t % 2, (t + 2) // 2)
                    router(t, t % 2)
                    if t + 1 < NT:
                        turn(t + 1, (t + 1) % 2)

            @block.scalar
            def _(act):
                AB.give(act)
                AF.give(act)
                AR.give(act)
                act.wait_ge(cv, 1)

                def front(t, h, k):
                    act.wait_ge(mld[h], 16 * (k + 1))
                    act.wait_ge(PF.sem, PF.at(t - 2, "o"))
                    act.activation(mh[:, h].rearrange("p a b -> p (a b)"),
                                   mT[:, h].rearrange("p a b -> p (a b)"), ACT.Copy).then_inc(*AF.inc("high"))

                def back(t, h, k, more):
                    act.wait_ge(VB.sem, VB.at(t, "x"))
                    act.activation(junk[:], x[:, h, :], ACT.Square, scale=DM ** -0.5, accum_out=ssq[:, h:h + 1])\
                       .then_inc(*AB.inc("sq"))
                    act.wait_ge(AB.sem, AB.at(t, "sq"))
                    act.activation(ssq[:, h:h + 1], ssq[:, h:h + 1], ACT.Sqrt, bias=eps[:]).then_inc(*AB.inc("std"))
                    if more:
                        front(t + 2, h, k + 1)
                    act.wait_ge(PB.sem, PB.at(t, "hT"))
                    act.wait_ge(PR.sem, PR.at(t - 2, "r"))
                    act.activation(hT[:, h, 0:4].rearrange("p a b -> p (a b)"), tp[:, 0:512], ACT.Copy)\
                       .then_inc(*AB.inc("hT"))

                def router(t, h):
                    act.wait_ge(VR.sem, VR.at(t, "mx"))
                    act.activation(ex[:, h, :], pr[:], ACT.Exp, bias=mx[:, h:h + 1], accum_out=sm[:, h:h + 1])\
                       .then_inc(*AR.inc("ex"))

                front(0, 0, 0)
                for j, (c, k) in enumerate(PIECES):
                    act.wait_ge(wld[j], 16)
                    act.activation(wh[:, k:k + 2, c:c + 512], w[:, k:k + 2, c:c + 512], ACT.Copy).then_inc(w_act, 1)
                front(1, 1, 0)
                back(0, 0, 0, True)
                with act.Fori(0, LOOP // 2, 1) as i:
                    for h in range(2):
                        back(i * 2 + (h + 1), 1 - h, i + h, True)
                        router(i * 2 + h, h)
                for t in range(LOOP + 1, NT + 1):
                    if t < NT:
                        back(t, t % 2, t // 2, t + 2 < NT)
                    router(t - 1, (t - 1) % 2)

            @block.vector
            def _(v):
                VB.give(v)
                v.memset(eps[:], EPS).then_inc(cv, 1)

                def front(t, h):
                    v.wait_ge(AF.sem, AF.at(t, "high"))
                    v.tensor_tensor(ml[:, h].rearrange("p a b -> p (a b)"), mT[:, h].rearrange("p a b -> p (a b)"), mh[:, h].rearrange("p a b -> p (a b)").bitcast(F32),
                                    ALU.subtract).then_inc(*VF.inc("low"))

                VF.give(v)
                VR.give(v)
                front(0, 0)
                for j, (c, k) in enumerate(PIECES):
                    v.wait_ge(w_act, j + 1)
                    v.tensor_tensor(wl[:, k:k + 2, c:c + 512], w[:, k:k + 2, c:c + 512],
                                    wh[:, k:k + 2, c:c + 512].bitcast(F32), ALU.subtract).then_inc(w_dve, 1)
                front(1, 1)
                v.wait_ge(ldw, 16 * 8)
                v.scalar_tensor_tensor(scale[:], scale[:], 1.0, gn[:].unsqueeze(1).broadcast_to([P, 2, DM]),
                                       ALU.add, ALU.mult).then_inc(cv, 1)
                v.wait_ge(cv, 2)

                def back(t, h, k, n, more):
                    v.wait_ge(PF.sem, PF.at(t, "o"))
                    v.tensor_tensor(t1[:], po[:, h, :], gate[:, n, :], ALU.mult).then_inc(*VB.inc("t1"))
                    v.wait_ge(ld[h], 16 * (k + 1))
                    v.wait_ge(VB.sem, VB.at(t, "t1"))
                    v.tensor_tensor(x[:, h, :], x[:, h, :], t1[:], ALU.add).then_inc(*VB.inc("x"))
                    v.wait_ge(AB.sem, AB.at(t, "std"))
                    v.reciprocal(ssq[:, h:h + 1], ssq[:, h:h + 1]).then_inc(*VB.inc("rstd"))
                    v.wait_ge(rst[h], 16 * k + HAD)
                    v.wait_ge(VB.sem, VB.at(t, "rstd"))
                    v.scalar_tensor_tensor(row[:, h, 0:DM], x[:, h, :], ssq[:, h:h + 1], scale[:, n, :],
                                           ALU.mult, ALU.mult).then_inc(*VB.inc("h2a"))
                    v.wait_ge(VB.sem, VB.at(t, "h2a"))
                    v.tensor_tensor(row[:, h, 0:DM], row[:, h, 0:DM], shift[:, n, :], ALU.add).then_inc(*VB.inc("h2"))
                    if more:
                        front(t + 2, h)
                    v.wait_ge(PB.sem, PB.at(t, "hT"))
                    v.wait_ge(PR.sem, PR.at(t - 2, "r"))
                    v.tensor_copy(hT[:, h, 4:8].rearrange("p a b -> p (a b)"), tp[:, 512:DM]).then_inc(*VB.inc("hT"))

                def router(t, h):
                    v.wait_ge(PR.sem, PR.at(t, "r"))
                    v.tensor_reduce(mx[:, h:h + 1], pr[:], AX.X, ALU.max, negate=True).then_inc(*VR.inc("mx"))
                    v.wait_ge(AR.sem, AR.at(t, "ex"))
                    v.reciprocal(sm[:, h:h + 1], sm[:, h:h + 1]).then_inc(*VR.inc("rs"))
                    v.wait_ge(VR.sem, VR.at(t, "rs"))
                    v.tensor_scalar(s["aff"][:, take(t, 1), :].squeeze(1) if isinstance(t, int) else
                                    s["aff"][:, take(t, 1), :], ex[:, h, :], sm[:, h:h + 1], None, ALU.mult)\
                     .then_inc(*VR.inc("aff"))
                    v.tensor_scalar(row[:, h, DM:ROW], ex[:, h, :], sm[:, h:h + 1], None, ALU.mult)\
                     .then_inc(*VR.inc("row"))

                back(0, 0, 0, 0, True)
                with v.Fori(0, LOOP // 2, 1) as i:
                    for h in range(2):
                        back(i * 2 + (h + 1), 1 - h, i + h, 0, True)
                        router(i * 2 + h, h)
                for t in range(LOOP + 1, NT + 1):
                    if t < NT:
                        back(t, t % 2, t // 2, int(t == NLAT), t + 2 < NT)
                    router(t - 1, (t - 1) % 2)


SLOTS = CAP + CCAP
GROUPS = [(0, P), (P, P), (CAP, CCAP)]
CTX_LO = CAP + 2 * CCAP
HID = CTX_LO + CCAP + CAP


def phase_experts(nc, d, s):
    BITS = 30
    with ExitStack() as ctx:
        sb, pb, sem, counted = makers(nc, ctx, s, "experts")
        wg = sb("wg", [P, 4, KT, 256])
        wu = sb("wu", [P, 4, KT, 256])
        wdh = sb("w_down_high", [P, 4, 2, DM], F32R)
        wdl = sb("w_down_low", [P, 4, 2, DM], F32R)
        raw = sb("w_down_row", [P, DM])
        caps = sb("caps", [P, 2])
        slot = sb("slot", [P, CAP])
        thr = sb("thr", [P, 2], I32)
        cand = sb("cand", [P, 2], I32)
        bit = sb("bit", [P, 2], I32)
        cnt = sb("cnt", [P, 2])
        met = sb("met", [P, 2], I32)
        need = sb("need", [P, 2])
        pos = sb("pos", [P, 3, P])
        ends = sb("ends", [P, 2])
        below = sb("below", [P, NLAT, CAP], BF16)
        below_c = sb("below_c", [P, CCAP], BF16)
        ones = sb("ones", [P, 1], BF16)
        ids = sb("ids", [P, 2, 3], I32)
        sids = sb("sids", [P, 2, 3], I32)
        vals = sb("vals", [P, 2, 3])
        xs = sb("xg", [P, 3, ROW])
        xT = sb("xT9", [P, KT, SLOTS])
        act_g = sb("act_g", [P, SLOTS])
        full = sb("full", [P, SLOTS])
        hid = sb("hid", [P, KT, HID], F32R)
        clow = sb("clow", [CCAP, 512])
        ye = sb("ye", [P, 3, DM])
        arr, prob, over, tie, scan = (ye[:].rearrange("p a b -> p (a b)")[:, 3 * P * n:3 * P * n + 3 * P]
                                      .rearrange("p (a b) -> p a b", b=P) for n in range(5))
        seg = ye[:].rearrange("p a b -> p (a b)")[:, 15 * P:17 * P]
        gate2 = sb("gate2", [P, 2, DM])
        pg = pb("pg9", [P, 2, 512])
        pu = pb("pu9", [P, 2, 512])
        px = pb("px9", [P, 2, 512])
        pi = pb("pi9", [P, 512])

        ldc = sem("ld_c9")
        gld = [sem(f"ld_g{j}") for j in range(4)]
        uld = [sem(f"ld_u{j}") for j in range(4)]
        rld = sem("ld_d")
        ga = sem("gather")
        sc = [sem(f"added{h}") for h in range(2)]
        pc = sem("pool_spare")
        CG, CP = counted("pool_gather", ["carry"]), counted("pool_add", ["before", "added"])
        spare = sb("spare9", [P, 4])
        R0 = counted("dve_arrange", ["zero", "a0", "a1", "ac", "prob", "thr", "bit"])
        RB = counted("dve_bits", ["cand", "cl", "cc", "met", "bit", "thr"])
        R1 = counted("dve_slots", ["gl", "gc", "need", "tl", "tc", "s0", "s1", "e0", "e1", "lim", "k0", "k1",
                                          "sel", "p0", "p1", "f0", "f1", "off", "q0", "q1", "pos", "ones"])
        QB = counted("pe_bits", ["sum"])
        Q1 = counted("pe_route", ["prob", "above", "ahead", "slots", "pos"])
        PG = counted("pe_gu", [f"{n}{f}" for f in range(KT) for n in "gu"])
        PI = counted("pe_ids", ["ids"])
        PX = counted("pe_xT", [f"x{k}" for k in range(KT)])
        PD = counted("pe_dn", [f"d{n}" for n in range(6)])
        AG = counted("act_g", [f"g{f}" for f in range(KT)])
        AX = counted("act_xT", [f"x{k}" for k in range(KT)])
        VG = counted("dve_hid", [f"{n}{f}" for f in range(KT) for n in "mlh"])
        AH = counted("act_hid", [f"h{f}" for f in range(KT)])
        AW, VW = counted("act_wd", [f"w{f}" for f in range(KT)]), counted("dve_wd", [f"w{f}" for f in range(KT)])
        AC, VC = counted("act_ctx", ["c0", "c1"]), counted("dve_ctx", ["sum0", "sum1"])
        empty = sem("empty")
        VM = counted("dve_below", [f"m{n}" for n in range(NLAT)] + ["mc"])
        VI = counted("dve_ids", ["i0", "i2"])
        VX = counted("dve_keep", ["s0", "s2", "v0", "v2"])
        VD = counted("dve_dn", [f"d{n}" for n in range(6)])
        LOOP = NE - 2

        def experts(eng, body):
            with eng.Fori(0, LOOP // 2, 1) as i:
                for h in range(2):
                    body(i * 2 + h, h, i, True, True)
            for e in range(LOOP, NE):
                body(e, e % 2, e // 2, e + 1 < NE, e + 2 < NE)

        with nc.Block() as block:
            @block.sync
            def _(sp):
                for dst, src in ((seg, d["seg"]), (caps[:], d["caps"]), (slot[:], d["slot"])):
                    sp.dma_start(dst, src).then_inc(ldc, 16)
                for n in range(2):
                    sp.dma_start(gate2[:, n, :], d["mod"][n:n + 1, 5 * DM:6 * DM].partition_broadcast(P)).then_inc(ldc, 16)

                def load_gate(e, j):
                    sp.dma_start(wg[:, j], d["w_gate"][take(e, 1), j]).then_inc(gld[j], 16)

                def load_up(e, j):
                    sp.dma_start(wu[:, j], d["w_up"][take(e, 1), j]).then_inc(uld[j], 16)

                follow = {2: (load_gate, 0), 3: (load_up, 0), 4: (load_gate, 1), 5: (load_up, 1)}

                def loads(e, more):
                    for f in range(KT):
                        sp.wait_ge(VW.sem, VW.at(e, f"w{f - 1}") if f else VW.at(e - 1, f"w{KT - 1}"))
                        sp.dma_start(raw[:].unsqueeze(1), d["w_down"][take(e, 1), f // 2, :, f % 2, :].rearrange("e p c -> p e c"))\
                          .then_inc(rld, 16)
                        if more and f in follow:
                            load, j = follow[f]
                            sp.wait_ge(PG.sem, PG.at(e, f"u{2 * j + 1}"))
                            load(e + 1, j)
                    if more:
                        for j in range(4):
                            for load in (load_gate, load_up):
                                if (load, j) not in follow.values():
                                    sp.wait_ge(PG.sem, PG.at(e, f"u{2 * j + 1}"))
                                    load(e + 1, j)

                sp.wait_ge(ldc, 80)
                for j in range(4):
                    load_gate(0, j)
                    load_up(0, j)
                with sp.Fori(0, NE - 1, 1) as e:
                    loads(e, True)
                loads(NE - 1, False)
                sp.wait_ge(VW.sem, VW.at(NE - 1, f"w{KT - 1}"))
                retire(sp, s)

            @block.tensor
            def _(pe):
                for steps in (PG, PI, PX, PD):
                    steps.give(pe)
                for steps in (QB, Q1):
                    steps.give(pe)
                pe.wait_ge(R0.sem, R0.at(0, "ac"))
                for n in range(3):
                    mm = pe.transpose(px[:, 0, P * n:P * n + P], arr[:, n, :], s["ident"][:])
                mm.then_inc(*Q1.inc("prob"))
                pe.wait_ge(ldc, 80)
                with pe.Fori(0, BITS, 1) as i:
                    pe.wait_ge(RB.sem, RB.at(i, "cc"))
                    pe.matmul(pi[:, 0:2], seg[:, 0:P], cnt[:], start=True, stop=True).then_inc(*QB.inc("sum"))
                for name, ready, half, src in (("above", "gc", 0, cnt), ("ahead", "e1", 1, ends), ("slots", "f1", 1, ends)):
                    pe.wait_ge(R1.sem, R1.at(0, ready))
                    pe.matmul(pi[:, 0:2], seg[:, P * half:P * half + P], src[:], start=True, stop=True)\
                      .then_inc(*Q1.inc(name))
                pe.wait_ge(R1.sem, R1.at(0, "q1"))
                for n in range(3):
                    mm = pe.transpose(px[:, 1, P * n:P * n + P], scan[:, n, :], s["ident"][:])
                mm.then_inc(*Q1.inc("pos"))
                pe.wait_ge(R1.sem, R1.at(0, "ones"))

                def index(e):
                    pe.wait_ge(VM.sem, VM.at(e, "mc"))
                    pe.wait_ge(VI.sem, VI.at(e - 1, "i2"))
                    for half in range(2):
                        for n in range(NLAT):
                            pe.matmul(pi[:, half:half + 1], below[:, n, P * half:P * half + P], ones[:],
                                      start=(n == 0), stop=(n == NLAT - 1))
                    pe.matmul(pi[0:CCAP, 2:3], below_c[:], ones[:], start=True, stop=True).then_inc(*PI.inc("ids"))

                def turn(e):
                    pe.wait_ge(ga, e * 48 + 48)
                    for q in range(KT):
                        pe.wait_ge(AX.sem, AX.at(e, f"x{q - 2}") if q >= 2 else AX.at(e - 1, f"x{q + KT - 2}"))
                        if q < 2:
                            pe.wait_ge(VD.sem, VD.at(e - 2, f"d{4 + q}"))
                        for n, (at, m) in enumerate(GROUPS):
                            mm = pe.transpose(px[:, q % 2, at:at + m], xs[0:m, n, P * q:P * q + P],
                                              s["ident"][0:m, 0:m])
                        mm.then_inc(*PX.inc(f"x{q}"))

                def gate_up(e, h, k):
                    for f in range(KT):
                        j, c = f // 2, f % 2
                        if c == 0:
                            pe.wait_ge(gld[j], (k * 2 + h) * 16 + 16)
                            pe.wait_ge(uld[j], (k * 2 + h) * 16 + 16)
                        if f == 0:
                            pe.wait_ge(AX.sem, AX.at(e, f"x{KT - 1}"))
                        for w, p, name, steps in ((wg, pg, "g", AG), (wu, pu, "u", VG)):
                            free = {"g": "g", "u": "m"}[name]
                            pe.wait_ge(steps.sem, steps.at(e, f"{free}{f - 2}") if f >= 2 else
                                       steps.at(e - 1, f"{free}{f + KT - 2}"))
                            for q in range(KT):
                                mm = pe.matmul(p[:, f % 2, 0:SLOTS], w[:, j, q, P * c:P * c + P], xT[:, q, :],
                                               start=(q == 0), stop=(q == KT - 1))
                            mm.then_inc(*PG.inc(f"{name}{f}"))

                def down(e, h, k, more):
                    pe.wait_ge(VW.sem, VW.at(e, f"w{KT - 1}"))
                    pe.wait_ge(VG.sem, VG.at(e, f"h{KT - 1}"))
                    for n in range(6):
                        (at, m), c = GROUPS[n // 2], n % 2
                        if n < 2 and more:
                            pe.wait_ge(AX.sem, AX.at(e + 1, f"x{KT - 2 + n}"))
                        if n >= 2:
                            pe.wait_ge(VD.sem, VD.at(e, f"d{n - 2}"))
                        elif not more:
                            pe.wait_ge(VD.sem, VD.at(e - 1, f"d{4 + n}"))
                        for f in range(KT):
                            high, low = (x[:, f // 2, f % 2, 512 * c:512 * c + 512] for x in (wdh, wdl))
                            first, last = f == 0, f == KT - 1
                            if n < 4:
                                rows = hid[:, f, at:at + m], hid[:, f, CTX_LO + CCAP + at:CTX_LO + CCAP + at + m]
                                mm = product(pe, px[0:m, n % 2, :], rows, (high, low), first, last)
                            else:
                                rows = hid[:, f, CAP:CTX_LO + CCAP]
                                pe.matmul(px[0:3 * CCAP, n % 2, :], rows, high, start=first, stop=False)
                                mm = pe.matmul(px[0:3 * CCAP, n % 2, :], rows, low, start=False, stop=last)
                        mm.then_inc(*PD.inc(f"d{n}"))

                index(0)
                turn(0)
                index(1)
                pe.wait_ge(empty, 1)

                def body(e, h, k, one, two):
                    gate_up(e, h, k)
                    if two:
                        index(e + 2)
                    if one:
                        turn(e + 1)
                    down(e, h, k, one)

                experts(pe, body)

            @block.scalar
            def _(act):
                AG.give(act)
                AX.give(act)

                for steps in (AH, AW, AC):
                    steps.give(act)

                def turned(e):
                    act.wait_ge(PG.sem, PG.at(e - 1, f"u{KT - 1}"))
                    for q in range(KT):
                        act.wait_ge(PX.sem, PX.at(e, f"x{q}"))
                        act.activation(xT[:, q, :], px[:, q % 2, 0:SLOTS], ACT.Copy).then_inc(*AX.inc(f"x{q}"))

                turned(0)

                def body(e, h, k, one, two):
                    for f in range(KT):
                        act.wait_ge(PG.sem, PG.at(e, f"g{f}"))
                        act.wait_ge(VG.sem, VG.at(e, f"m{f - 1}") if f else VG.at(e - 1, f"m{KT - 1}"))
                        act.activation(act_g[:], pg[:, f % 2, 0:SLOTS], ACT.Silu).then_inc(*AG.inc(f"g{f}"))
                        act.wait_ge(VG.sem, VG.at(e, f"m{f}"))
                        if f == 0:
                            act.wait_ge(PD.sem, PD.at(e - 1, "d5"))
                        act.activation(hid[:, f, 0:SLOTS], full[:], ACT.Copy).then_inc(*AH.inc(f"h{f}"))
                        act.wait_ge(rld, e * (16 * KT) + 16 * (f + 1))
                        act.activation(wdh[:, f // 2, f % 2, :], raw[:], ACT.Copy).then_inc(*AW.inc(f"w{f}"))
                    if one:
                        turned(e + 1)
                    for c in range(2):
                        act.wait_ge(PD.sem, PD.at(e, f"d{4 + c}"))
                        act.wait_ge(VD.sem, VD.at(e, "d4") if c else VD.at(e - 1, "d5"))
                        act.activation(clow[:], px[2 * CCAP:3 * CCAP, c, :], ACT.Copy).then_inc(*AC.inc(f"c{c}"))

                experts(act, body)

            @block.vector
            def _(v):
                for steps in (VG, VM, VI, VX, VD, VW, VC):
                    steps.give(v)
                for steps in (R0, RB, R1):
                    steps.give(v)
                v.memset(hid[:, :, SLOTS:CTX_LO].bitcast(F32), 0.0).then_inc(empty, 1)
                v.memset(arr[:], 0.0).then_inc(*R0.inc("zero"))
                v.wait_ge(R0.sem, R0.at(0, "zero"))
                lat = s["aff"][:, 0:NLAT, :].rearrange("p (g b) e -> p b e g", b=2)
                for b in range(2):
                    v.tensor_copy(arr[:, b, :].rearrange("p (e g) -> p e g", g=8), lat[:, b]).then_inc(*R0.inc(f"a{b}"))
                v.tensor_copy(arr[:, 2, 0:P:8], s["aff"][:, NLAT, :]).then_inc(*R0.inc("ac"))
                v.wait_ge(Q1.sem, Q1.at(0, "prob"))
                v.tensor_copy(prob[:].rearrange("p a b -> p (a b)"), px[:, 0, 0:3 * P]).then_inc(*R0.inc("prob"))
                v.memset(thr[:], 0).then_inc(*R0.inc("thr"))
                v.memset(bit[:], 1 << (BITS - 1)).then_inc(*R0.inc("bit"))
                v.wait_ge(R0.sem, R0.at(0, "bit"))
                v.wait_ge(ldc, 80)
                parts = lambda a, n: a[:, 0:2, :] if n == 0 else a[:, 2, :]
                with v.Fori(0, BITS, 1) as i:
                    v.wait_ge(RB.sem, RB.at(i - 1, "thr"))
                    v.tensor_tensor(cand[:], thr[:], bit[:], ALU.bitwise_or).then_inc(*RB.inc("cand"))
                    v.wait_ge(RB.sem, RB.at(i, "cand"))
                    for n, name in enumerate(("cl", "cc")):
                        v.tensor_scalar(parts(over, n), parts(prob, n), cand[:, n:n + 1].bitcast(F32), 0.0, ALU.is_ge,
                                        ALU.add, accum_out=cnt[:, n:n + 1]).then_inc(*RB.inc(name))
                    v.wait_ge(QB.sem, QB.at(i, "sum"))
                    v.tensor_tensor(met[:], pi[:, 0:2], caps[:], ALU.is_ge).then_inc(*RB.inc("met"))
                    v.wait_ge(RB.sem, RB.at(i, "met"))
                    v.tensor_single_scalar(bit[:], bit[:], 1, ALU.logical_shift_right).then_inc(*RB.inc("bit"))
                    v.copy_predicated(thr[:], met[:], cand[:]).then_inc(*RB.inc("thr"))
                v.wait_ge(RB.sem, RB.at(BITS - 1, "thr"))
                t = lambda n: thr[:, n:n + 1].bitcast(F32)
                done = lambda name: v.wait_ge(R1.sem, R1.at(0, name))
                for n, name in enumerate(("gl", "gc")):
                    v.tensor_scalar(parts(over, n), parts(prob, n), t(n), 0.0, ALU.is_gt, ALU.add,
                                    accum_out=cnt[:, n:n + 1]).then_inc(*R1.inc(name))
                v.wait_ge(Q1.sem, Q1.at(0, "above"))
                v.tensor_tensor(need[:], caps[:], pi[:, 0:2], ALU.subtract).then_inc(*R1.inc("need"))
                for n, name in enumerate(("tl", "tc")):
                    v.tensor_scalar(parts(tie, n), parts(prob, n), t(n), None, ALU.is_equal).then_inc(*R1.inc(name))
                flat = lambda a, n: a[:].rearrange("p a b -> p (a b)")[:, 0:256] if n == 0 else a[:, 2, :]

                def running(src, a, b):
                    for n in range(2):
                        v.tensor_tensor_scan(flat(scan, n), flat(src, n), flat(src, n), 0.0, ALU.add, ALU.bypass)\
                         .then_inc(*R1.inc(f"{a}{n}"))
                    done(f"{a}1")
                    for n in range(2):
                        v.tensor_copy(ends[:, n:n + 1], scan[:, 1 + n, P - 1:P]).then_inc(*R1.inc(f"{b}{n}"))

                done("tc")
                running(tie, "s", "e")
                v.wait_ge(Q1.sem, Q1.at(0, "ahead"))
                v.tensor_tensor(need[:], need[:], pi[:, 0:2], ALU.subtract).then_inc(*R1.inc("lim"))
                done("lim")
                for n in range(2):
                    v.scalar_tensor_tensor(flat(tie, n), flat(scan, n), need[:, n:n + 1], flat(tie, n), ALU.is_le,
                                           ALU.mult).then_inc(*R1.inc(f"k{n}"))
                done("k1")
                v.tensor_tensor(tie[:], tie[:], over[:], ALU.add).then_inc(*R1.inc("sel"))
                done("sel")
                running(tie, "p", "f")
                v.wait_ge(Q1.sem, Q1.at(0, "slots"))
                v.tensor_copy(need[:], pi[:, 0:2]).then_inc(*R1.inc("off"))
                done("off")
                for n in range(2):
                    v.tensor_scalar(flat(scan, n), flat(scan, n), need[:, n:n + 1], None, ALU.add)\
                     .then_inc(*R1.inc(f"q{n}"))
                v.wait_ge(Q1.sem, Q1.at(0, "pos"))
                v.tensor_copy(pos[:].rearrange("p a b -> p (a b)"), px[:, 1, 0:3 * P]).then_inc(*R1.inc("pos"))
                v.memset(ones[:], 1.0).then_inc(*R1.inc("ones"))
                done("ones")

                def passed(e, n):
                    g, b = n // 2, n % 2
                    v.tensor_scalar(below[:, n, :], slot[:], pos[:, b, take(e * 8 + g, 1)], None, ALU.is_ge)\
                     .then_inc(*VM.inc(f"m{n}"))

                def passed_context(e):
                    v.tensor_scalar(below_c[:], slot[:, 0:CCAP], pos[:, 2, take(e * 8, 1)], None, ALU.is_ge)\
                     .then_inc(*VM.inc("mc"))

                def numbers(e, h, k):
                    v.wait_ge(PI.sem, PI.at(e, "ids"))
                    if not (isinstance(k, int) and k == 0):
                        v.wait_ge(ga, e * 48 - 48)
                    v.tensor_copy(ids[:, h, 0:2], pi[:, 0:2]).then_inc(*VI.inc("i0"))
                    v.tensor_scalar(ids[0:CCAP, h, 2:3], pi[0:CCAP, 2:3], float(LAT), None, ALU.add)\
                     .then_inc(*VI.inc("i2"))

                for e in range(2):
                    v.wait_ge(PI.sem, PI.at(e - 1, "ids"))
                    for n in range(NLAT):
                        passed(e, n)
                    passed_context(e)
                    numbers(e, e, 0)

                def body(e, h, k, one, two):
                    v.wait_ge(ga, e * 48 + 48)
                    v.wait_ge(CP.sem, CP.at(e - 2, "added"))
                    v.wait_ge(VI.sem, VI.at(e, "i2"))
                    v.tensor_copy(sids[:, h, 0:2], ids[:, h, 0:2]).then_inc(*VX.inc("s0"))
                    v.tensor_copy(sids[0:CCAP, h, 2:3], ids[0:CCAP, h, 2:3]).then_inc(*VX.inc("s2"))
                    v.tensor_copy(vals[:, h, 0:2], xs[:, 0:2, take(e + DM, 1)].rearrange("p a b -> p (a b)"))\
                     .then_inc(*VX.inc("v0"))
                    v.tensor_copy(vals[0:CCAP, h, 2:3], xs[0:CCAP, 2, take(e + DM, 1)]).then_inc(*VX.inc("v2"))
                    for f in range(KT):
                        v.wait_ge(AG.sem, AG.at(e, f"g{f}"))
                        v.wait_ge(PG.sem, PG.at(e, f"u{f}"))
                        if f == 0:
                            v.wait_ge(PD.sem, PD.at(e - 1, "d5"))
                        v.wait_ge(VG.sem, VG.at(e, f"h{f - 1}") if f else VG.at(e - 1, f"h{KT - 1}"))
                        v.tensor_tensor(full[:], pu[:, f % 2, 0:SLOTS], act_g[:], ALU.mult)\
                         .then_inc(*VG.inc(f"m{f}"))
                        v.wait_ge(VG.sem, VG.at(e, f"m{f}"))
                        v.wait_ge(AH.sem, AH.at(e, f"h{f}"))
                        for name, (at, n), to in (("l", (0, CAP), CTX_LO + CCAP), ("h", (CAP, CCAP), CTX_LO)):
                            v.tensor_tensor(hid[:, f, to:to + n], full[:, at:at + n],
                                            hid[:, f, at:at + n].bitcast(F32), ALU.subtract).then_inc(*VG.inc(f"{name}{f}"))
                        v.wait_ge(AW.sem, AW.at(e, f"w{f}"))
                        v.tensor_tensor(wdl[:, f // 2, f % 2, :], raw[:], wdh[:, f // 2, f % 2, :].bitcast(F32),
                                        ALU.subtract).then_inc(*VW.inc(f"w{f}"))
                        if two:
                            if f == 0:
                                v.wait_ge(PI.sem, PI.at(e + 1, "ids"))
                            for n in range(3 * f, min(3 * f + 3, NLAT)):
                                passed(e + 2, n)
                            if f == KT - 2:
                                passed_context(e + 2)
                    if two:
                        numbers(e + 2, h, k + 1)
                    v.wait_ge(CP.sem, CP.at(e - 1, "added"))
                    v.wait_ge(VX.sem, VX.at(e, "v2"))
                    for n in range(6):
                        g, c = n // 2, n % 2
                        m = GROUPS[g][1]
                        v.wait_ge(PD.sem, PD.at(e, f"d{n}"))
                        rows = px[0:m, c, :]
                        if g == 2:
                            v.wait_ge(AC.sem, AC.at(e, f"c{c}"))
                            v.tensor_tensor(clow[:], px[0:m, c, :], clow[:], ALU.add).then_inc(*VC.inc(f"sum{c}"))
                            v.wait_ge(VC.sem, VC.at(e, f"sum{c}"))
                            rows = clow[:]
                        v.scalar_tensor_tensor(ye[0:m, g, 512 * c:512 * c + 512], rows, vals[0:m, h, g:g + 1],
                                               gate2[0:m, g // 2, 512 * c:512 * c + 512], ALU.mult, ALU.mult)\
                         .then_inc(*VD.inc(f"d{n}"))

                experts(v, body)

            @block.gpsimd
            def _(g):
                g.memset(spare[:], 0.0).then_inc(pc, 1)
                g.wait_ge(pc, 1)

                CG.give(g)
                CP.give(g)

                def carry(steps, name, column):
                    g.tensor_tensor(spare[:, column:column + 1], spare[:, 0:1], spare[:, 0:1], ALU.add)\
                     .then_inc(*steps.inc(name))

                def gather(e, h):
                    g.wait_ge(VI.sem, VI.at(e, "i2"))
                    g.wait_ge(PX.sem, PX.at(e - 1, f"x{KT - 1}"))
                    g.wait_ge(VX.sem, VX.at(e - 1, "v2"))
                    g.wait_ge(CG.sem, CG.at(e - 1, "carry"))
                    carry(CG, "carry", 1)
                    for n, (at, m) in enumerate(GROUPS):
                        g.indirect_dma_start(xs[0:m, n, :], None, d["h2"],
                                             bass.IndirectOffsetOnAxis(ap=ids[0:m, h, n:n + 1], axis=0)).then_inc(ga, 16)

                gather(0, 0)

                def body(e, h, k, one, two):
                    if one:
                        gather(e + 1, 1 - h)
                    g.wait_ge(VD.sem, VD.at(e, "d5"))
                    g.wait_ge(CP.sem, CP.at(e - 1, "added"))
                    carry(CP, "before", 2)
                    for n, (at, m) in enumerate(GROUPS):
                        g.indirect_dma_start(d["xacc"], bass.IndirectOffsetOnAxis(ap=sids[0:m, h, n:n + 1], axis=0),
                                             ye[0:m, n, :], None, compute_op=ALU.add).then_inc(sc[h], 16)
                    g.wait_ge(sc[h], 48 * (k + 1))
                    carry(CP, "added", 3)

                experts(g, body)
                for h in range(2):
                    g.wait_ge(sc[h], 48 * NE // 2)


def phase_final(nc, d, s):
    SL = 4
    with ExitStack() as ctx:
        sb, pb, sem, counted = makers(nc, ctx, s, "final")
        x = sb("xf", [P, SL, DM])
        y = sb("yf", [P, SL, DM])
        junk = sb("junkf", [P, DM])
        gf = sb("gf", [P, DM])
        rstd = sb("rstdf", [P, SL])
        eps = sb("epsf", [P, 1])
        ldc, cv = sem("ld_cf"), sem("consts_f")
        ld = [sem(f"ld_f{m}") for m in range(SL)]
        st = [sem(f"st_f{m}") for m in range(SL)]
        AS = counted("act_final", ["sq", "std"])
        VS = counted("dve_final", ["rstd", "y"])

        def in_loop(eng, body):
            with eng.Fori(0, NLAT // SL, 1) as i:
                for m in range(SL):
                    body(i * SL + m, m, i)
            body(NLAT, 0, NLAT // SL)

        with nc.Block() as block:
            @block.sync
            def _(sp):
                had(sp, st)
                def load(t, m):
                    sp.dma_start(x[:, m], d["xacc"][take(t * P, P), :]).then_inc(ld[m], 16)

                def store(t, m):
                    at = t * P if isinstance(t, int) else sp.snap(t * P)
                    sp.wait_ge(VS.sem, VS.at(t, "y"))
                    sp.dma_start(d["y_sample"][take(at, P), :], y[:, m]).then_inc(st[m], 16)

                sp.dma_start(gf[:], d["norm_f_g"].partition_broadcast(P)).then_inc(ldc, 16)
                for m in range(SL):
                    load(m, m)
                with sp.Fori(0, NLAT // SL - 1, 1) as i:
                    for m in range(SL):
                        store(i * SL + m, m)
                        load(i * SL + (m + SL), m)
                for t in range(NLAT - SL, NLAT):
                    store(t, t % SL)
                    if t == NLAT - SL:
                        load(NLAT, 0)
                sp.wait_ge(VS.sem, VS.at(NLAT, "y"))
                sp.dma_start(d["y_prompt"], y[:, 0]).then_inc(st[0], 16)
                for m in range(SL):
                    sp.wait_ge(st[m], 16 * (NLAT // SL + (m == 0)) + HAD)
                retire(sp, s)

            @block.scalar
            def _(act):
                AS.give(act)
                act.wait_ge(cv, 1)

                def body(t, m, k):
                    act.wait_ge(ld[m], 16 * (k + 1))
                    act.wait_ge(VS.sem, VS.at(t - SL // 2, "y") if False else VS.at(t - 2, "y"))
                    act.activation(junk[:], x[:, m], ACT.Square, scale=DM ** -0.5, accum_out=rstd[:, m:m + 1])\
                       .then_inc(*AS.inc("sq"))
                    act.wait_ge(AS.sem, AS.at(t, "sq"))
                    act.activation(rstd[:, m:m + 1], rstd[:, m:m + 1], ACT.Sqrt, bias=eps[:]).then_inc(*AS.inc("std"))

                in_loop(act, body)

            @block.vector
            def _(v):
                VS.give(v)
                v.memset(eps[:], EPS).then_inc(cv, 1)
                v.wait_ge(ldc, 16)

                def body(t, m, k):
                    v.wait_ge(AS.sem, AS.at(t, "std"))
                    v.reciprocal(rstd[:, m:m + 1], rstd[:, m:m + 1]).then_inc(*VS.inc("rstd"))
                    v.wait_ge(st[m], 16 * k + HAD)
                    v.wait_ge(VS.sem, VS.at(t, "rstd"))
                    v.scalar_tensor_tensor(y[:, m], x[:, m], rstd[:, m:m + 1], gf[:], ALU.mult, ALU.mult)\
                     .then_inc(*VS.inc("y"))

                in_loop(v, body)


PHASES = [phase_filters, phase_tokens, phase_hyena_in, phase_spectrum, phase_hyena_out, phase_retention,
          phase_merge, phase_out, phase_experts, phase_final]

SCRATCH = {
    "mod": (2, 6 * DM), "kspec": (P, N2, DH), "cspec": (2, P, DH),
    "hT": (P, KT, TOK), "state": (NLAT, P, 512), "v": (NT, P, 512), "gs": (NT, P, 512), "qkT": (NT, P, 1024),
    "kvb": (NLAT, P, 512), "x2": (CB, P, TOK + 2), "uspec": (P, N2, DH), "uctx": (P, DH), "qspec": (P, N2, DH),
    "yhy": (P, CB, TOK), "yret": (P, CB, TOK), "merged": (P, KT, TOK), "xacc": (TOK, DM), "h2": (TOK, ROW),
}
OUTPUTS = {"y_prompt": (CTX, DM), "y_sample": (LAT, DM), "new_f": (HEADS, HD, HD), "new_b": (HEADS, HD, HD)}


def build(nc, d):
    with ExitStack() as ctx:
        s = persistent(nc, ctx)
        for phase in PHASES:
            s["own"], s["stack"] = [], ExitStack()
            phase(nc, d, s)
            s["last_stack"].close()
            s["last"], s["last_stack"] = s["own"], s["stack"]
        s["last_stack"].close()


def kernel(**inputs):
    import concourse.bacc as bacc
    from concourse.bass_utils import run_bass_kernel_spmd

    arrays = {**layout({k: np.asarray(v) for k, v in inputs.items()}), **constants()}
    nc = bacc.Bacc("TRN2", target_bir_lowering=False, num_devices=1)
    d = {k: nc.dram_tensor(f"in_{k}", a.shape, F32, kind="ExternalInput").ap() for k, a in arrays.items()}
    for k, shape in SCRATCH.items():
        d[k] = nc.dram_tensor(f"scratch_{k}", shape, F32, kind="Internal").ap()
    for k, shape in OUTPUTS.items():
        d[k] = nc.dram_tensor(f"out_{k}", shape, F32, kind="ExternalOutput").ap()
    build(nc, d)
    r = run_bass_kernel_spmd(nc, [{f"in_{k}": a for k, a in arrays.items()}], core_ids=[0]).results[0]
    state = (1, 1, HEADS, HD, HD)
    return (r["out_y_prompt"].reshape(1, CTX, DM), r["out_y_sample"].reshape(1, LAT, DM),
            r["out_new_f"].reshape(state), r["out_new_b"].reshape(state))
```
